# Optimizing a Trainium2 kernel written in Bass

```python
import math
import jax, jax.numpy as jnp
from jax import lax
import numpy as np

'''
Hybrid autoregressive decoder step: DEPTH trunk layers serving a prompt group and a sample group
with the same parameter arrays.

Layer (sandwich RMSNorm, parallel gated branches):
  h = RMSNorm(x); z = h @ w_in   (single combined projection; columns partitioned among all head groups)
  branch A: HGRN2 gated linear recurrence with state expansion (8 heads, 128x128 state per head)
  branch B: NSA sparse attention (16 query heads, 4 kv heads, NoPE): compressed-block means,
            top-k selected blocks (gathered) and sliding window (banded), combined by per-head sigmoid gates
  u = sigmoid(gA) * oA + sigmoid(gB) * oB ; x = x + RMSNorm(u @ w_out)
  x = x + RMSNorm(ConvFFN(RMSNorm(x)))   (up-proj -> causal depthwise conv width 3 -> SwiGLU -> down-proj)

Inputs:
  x_prompt (BATCH, SEQ, D_MODEL); x_sample (DEC_BATCH, DEC_SEQ, D_MODEL)
  cache_cmp_kv, cache_sel_kv (DEPTH, N_POOL, PAGE_SIZE, 2, NSA_KV_HEADS, NSA_HD)  paged K/V pools
  page_table (DEC_BATCH, N_PAGES) int32, N_PAGES = PAST_LEN // PAGE_SIZE
  state_win_kv (DEPTH, DEC_BATCH, min(WINDOW, PAST_LEN), 2, NSA_KV_HEADS, NSA_HD)
  state_hgrn (DEPTH, DEC_BATCH, HG_HEADS, HG_DK, HG_DV)
  state_conv (DEPTH, DEC_BATCH, CONV_W - 1, 2 * D_FF)
  then the weights.
Returns the tuple
  (y_prompt (BATCH, SEQ, D_MODEL), y_sample (DEC_BATCH, DEC_SEQ, D_MODEL),
   cmp_kv_prompt (DEPTH, BATCH, SEQ, 2, KVH, HD), cmp_kv_sample (DEPTH, DEC_BATCH, DEC_SEQ, 2, KVH, HD),
   sel_kv_prompt (DEPTH, BATCH, SEQ, 2, KVH, HD), sel_kv_sample (DEPTH, DEC_BATCH, DEC_SEQ, 2, KVH, HD),
   win_kv_prompt (DEPTH, BATCH, min(WINDOW, SEQ), 2, KVH, HD),
   win_kv_sample (DEPTH, DEC_BATCH, min(WINDOW, PAST_LEN), 2, KVH, HD),
   hgrn_prompt (DEPTH, BATCH, HG_HEADS, HG_DK, HG_DV), hgrn_sample (DEPTH, DEC_BATCH, HG_HEADS, HG_DK, HG_DV),
   conv_prompt (DEPTH, BATCH, CONV_W - 1, 2 * D_FF), conv_sample (DEPTH, DEC_BATCH, CONV_W - 1, 2 * D_FF))
K/V rows are [k, v] stacked on axis 2; new paged rows are returned per sequence in logical order.
'''

D_MODEL = 1024
BATCH = 1
SEQ = 512
DEPTH = 1
DEC_BATCH = 8
DEC_SEQ = 8
PAST_LEN = 4096
PAGE_SIZE = 128

HG_HEADS = 8
HG_DK = D_MODEL // HG_HEADS
HG_DV = HG_DK
HG_WIDTH = HG_HEADS * HG_DK
HG_CHUNK = 32

NSA_HEADS = 16
NSA_HD = D_MODEL // NSA_HEADS
NSA_KV_HEADS = 4
NSA_GROUP = NSA_HEADS // NSA_KV_HEADS
NSA_WIDTH = NSA_HEADS * NSA_HD
KV_WIDTH = NSA_KV_HEADS * NSA_HD
N_NSA_BRANCH = 3
CMP_BLOCK = 32
SEL_BLOCK = 64
SEL_TOPK = 8
WINDOW = 512
Q_BLOCK = 128
SEL_Q_BLOCK = 64
FORCE_BONUS = 1.0e4
ATT_SCALE = NSA_HD ** -0.5

N_BRANCH = 2
D_FF = 2816
CONV_W = 3

EPS = 1e-6
NEG = -1e30

IN_SPLITS = (HG_WIDTH,) * 4 + (NSA_WIDTH,) + (KV_WIDTH,) * 6 + (NSA_HEADS * N_NSA_BRANCH, N_BRANCH * D_MODEL)
IN_COLS = sum(IN_SPLITS)
IN_OFFSETS = [int(o) for o in np.cumsum(IN_SPLITS)[:-1]]

kernel_name = 'hybrid_hgrn2_nsa_convffn_step'

def rmsnorm(x, g):
    x32 = x.astype(jnp.float32)
    y = x32 * lax.rsqrt(jnp.mean(x32 * x32, axis=-1, keepdims=True) + EPS)
    return (y * g.astype(jnp.float32)).astype(x.dtype)

def masked_softmax(s, mask):
    s = jnp.where(mask, s.astype(jnp.float32), NEG)
    e = jnp.where(mask, jnp.exp(s - jnp.max(s, axis=-1, keepdims=True)), 0.0)
    return e / jnp.maximum(jnp.sum(e, axis=-1, keepdims=True), 1e-30)

def mixer_inputs(x, g_pre, w_in):
    h = rmsnorm(x, g_pre)
    return jnp.split(h @ w_in, IN_OFFSETS, axis=-1)

def stack_kv(k, v):
    B, T = k.shape[:2]
    return jnp.stack([k.reshape(B, T, NSA_KV_HEADS, NSA_HD), v.reshape(B, T, NSA_KV_HEADS, NSA_HD)], axis=2)

def hgrn2_scan(q, logf, k, v, s0):
    B, T, H, _ = q.shape
    C = math.gcd(T, HG_CHUNK)
    N = T // C
    f32 = jnp.float32
    rs = lambda a: a.astype(f32).reshape(B, N, C, H, a.shape[-1]).transpose(1, 0, 3, 2, 4)
    qc, gc, kc, vc = rs(q), rs(logf), rs(k), rs(v)
    b = jnp.cumsum(gc, axis=3)
    b_last = b[:, :, :, -1:, :]
    q_in = qc * jnp.exp(b)
    k_out = kc * jnp.exp(b_last - b)
    q_rel = qc * jnp.exp(b - b_last)
    causal = jnp.tril(jnp.ones((C, C), dtype=bool))
    attn = jnp.where(causal, jnp.einsum('nbhtk,nbhsk->nbhts', q_rel, k_out), 0.0)
    o_intra = jnp.einsum('nbhts,nbhsv->nbhtv', attn, vc)
    chunk_update = jnp.einsum('nbhsk,nbhsv->nbhkv', k_out, vc)
    decay = jnp.exp(b_last[:, :, :, 0, :])

    def step(S, inp):
        d, u = inp
        return d[..., None] * S + u, S

    s_final, s_prev = lax.scan(step, s0.astype(f32), (decay, chunk_update))
    o_inter = jnp.einsum('nbhtk,nbhkv->nbhtv', q_in, s_prev)
    o = (o_intra + o_inter).transpose(1, 0, 3, 2, 4).reshape(B, T, H, v.shape[-1])
    return o, s_final

def hgrn2_branch(hq, hf, hi, hg, lb, norm_g, s0):
    B, T = hq.shape[:2]
    f32 = jnp.float32
    heads = lambda a: a.reshape(B, T, HG_HEADS, -1)
    lbh = lb.reshape(HG_HEADS, HG_DK)
    z = heads(hf).astype(f32)
    logf = jnp.log(lbh + (1.0 - lbh) * jax.nn.sigmoid(z))
    k = (1.0 - lbh) * jax.nn.sigmoid(-z)
    o, s_new = hgrn2_scan(jax.nn.silu(heads(hq)), logf, k, heads(hi), s0)
    o = rmsnorm(o, norm_g) * jax.nn.silu(heads(hg).astype(f32))
    return o.reshape(B, T, HG_WIDTH).astype(hq.dtype), s_new

def gqa_attend(q, k, v, mask):
    s = jnp.einsum('bntgrd,bnsgd->bngrts', q, k) * ATT_SCALE
    p = masked_softmax(s, mask)
    return jnp.einsum('bngrts,bnsgd->bntgrd', p.astype(v.dtype), v), p

def block_means(rows):
    B, L = rows.shape[:2]
    nc = L // CMP_BLOCK
    blk = rows[:, :nc * CMP_BLOCK].astype(jnp.float32).reshape((B, nc, CMP_BLOCK) + rows.shape[2:])
    return blk.mean(axis=2).astype(rows.dtype)

def compressed_branch(qg, kc, q_pos):
    nc = kc.shape[1]
    blk_end = (jnp.arange(nc) + 1) * CMP_BLOCK - 1
    mask = blk_end[None, :] <= q_pos[:, None]
    o, p = gqa_attend(qg[:, None], kc[:, None, :, 0], kc[:, None, :, 1], mask)
    return o[:, 0], p[:, 0].sum(axis=2)

def select_blocks(imp, q_pos, n_sel):
    B, G, T, nc = imp.shape
    ratio = SEL_BLOCK // CMP_BLOCK
    imp = jnp.pad(imp, ((0, 0), (0, 0), (0, 0), (0, n_sel * ratio - nc))).reshape(B, G, T, n_sel, ratio).sum(-1)
    blk = jnp.arange(n_sel)[None, :]
    cur = (q_pos // SEL_BLOCK)[:, None]
    forced = (blk == 0) | (blk == cur)
    score = jnp.where(blk <= cur, imp + jnp.where(forced, FORCE_BONUS, 0.0), NEG)
    top, idx = lax.top_k(score, min(SEL_TOPK, n_sel))
    return idx, top > NEG / 2

def sel_attend(qg, kv, idx, valid, q_pos):
    B, G, T, K = idx.shape
    k = kv[..., 0, :].reshape(B, G, T, K * SEL_BLOCK, NSA_HD)
    v = kv[..., 1, :].reshape(B, G, T, K * SEL_BLOCK, NSA_HD)
    key_pos = (idx[..., None] * SEL_BLOCK + jnp.arange(SEL_BLOCK)).reshape(B, G, T, K * SEL_BLOCK)
    mask = jnp.repeat(valid, SEL_BLOCK, axis=-1) & (key_pos <= q_pos[:, None])
    s = jnp.einsum('btgrd,bgtsd->bgrts', qg, k) * ATT_SCALE
    p = masked_softmax(s, mask[:, :, None])
    return jnp.einsum('bgrts,bgtsd->btgrd', p.astype(v.dtype), v)

def window_prompt(qg, kvw):
    B, T = qg.shape[:2]
    qb = math.gcd(T, Q_BLOCK)
    nqb = T // qb
    span = WINDOW + qb
    kv_pad = jnp.pad(kvw, ((0, 0), (WINDOW, 0), (0, 0), (0, 0), (0, 0)))
    rows = jnp.arange(nqb)[:, None] * qb + jnp.arange(span)[None, :]
    kvb = kv_pad[:, rows]
    key_pos = rows - WINDOW
    q_pos = jnp.arange(T).reshape(nqb, qb)
    d = q_pos[:, :, None] - key_pos[:, None, :]
    mask = (key_pos[:, None, :] >= 0) & (d >= 0) & (d < WINDOW)
    o, _ = gqa_attend(qg.reshape(B, nqb, qb, NSA_KV_HEADS, NSA_GROUP, NSA_HD),
                      kvb[:, :, :, 0], kvb[:, :, :, 1], mask[None, :, None, None])
    return o.reshape(B, T, NSA_KV_HEADS, NSA_GROUP, NSA_HD)

def window_sample(qg, win_buf, kvw_new, q_pos):
    wb = win_buf.shape[1]
    kv = jnp.concatenate([win_buf.astype(kvw_new.dtype), kvw_new], axis=1)
    key_pos = PAST_LEN - wb + jnp.arange(kv.shape[1])
    d = q_pos[:, None] - key_pos[None, :]
    mask = (d >= 0) & (d < WINDOW)
    o, _ = gqa_attend(qg[:, None], kv[:, None, :, 0], kv[:, None, :, 1], mask)
    return o[:, 0], kv[:, -wb:]

def nsa_combine(o_c, o_s, o_w, ngate):
    B, T = o_c.shape[:2]
    g = jax.nn.sigmoid(ngate.astype(jnp.float32)).reshape(B, T, NSA_KV_HEADS, NSA_GROUP, N_NSA_BRANCH)
    o = g[..., 0:1] * o_c + g[..., 1:2] * o_s + g[..., 2:3] * o_w
    return o.reshape(B, T, NSA_WIDTH).astype(o_c.dtype)

def nsa_prompt(nq, kvc, kvs, kvw, ngate):
    B, T = nq.shape[:2]
    qg = nq.reshape(B, T, NSA_KV_HEADS, NSA_GROUP, NSA_HD)
    q_pos = jnp.arange(T)
    o_c, imp = compressed_branch(qg, block_means(kvc), q_pos)
    n_sel = -(-T // SEL_BLOCK)
    idx, valid = select_blocks(imp, q_pos, n_sel)
    k_top = idx.shape[-1]
    sel_blocks = jnp.pad(kvs, ((0, 0), (0, n_sel * SEL_BLOCK - T), (0, 0), (0, 0), (0, 0))).reshape(
        B, n_sel, SEL_BLOCK, 2, NSA_KV_HEADS, NSA_HD)
    b_idx = jnp.arange(B)[:, None, None, None]
    g_idx = jnp.arange(NSA_KV_HEADS)[None, :, None, None]
    qb = math.gcd(T, SEL_Q_BLOCK)
    nqb = T // qb

    def sweep(args):
        q_blk, idx_blk, valid_blk, pos_blk = args
        kv = sel_blocks[b_idx, idx_blk, :, :, g_idx, :]
        return sel_attend(q_blk, kv, idx_blk, valid_blk, pos_blk)

    o_s = lax.map(sweep, (qg.reshape(B, nqb, qb, NSA_KV_HEADS, NSA_GROUP, NSA_HD).swapaxes(0, 1),
                          idx.reshape(B, NSA_KV_HEADS, nqb, qb, k_top).transpose(2, 0, 1, 3, 4),
                          valid.reshape(B, NSA_KV_HEADS, nqb, qb, k_top).transpose(2, 0, 1, 3, 4),
                          q_pos.reshape(nqb, qb)))
    o_s = o_s.swapaxes(0, 1).reshape(B, T, NSA_KV_HEADS, NSA_GROUP, NSA_HD)
    o_w = window_prompt(qg, kvw)
    return nsa_combine(o_c, o_s, o_w, ngate)

def nsa_sample(nq, kvc, kvs, kvw, ngate, pool_c, pool_s, win_buf, page_table):
    B, T = nq.shape[:2]
    qg = nq.reshape(B, T, NSA_KV_HEADS, NSA_GROUP, NSA_HD)
    q_pos = PAST_LEN + jnp.arange(T)
    past_c = pool_c[page_table].reshape(B, PAST_LEN, 2, NSA_KV_HEADS, NSA_HD)
    kc = jnp.concatenate([block_means(past_c).astype(kvc.dtype), block_means(kvc)], axis=1)
    o_c, imp = compressed_branch(qg, kc, q_pos)
    n_sel = -(-(PAST_LEN + T) // SEL_BLOCK)
    idx, valid = select_blocks(imp, q_pos, n_sel)
    bpp = PAGE_SIZE // SEL_BLOCK
    n_past_blk = PAST_LEN // SEL_BLOCK
    pool_blk = pool_s.reshape(-1, SEL_BLOCK, 2, NSA_KV_HEADS, NSA_HD)
    b_idx = jnp.arange(B)[:, None, None, None]
    g_idx = jnp.arange(NSA_KV_HEADS)[None, :, None, None]
    pidx = jnp.minimum(idx, n_past_blk - 1)
    phys = page_table[b_idx, pidx // bpp] * bpp + pidx % bpp
    n_new_blk = -(-T // SEL_BLOCK)
    new_blk = jnp.pad(kvs, ((0, 0), (0, n_new_blk * SEL_BLOCK - T), (0, 0), (0, 0), (0, 0))).reshape(
        B, n_new_blk, SEL_BLOCK, 2, NSA_KV_HEADS, NSA_HD)
    nidx = jnp.clip(idx - n_past_blk, 0, n_new_blk - 1)
    kv_sel = jnp.where((idx < n_past_blk)[..., None, None, None],
                       pool_blk[phys, :, :, g_idx, :].astype(kvs.dtype),
                       new_blk[b_idx, nidx, :, :, g_idx, :])
    o_s = sel_attend(qg, kv_sel, idx, valid, q_pos)
    o_w, win_new = window_sample(qg, win_buf, kvw, q_pos)
    return nsa_combine(o_c, o_s, o_w, ngate), win_new

def merge_out(o_hg, o_nsa, mgate, w_out):
    B, T = o_hg.shape[:2]
    g = jax.nn.sigmoid(mgate.astype(jnp.float32)).reshape(B, T, N_BRANCH, D_MODEL)
    u = g[:, :, 0] * o_hg + g[:, :, 1] * o_nsa
    return u.astype(o_hg.dtype) @ w_out

def conv_ffn(h, w_up, conv_w, conv_b, w_down, buf):
    T = h.shape[1]
    up = h @ w_up
    ext = jnp.concatenate([buf.astype(up.dtype), up], axis=1)
    c = conv_b + ext[:, 0:T] * conv_w[0]
    for j in range(1, CONV_W):
        c = c + ext[:, j:j + T] * conv_w[j]
    a, b = jnp.split(c, 2, axis=-1)
    return (jax.nn.silu(a) * b) @ w_down, ext[:, T:]

def setup_inputs(seed: int = 0) -> dict:
    key = jax.random.key(seed)
    ks = jax.random.split(key, 24)
    f32 = jnp.float32
    n_pages = PAST_LEN // PAGE_SIZE
    n_used = DEC_BATCH * n_pages
    n_pool = (5 * n_used + 3) // 4
    wb = min(WINDOW, PAST_LEN)
    nrm = lambda k, shape, s: jax.random.normal(k, shape, f32) * s
    page_table = jax.random.permutation(ks[0], n_pool)[:n_used].reshape(DEC_BATCH, n_pages).astype(jnp.int32)
    return {
        'x_prompt': nrm(ks[1], (BATCH, SEQ, D_MODEL), 1.0),
        'x_sample': nrm(ks[2], (DEC_BATCH, DEC_SEQ, D_MODEL), 1.0),
        'cache_cmp_kv': nrm(ks[3], (DEPTH, n_pool, PAGE_SIZE, 2, NSA_KV_HEADS, NSA_HD), 1.0),
        'cache_sel_kv': nrm(ks[4], (DEPTH, n_pool, PAGE_SIZE, 2, NSA_KV_HEADS, NSA_HD), 1.0),
        'page_table': page_table,
        'state_win_kv': nrm(ks[5], (DEPTH, DEC_BATCH, wb, 2, NSA_KV_HEADS, NSA_HD), 1.0),
        'state_hgrn': nrm(ks[6], (DEPTH, DEC_BATCH, HG_HEADS, HG_DK, HG_DV), 0.5),
        'state_conv': nrm(ks[7], (DEPTH, DEC_BATCH, CONV_W - 1, 2 * D_FF), 1.0),
        'w_in': nrm(ks[8], (DEPTH, D_MODEL, IN_COLS), D_MODEL ** -0.5),
        'hg_lb_logits': nrm(ks[9], (DEPTH + 1, HG_WIDTH), 0.1),
        'hg_norm_g': 1.0 + nrm(ks[10], (DEPTH, HG_DV), 0.05),
        'w_out': nrm(ks[11], (DEPTH, D_MODEL, D_MODEL), D_MODEL ** -0.5),
        'w_up': nrm(ks[12], (DEPTH, D_MODEL, 2 * D_FF), D_MODEL ** -0.5),
        'conv_w': nrm(ks[13], (DEPTH, CONV_W, 2 * D_FF), 0.5),
        'conv_b': nrm(ks[14], (DEPTH, 2 * D_FF), 0.01),
        'w_down': nrm(ks[15], (DEPTH, D_FF, D_MODEL), D_FF ** -0.5),
        'g_pre_mix': 1.0 + nrm(ks[16], (DEPTH, D_MODEL), 0.05),
        'g_post_mix': 1.0 + nrm(ks[17], (DEPTH, D_MODEL), 0.05),
        'g_pre_ffn': 1.0 + nrm(ks[18], (DEPTH, D_MODEL), 0.05),
        'g_post_ffn': 1.0 + nrm(ks[19], (DEPTH, D_MODEL), 0.05),
    }

def reference(x_prompt, x_sample, cache_cmp_kv, cache_sel_kv, page_table, state_win_kv, state_hgrn, state_conv,
              w_in, hg_lb_logits, hg_norm_g, w_out, w_up, conv_w, conv_b, w_down,
              g_pre_mix, g_post_mix, g_pre_ffn, g_post_ffn):
    B, T = x_prompt.shape[:2]
    DB = x_sample.shape[0]
    lbs = jnp.cumsum(jax.nn.softmax(hg_lb_logits.astype(jnp.float32), axis=0), axis=0)
    xp, xs = x_prompt, x_sample
    cmp_p, cmp_s, sel_p, sel_s, win_p, win_s, hg_p, hg_s, cv_p, cv_s = ([] for _ in range(10))
    for l in range(DEPTH):
        hq, hf, hi, hg, nq, kc, vc, ksl, vsl, kw, vw, ng, mg = mixer_inputs(xp, g_pre_mix[l], w_in[l])
        o_hg, s_hg = hgrn2_branch(hq, hf, hi, hg, lbs[l], hg_norm_g[l],
                                  jnp.zeros((B, HG_HEADS, HG_DK, HG_DV), jnp.float32))
        kvc, kvs, kvw = stack_kv(kc, vc), stack_kv(ksl, vsl), stack_kv(kw, vw)
        o_nsa = nsa_prompt(nq, kvc, kvs, kvw, ng)
        xp = xp + rmsnorm(merge_out(o_hg, o_nsa, mg, w_out[l]), g_post_mix[l])
        f_out, cbuf = conv_ffn(rmsnorm(xp, g_pre_ffn[l]), w_up[l], conv_w[l], conv_b[l], w_down[l],
                               jnp.zeros((B, CONV_W - 1, 2 * D_FF), xp.dtype))
        xp = xp + rmsnorm(f_out, g_post_ffn[l])
        cmp_p.append(kvc)
        sel_p.append(kvs)
        win_p.append(kvw[:, -min(WINDOW, T):])
        hg_p.append(s_hg)
        cv_p.append(cbuf)
        hq, hf, hi, hg, nq, kc, vc, ksl, vsl, kw, vw, ng, mg = mixer_inputs(xs, g_pre_mix[l], w_in[l])
        o_hg, s_hg = hgrn2_branch(hq, hf, hi, hg, lbs[l], hg_norm_g[l], state_hgrn[l])
        kvc, kvs, kvw = stack_kv(kc, vc), stack_kv(ksl, vsl), stack_kv(kw, vw)
        o_nsa, wbuf = nsa_sample(nq, kvc, kvs, kvw, ng, cache_cmp_kv[l], cache_sel_kv[l], state_win_kv[l], page_table)
        xs = xs + rmsnorm(merge_out(o_hg, o_nsa, mg, w_out[l]), g_post_mix[l])
        f_out, cbuf = conv_ffn(rmsnorm(xs, g_pre_ffn[l]), w_up[l], conv_w[l], conv_b[l], w_down[l], state_conv[l])
        xs = xs + rmsnorm(f_out, g_post_ffn[l])
        cmp_s.append(kvc)
        sel_s.append(kvs)
        win_s.append(wbuf)
        hg_s.append(s_hg)
        cv_s.append(cbuf)
    return (xp, xs,
            jnp.stack(cmp_p), jnp.stack(cmp_s),
            jnp.stack(sel_p), jnp.stack(sel_s),
            jnp.stack(win_p), jnp.stack(win_s),
            jnp.stack(hg_p), jnp.stack(hg_s),
            jnp.stack(cv_p), jnp.stack(cv_s))


_drawn_inputs = setup_inputs


def setup_inputs(seed=0):
    import zlib

    import numpy as np

    out = dict(_drawn_inputs(seed))
    spreads = {}
    factors = {'conv_b': 6.082}
    for name, (base, spread) in spreads.items():
        noise = np.random.default_rng([zlib.crc32(name.encode()), seed]).standard_normal(out[name].shape)
        drawn = base * np.exp(spread * noise) if base else spread * noise
        out[name] = __import__('jax').numpy.asarray(drawn.astype(out[name].dtype))
    for name, factor in factors.items():
        out[name] = (out[name] * factor).astype(out[name].dtype)
    return out
```

```python
import numpy as np
import concourse.bass as bass
from concourse import mybir
from contextlib import ExitStack

F32 = mybir.dt.float32
BF16 = mybir.dt.bfloat16
U32 = mybir.dt.uint32
I32 = mybir.dt.int32
ALU = mybir.AluOpType
ACT = mybir.ActivationFunctionType
AX = mybir.AxisListType

P = 128
D = 1024
T = 512
SB = 8
ST = 8
S = SB * ST
N = T + S
NHF = N // 2
KD = D // P
PT = T // P
TT = PT + 1
TR = [P] * PT + [S]
HH = 8
CH = 32
NCH = T // CH
CPT = P // CH
NH, G, R, HD = 16, 4, 4, 64
KV = G * HD
BR = 3
CB = 32
PB = T // CB
NPG = 32
SELB = 64
NSB = NPG * P // SELB
WIN = 512
FF = 2816
NF = FF // P
EPS = 1e-6
NEG = -1.0e30
BONUS = 1.0e4
SCALE = HD ** -0.5
WB = 256
O_HQ, O_HF, O_HI, O_HG, O_NQ, O_KV = 0, D, 2 * D, 3 * D, 4 * D, 5 * D
O_NG = O_KV + 6 * KV
O_MG = O_NG + NH * BR
C_KS, C_VS, C_KW, C_VW = 2 * KV, 3 * KV, 4 * KV, 5 * KV
NSLOT = 4
U_KV = 4 * HH
U_KT = U_KV + 18
U_CM = U_KT + 4
U_NQ = U_CM + 1
U_NG = U_NQ + 8
U_MG = U_NG + 1
U_UP = U_MG + 16
B_KV = 4 * HH
B_NQ = B_KV + 6
B_NG = B_NQ + 4
B_MG = B_NG + 1
B_WO = B_MG + 8
B_UP = B_WO + 4
B_DN = B_UP + NF
DN_T = [(0, 4), (4, 4), (8, 4), (12, 4), (16, 4), (20, 2)]
PGC = 4
NPC = NPG // PGC
NC = NPC + 2
LAG = NC + 3
NKR, NVR = 3, 8


def wait(eng, semaphore, value):
    if value > 0:
        eng.wait_ge(semaphore, value)


def build(nc, x_p, x_s, cache_c, cache_s, ptab, win_kv, st_hg, st_cv, w_in, lb_lg, hg_g, w_out, w_up,
          conv_w, conv_b, w_down, g_pm, g_qm, g_pf, g_qf,
          y_p, y_s, cmp_p, cmp_s, sel_p, sel_s, win_p, win_s, hgo_p, hgo_s, cv_p, cv_s):
    ctx = ExitStack()
    with ctx:
        def sb(name, shape, dt=F32):
            return ctx.enter_context(nc.sbuf_tensor(name, shape, dt))

        def sem(name):
            return ctx.enter_context(nc.semaphore(name))

        ident = sb("ident", [P, P])
        identb = sb("identb", [P, P], BF16)
        ones = sb("ones", [P, P])
        zerob = sb("zerob", [P, P], BF16)
        swap = sb("swap", [P, P])
        penf = sb("penf", [P, P])
        penb = sb("penb", [P, P], BF16)
        hmask = sb("hmask", [P, P])
        hmask_s = sb("hmask_s", [S, S])
        scanm = sb("scanm", [P, N])
        cmask = sb("cmask", [P, CPT])
        cmask_s = sb("cmask_s", [S, SB])
        amean = sb("amean", [P, CPT])
        avm = sb("avm", [P, PT, R, CB])
        cm01 = sb("cm01", [P, PT, PB])
        cpen = sb("cpen", [P, PT, PB])
        rmat = sb("rmat", [P, G * ST])
        rmatT = sb("rmatT", [G * ST, P])
        rep8 = sb("rep8", [ST, P])
        c16 = sb("c16", [ST, 2, ST])
        pen8 = sb("pen8", [P, 2, ST])
        pnew = sb("pnew", [P, SB, S])
        epsc = sb("epsc", [P, 1])
        prow = sb("prow", [33, P])
        par = sb("par", [P, 33])
        cpar = sb("cpar", [P, 4, 2 * NF])
        lbt = sb("lbt", [P, 4, HH])
        lb = sb("lb", [P, HH])
        oml = sb("oml", [P, HH])
        ptb = sb("ptb", [1, SB * NPG], I32)
        pti = sb("pti", [P, SB], I32)
        ptf = sb("ptf", [P, SB])
        q8i = sb("q8i", [P, 1], I32)
        q8f = sb("q8f", [P, 1])
        pidx = sb("pidx", [P, SB, 8], U32)
        gate = sb("gate", [P, TT, NH * BR])
        gateq = sb("gateq", [P, SB, BR])
        st_ss = sb("st_ss", [P, 4, TT])
        st_rs = sb("st_rs", [P, 4, TT])
        nmx = sb("nmx", [P, 4])
        ssm = sb("ssm", [P, 4])
        cfa = sb("cfa", [P, 4])
        cst1 = sb("cst1", [P, 3, NH])
        est = sb("est", [P, 2, 32])
        cst2 = sb("cst2", [P, 4])

        M = 48960
        mem = sb("mem", [P, M])
        at = [0]

        def view(n, start=None):
            a = at[0] if start is None else start
            at[0] = a + n
            assert at[0] <= M, (at[0], M)
            return mem[:, a:a + n]

        hT = view(KD * N).rearrange("p (k n) -> p k n", n=N)
        a_ohg = at[0]
        ohg = view(KD * N).rearrange("p (k n) -> p k n", n=N)
        wring = view(NSLOT * KD * WB)
        wslot = [wring[:, s * KD * WB:(s + 1) * KD * WB] for s in range(NSLOT)]
        cmt = view(SB * 2 * KV).rearrange("p (b c) -> p b c", c=2 * KV)
        a_kvt = at[0]
        kvt = view(TT * 6 * KV).rearrange("p (i c) -> p i c", c=6 * KV)
        a_r = at[0]
        CROW = 4 * 2 * KV
        cring = [view(CROW, a_kvt + i * CROW) for i in range(3)]
        cpart = view(2 * KV)
        at[0] = a_r
        qb, gb, eb, rb, fb, xb = [[view(N) for _ in range(2)] for _ in range(6)]
        vt = [view(TT * P).rearrange("p (i c) -> p i c", c=P) for _ in range(2)]
        vm = [view(CPT * P).rearrange("p (c v) -> p c v", v=P) for _ in range(2)]
        vms = view(SB * P).rearrange("p (b v) -> p b v", v=P)
        att = view(T).rearrange("p (i t) -> p i t", t=P)
        att_s = view(S)
        ktok = view(T).rearrange("p (i t) -> p i t", t=P)
        ktok_s = view(P)
        dec = [view(NCH + SB) for _ in range(2)]
        st = view((NCH + 1) * P).rearrange("p (c v) -> p c v", v=P)
        s0s = [view(SB * P).rearrange("p (b v) -> p b v", v=P) for _ in range(2)]
        s1s = view(SB * P).rearrange("p (b v) -> p b v", v=P)
        at[0] = a_r
        xt = [view(D) for _ in range(2)]
        xn = [view(D) for _ in range(2)]
        junk = view(D)
        crow = view(4 * P).rearrange("p (a c) -> p a c", c=P)
        at[0] = a_r
        onsa = view(KD * N).rearrange("p (k n) -> p k n", n=N)
        kT = view(4 * N).rearrange("p (b g n) -> p b g n", b=2, g=2)
        kcz = view(4 * PB).rearrange("p (g e c) -> p g e c", g=2, e=2)
        qbd = view(SB * 2 * S).rearrange("p (b g q) -> p b g q", b=SB, g=2)
        a_vcz = at[0]
        vcz = view(G * R * HD).rearrange("p (g r d) -> p g r d", g=G, r=R)
        a_d = at[0]
        nqT = view(KD * N).rearrange("p (k n) -> p k n", n=N)
        pr = [view(T) for _ in range(4)]
        pT = [view(T).rearrange("p (j t) -> p j t", t=P) for _ in range(4)]
        pcw = view(NH * PB).rearrange("p (h c) -> p h c", c=PB)
        pcm = view(NH * CB).rearrange("p (h c) -> p h c", c=CB)
        pcT = [view(T).rearrange("p (g t) -> p g t", t=P) for _ in range(2)]
        at[0] = a_d
        SELW = NPG * P + S
        SCW = SELW + WIN + S
        sc = [view(SCW), None]
        kring = [view(PGC * KV).rearrange("p (g c) -> p g c", c=KV) for _ in range(NKR)]
        kTs = [view(2 * PGC * P).rearrange("p (g n) -> p g n", g=2) for _ in range(2)]
        pTs = [view(PGC * P).rearrange("p (j q) -> p j q", q=P)]
        vring = [wring[:, s * PGC * KV:(s + 1) * PGC * KV].rearrange("p (g c) -> p g c", c=KV)
                 for s in range(2 * NSLOT)]
        sc[1] = view(SCW, a_kvt)
        osb = view(SB * 2 * G * ST).rearrange("p (b g q) -> p b g q", b=SB, g=2)
        kcs = view(2 * P).rearrange("p (g n) -> p g n", g=2)
        pTs.append(view(PGC * P).rearrange("p (j q) -> p j q", q=P))
        assert at[0] <= a_kvt + PT * 6 * KV
        at[0] = a_vcz
        psm, psg, pscT = view(P), view(P), [view(P) for _ in range(2)]
        pair, imp, imr, pen32 = view(NSB), view(NSB + 1), view(NSB + 1), view(NSB + 1)
        penq = [view(NSB + 1) for _ in range(2)]
        assert at[0] <= a_d
        a_x1 = a_kvt - SB * 2 * KV
        at[0] = a_x1
        x1 = view(TT * D).rearrange("p (i c) -> p i c", c=D)
        gqm, gqf = view(D), view(D)
        a_f = at[0]
        xr = [view(D) for _ in range(2)]
        hn = [view(D) for _ in range(2)]
        assert at[0] <= a_r
        at[0] = a_r + KD * N
        mgb = [view(N) for _ in range(2)]
        junk2 = view(D)
        at[0] = a_f
        gT = view(NF * N).rearrange("p (j n) -> p j n", n=N)
        EXS = 2 + T
        EXT = EXS + SB * (ST + 2)
        ext = [[view(EXT) for _ in range(2)] for _ in range(2)]
        CVW = EXT - 2
        cva = [[view(EXT) for _ in range(2)] for _ in range(2)]
        sge = [view(EXT) for _ in range(2)]
        cog = [view(2 * (2 + 2 * SB)) for _ in range(2)]
        NCO = 2 + 2 * SB
        cvx = view(2 * FF)
        cvi, cvo = cvx[0:2 * SB, :], cvx[32:32 + NCO, :]
        fo = view(TT * 512, a_ohg).rearrange("p (i c) -> p i c", c=512)
        junk3 = view(D)
        ftmp = view(512)
        ps = ctx.enter_context(nc.psum_tensor("ps", [P, 8, 512], F32))

        par_in = sem("par_in")
        pt_in = sem("pt_in")
        const = sem("const")
        dconst = sem("dconst")
        econst = sem("econst")
        actc = sem("actc")
        x_in = [sem("x_in0"), sem("x_in1")]
        rs_ok = sem("rs_ok")
        xn_ok = sem("xn_ok")
        xtr_ok = sem("xtr_ok")
        hT_ok = sem("hT_ok")
        w_in_s = [sem(f"w_in{i}") for i in range(NSLOT)]
        dnb_ok = sem("dnb_ok")
        proj = sem("proj")
        qg_ok = sem("qg_ok")
        cm_ok = sem("cm_ok")
        up_ok = sem("up_ok")
        ssum_ok = sem("ssum_ok")
        a_dn = sem("a_dn")
        v_dn = sem("v_dn")
        idx_ok = sem("idx_ok")
        cg_in = [sem(f"cg_in{i}") for i in range(3)]
        cg_used = sem("cg_used")
        ef_ok = sem("ef_ok")
        rr_ok = sem("rr_ok")
        lf_ok = sem("lf_ok")
        d_ok = sem("d_ok")
        ex_ok = sem("ex_ok")
        eq_ok = sem("eq_ok")
        kq_ok = sem("kq_ok")
        vt_ok = sem("vt_ok")
        s0_in = [sem("s0_in0"), sem("s0_in1")]
        ktr_ok = sem("ktr_ok")
        ktok_ok = sem("ktok_ok")
        at_ok = sem("at_ok")
        att_ok = sem("att_ok")
        vm_ok = sem("vm_ok")
        u_ok = sem("u_ok")
        st_ok = sem("st_ok")
        o_ok = sem("o_ok")
        osq_ok = sem("osq_ok")
        oss_ok = sem("oss_ok")
        ors_ok = sem("ors_ok")
        ohg_ok = sem("ohg_ok")
        hgo_out = sem("hgo_out")
        kv_ok = sem("kv_ok")
        kvo_out = sem("kvo_out")
        kT_ok = sem("kT_ok")
        nq_ok = sem("nq_ok")
        qbd_ok = sem("qbd_ok")
        ge_ok = sem("ge_ok")
        gate_ok = sem("gate_ok")
        gate_out = sem("gate_out")
        gq_in = sem("gq_in")
        csc_ok = sem("csc_ok")
        cms_ok = sem("cms_ok")
        cex_ok = sem("cex_ok")
        cpr_ok = sem("cpr_ok")
        cpt_ok = sem("cpt_ok")
        cpT_ok = sem("cpT_ok")
        sc_ok = sem("sc_ok")
        nm_ok = sem("nm_ok")
        p_ok = sem("p_ok")
        cf_ok = sem("cf_ok")
        pn_ok = sem("pn_ok")
        t_ok = sem("t_ok")
        pT_ok = sem("pT_ok")
        pv_ok = sem("pv_ok")
        on_ok = sem("on_ok")
        pg_k = [sem(f"pg_k{i}") for i in range(NKR)]
        pg_v = [sem(f"pg_v{i}") for i in range(NVR)]
        ek_ok = sem("ek_ok")
        ekT_ok = sem("ekT_ok")
        es_ok = sem("es_ok")
        esc_ok = sem("esc_ok")
        enm_ok = sem("enm_ok")
        eex_ok = sem("eex_ok")
        ecf_ok = sem("ecf_ok")
        epn_ok = sem("epn_ok")
        et_ok = sem("et_ok")
        epT_ok = sem("epT_ok")
        epv_ok = sem("epv_ok")
        eo_ok = sem("eo_ok")
        c1_ok = sem("c1_ok")
        c2_ok = sem("c2_ok")
        c3_ok = sem("c3_ok")
        c4_ok = sem("c4_ok")
        c5_ok = sem("c5_ok")
        c6_ok = sem("c6_ok")
        c7_ok = sem("c7_ok")
        c8_ok = sem("c8_ok")
        c9_ok = sem("c9_ok")
        c10_ok = sem("c10_ok")
        pq_ok = sem("pq_ok")
        sw_ok = sem("sw_ok")
        ons_ok = sem("ons_ok")
        mge_ok = sem("mge_ok")
        u_hT = sem("u_hT")
        wo_ok = sem("wo_ok")
        x1_ok = sem("x1_ok")
        xr_in = [sem("xr_in0"), sem("xr_in1")]
        cvi_in = sem("cvi_in")
        cin_ok = sem("cin_ok")
        ext_ok = sem("ext_ok")
        cnv_ok = sem("cnv_ok")
        sg_ok = sem("sg_ok")
        g_ok = sem("g_ok")
        cog_ok = sem("cog_ok")
        cot_ok = sem("cot_ok")
        cvo_ok = sem("cvo_ok")
        dn_ok = sem("dn_ok")
        fo_ok = sem("fo_ok")
        y_ok = sem("y_ok")
        y_out = sem("y_out")
        win_out = sem("win_out")

        gate_d = nc.dram_tensor("gate_scratch", (S, NH * BR), F32, kind="Internal").ap()

        cache_rows = cache_c.rearrange("l n (q r) h g d -> (l n q) (r h g d)", r=4)
        pages = cache_s.rearrange("l n r h g d -> (l n) r h (g d)")
        winr = win_kv.rearrange("l b w h g d -> (l b) w h (g d)")
        w_in3 = w_in.rearrange("l (k p) c -> p (l k) c", p=P)
        w_out3 = w_out.rearrange("l (k p) c -> p (l k) c", p=P)
        w_up3 = w_up.rearrange("l (k p) c -> p (l k) c", p=P)
        w_dn3 = w_down.rearrange("l (k p) c -> p (l k) c", p=P)
        xp2 = x_p.rearrange("b t c -> (b t) c")
        xs2 = x_s.rearrange("b t c -> (b t) c")

        def xrows(i):
            return xp2[i * P:(i + 1) * P, :] if i < PT else xs2

        def wcols(b):
            s = wslot[b % NSLOT]
            v = s.rearrange("p (k c) -> p k c", c=WB)
            if b < B_KV:
                o = [O_HF, O_HQ, O_HI, O_HG][b % 4] + P * (b // 4)
                return [(v[:, :, 0:P], w_in3[:, :, o:o + P])]
            if b < B_NQ:
                o = O_KV + WB * (b - B_KV)
                return [(v, w_in3[:, :, o:o + WB])]
            if b < B_NG:
                gp, rp = divmod(b - B_NQ, 2)
                o = O_NQ + 512 * gp + P * rp
                v4 = s.rearrange("p (k r e d) -> p k r e d", r=2, e=2, d=HD)
                return [(v4[:, :, r, e, :], w_in3[:, :, o + R * HD * e + r * HD:o + R * HD * e + (r + 1) * HD])
                        for r in range(2) for e in range(2)]
            if b < B_MG:
                return [(s[:, 0:KD * NH * BR].rearrange("p (k c) -> p k c", c=NH * BR),
                         w_in3[:, :, O_NG:O_NG + NH * BR])]
            if b < B_WO:
                o = O_MG + WB * (b - B_MG)
                return [(v, w_in3[:, :, o:o + WB])]
            if b < B_UP:
                k = 2 * (b - B_WO)
                return [(s.rearrange("p (k c) -> p k c", c=D), w_out3[:, k:k + 2, :])]
            if b < B_DN:
                j = b - B_UP
                return [(v[:, :, 0:P], w_up3[:, :, j * P:(j + 1) * P]),
                        (v[:, :, P:2 * P], w_up3[:, :, FF + j * P:FF + (j + 1) * P])]
            h, q = divmod(b - B_DN, len(DN_T))
            k, n = DN_T[q]
            return [(s[:, 0:n * 512].rearrange("p (k c) -> p k c", c=512),
                     w_dn3[:, k:k + n, h * 512:(h + 1) * 512])]

        B_ALL = B_DN + 2 * len(DN_T)
        landed, n_in = [], [0] * NSLOT
        for b in range(B_ALL):
            n_in[b % NSLOT] += 16 * len(wcols(b))
            landed.append(n_in[b % NSLOT])

        def pu(u):
            return ps[:, 2 * (u % 2):2 * (u % 2) + 2, 0:NHF]

        def halves(v):
            return v.rearrange("p (a n) -> p a n", a=2)

        def block_used(b):
            if b < B_KV:
                return proj, b + 1
            if b < B_NQ:
                return proj, U_KV + 3 * (b - B_KV) + 3
            if b < B_NG:
                return proj, U_NQ + 2 * (b - B_NQ) + 2
            if b < B_MG:
                return proj, U_NG + 1
            if b < B_WO:
                return proj, U_MG + 2 * (b - B_MG) + 2
            if b < B_UP:
                return wo_ok, TT
            if b < B_DN:
                return proj, U_UP + 2 * (b - B_UP) + 2
            h, q = divmod(b - B_DN, len(DN_T))
            return (dn_ok, TT * (h + 1)) if q == len(DN_T) - 1 else (dnb_ok, (len(DN_T) - 1) * h + q + 1)

        def cbank(b):
            return ps[:, 6 + (b + 1) % 2, :]

        block = ctx.enter_context(nc.Block())

        UNITS = [(i, h, br) for i in range(PT) for h in range(NH) for br in range(2)]
        NU = len(UNITS)
        TLAG, VLAG = 3, 5
        NP = 5
        PIECES = [[(2 * 512 * k, 1024)] for k in range(4)] + [[(NPG * P, S), (SELW, WIN + S)]]
        kland, kcount = [], [0] * NKR
        for kq in range(SB * (NPC + 1)):
            kcount[kq % NKR] += 16 * (PGC if kq % (NPC + 1) < NPC else 1)
            kland.append(kcount[kq % NKR])
        vland, vcount = [], [0] * NVR
        for kq in range(SB * (NPC + 1)):
            vcount[kq % NVR] += 16 * (PGC if kq % (NPC + 1) < NPC else 1)
            vland.append(vcount[kq % NVR])
        NCST = 27
        WSEQ = [("wo", 0)] + [x for i in range(1, TT) for x in (("wo", i), ("tr", i - 1))] + [("tr", TT - 1)]

        def head(h):
            gp, e, r = h // 8, (h // 4) % 2, h % 4
            return gp, e, gp * 4 + r

        @block.sync
        def _(sp):
            for k, a in enumerate((g_pm, g_pf)):
                sp.dma_start(prow[8 * k:8 * k + 8, :], a.rearrange("l (k p) -> (l k) p", p=P)).then_inc(par_in, 16)
            sp.dma_start(prow[16:32, :], lb_lg.rearrange("l (k p) -> (l k) p", p=P)).then_inc(par_in, 16)
            sp.dma_start(prow[32:33, :], hg_g).then_inc(par_in, 16)
            sp.dma_start(crow[0:2 * NF, 0:3, :], conv_w.rearrange("l w (c p) -> (l c) w p", p=P)).then_inc(par_in, 16)
            sp.dma_start(crow[0:2 * NF, 3, :], conv_b.rearrange("l (c p) -> (l c) p", p=P)).then_inc(par_in, 16)
            sp.dma_start(ptb[:, :], ptab.rearrange("(o b) j -> o (b j)", o=1)).then_inc(pt_in, 16)
            for i in range(TT):
                wait(sp, xn_ok, i - 1)
                sp.dma_start(xt[i % 2][0:TR[i], :], xrows(i)).then_inc(x_in[i % 2], 16)

            def weights(b):
                if b >= NSLOT:
                    sp.wait_ge(*block_used(b - NSLOT))
                for dst, src in wcols(b):
                    sp.dma_start(dst, src).then_inc(w_in_s[b % NSLOT], 16)

            for b in range(B_MG):
                weights(b)
            sp.wait_ge(gate_ok, 1)
            sp.dma_start(gate_d, gate[0:S, PT, :]).then_inc(gate_out, 16)
            sp.wait_ge(gate_out, 16)
            for h in range(NH):
                sp.dma_start(gateq[h * ST:(h + 1) * ST, :, :],
                             gate_d.rearrange("(b t) c -> t b c", t=ST)[:, :, h * BR:(h + 1) * BR]).then_inc(gq_in, 16)
            sp.wait_ge(pt_in, 80)
            sp.wait_ge(proj, U_NG + 1)
            sp.wait_ge(pv_ok, NU)
            sp.wait_ge(qbd_ok, 1)

            def page(b, j):
                return sp.value_load(ptb[0:1, b * NPG + j:b * NPG + j + 1], min_val=0, max_val=cache_s.shape[1] - 1)

            def loads(kq, ring, sems, what):
                b, c = divmod(kq, NPC + 1)
                slot = kq % len(ring)
                if c < NPC:
                    for j in range(PGC):
                        p = page(b, c * PGC + j)
                        sp.dma_start(ring[slot][:, j, :], pages[bass.ds(p, 1), :, what, :].rearrange("n r c -> (n r) c")).then_inc(sems[slot], 16)
                else:
                    sp.dma_start(ring[slot][:, :, :], winr[b].rearrange("(j p) h c -> p j h c", p=P)[:, :, what, :])\
                      .then_inc(sems[slot], 16)

            VD = 7
            for kq in range(SB * (NPC + 1) + VD):
                if kq < SB * (NPC + 1):
                    wait(sp, ek_ok, kq - NKR + 1)
                    loads(kq, kring, pg_k, 0)
                m = kq - VD
                if m >= 0:
                    if m >= NVR:
                        bb, cc = divmod(m - NVR, NPC + 1)
                        sp.wait_ge(epv_ok, NC * bb + cc + 1)
                    loads(m, vring, pg_v, 1)
            sp.wait_ge(epv_ok, NC * SB)
            sp.wait_ge(eo_ok, SB)
            sp.wait_ge(ons_ok, 1)
            sp.dma_start(gqm, g_qm.to_broadcast([P, D])).then_inc(par_in, 16)
            sp.dma_start(gqf, g_qf.to_broadcast([P, D])).then_inc(par_in, 16)
            sp.dma_start(cvi, st_cv.rearrange("l b w c -> (l b w) c")).then_inc(cvi_in, 16)
            for b in range(B_MG, B_UP):
                weights(b)
            for i in range(TT):
                wait(sp, x1_ok, i - 1)
                sp.dma_start(xr[i % 2][0:TR[i], :], xrows(i)).then_inc(xr_in[i % 2], 16)
            for b in range(B_UP, B_ALL):
                weights(b)
            sp.wait_ge(cvo_ok, NF)
            sp.dma_start(cv_p.rearrange("l b w c -> (l b w) c"), cvo[0:2, :]).then_inc(y_out, 16)
            sp.dma_start(cv_s.rearrange("l b w c -> (l b w) c"), cvo[2:NCO, :]).then_inc(y_out, 16)
            for i in range(TT):
                sp.wait_ge(y_ok, i + 1)
                dst = y_p.rearrange("b t c -> (b t) c")[i * P:(i + 1) * P, :] if i < PT else y_s.rearrange("b t c -> (b t) c")
                sp.dma_start(dst, x1[0:TR[i], i, :]).then_inc(y_out, 16)
            sp.wait_ge(y_out, 16 * (TT + 2))
            sp.wait_ge(kvo_out, 16 * (5 + SB))
            sp.wait_ge(hgo_out, 32 * HH)
            sp.wait_ge(win_out, 16 * SB)

        @block.gpsimd
        def _(pool):
            g = nc.gpsimd
            done = [0]

            def c(ins):
                ins.then_inc(const, 1)
                done[0] += 1

            for v, x in ((ident, 0.0), (ones, 1.0), (penf, 0.0), (hmask, 1.0), (hmask_s, 1.0), (scanm, 1.0),
                         (cmask, 1.0), (cmask_s, 1.0), (cm01, 1.0), (c16, 0.0), (epsc, EPS), (pnew, NEG), (zerob, 0.0)):
                c(g.memset(v[:], x))
            c(g.iota(q8i[:, :], [[0, 1]], base=0, channel_multiplier=8))
            pool.wait_ge(const, done[0])

            def sel(v, pattern, base, mult, fill, op=ALU.is_ge):
                c(g.affine_select(out=v, in_=v, pattern=pattern, compare_op=op, fill=fill, base=base,
                                  channel_multiplier=mult))

            sel(ident[:, :], [[-1, P]], 0, 1, 1.0, ALU.not_equal)
            sel(penf[:, :], [[-1, P]], 0, 1, NEG)
            sel(hmask[:, :], [[1, P]], 0, -1, 0.0)
            sel(hmask_s[:, :], [[1, S]], 0, -1, 0.0)
            c(g.memset(scanm[:, 0:T].rearrange("p (c t) -> p c t", t=CH)[:, :, 0:1], 0.0))
            c(g.memset(scanm[:, T:N].rearrange("p (c t) -> p c t", t=ST)[:, :, 0:1], 0.0))
            sel(cmask[:, :], [[-CH, CPT]], 0, 1, 0.0)
            sel(cmask_s[:, :], [[-ST, SB]], 0, 1, 0.0)
            sel(cm01[:, :, :], [[P, PT], [-CB, PB]], 1 - CB, 1, 0.0)
            sel(c16[:, 0, :], [[-1, ST]], 0, 1, NEG)
            sel(c16[:, 1, :], [[1, ST]], -1, -1, NEG)
            pool.wait_ge(const, done[0])
            sel(hmask[:, :].rearrange("p (c t) -> p c t", t=CH), [[-CH, CPT], [0, CH]], 0, 1, 0.0)
            sel(hmask_s[:, :].rearrange("p (c t) -> p c t", t=ST), [[-ST, SB], [0, ST]], 0, 1, 0.0)
            sel(cmask[:, :], [[CH, CPT]], CH - 1, -1, 0.0)
            sel(cmask_s[:, :], [[ST, SB]], ST - 1, -1, 0.0)
            assert done[0] == NCST + 2, done[0]

            pool.wait_ge(idx_ok, 1)
            gathers = [0]

            def gather(n):
                for _ in range(n):
                    k = gathers[0]
                    if k == SB * 8:
                        return
                    wait(pool, cg_used, k - 2)
                    b, q = divmod(k, 8)
                    pool.indirect_dma_start(cring[k % 3], None, cache_rows,
                                            bass.IndirectOffsetOnAxis(pidx[:, b, q:q + 1], 0)).then_inc(cg_in[k % 3], 16)
                    gathers[0] += 1

            gather(3)
            for h in range(HH + 1):
                if h < HH:
                    wait(pool, ohg_ok, h - 1)
                    pool.dma_start(s0s[h % 2], st_hg[0, :, h, :, :].rearrange("b k v -> k b v")).then_inc(s0_in[h % 2], 16)
                if h > 0:
                    o = h - 1
                    vo = vt[o % 2]
                    pool.wait_ge(vt_ok, o + 1)
                    for i in range(PT):
                        wait(pool, u_ok, 6 * (o - 1) + i + 3 if i < 2 else 6 * o + i - 1)
                        g.tensor_tensor(vm[i % 2], vo[:, i, :].unsqueeze(1).to_broadcast([P, CPT, P]),
                                        cmask[:, :].unsqueeze(2).to_broadcast([P, CPT, P]), ALU.mult).then_inc(vm_ok, 1)
                    wait(pool, u_ok, 6 * o)
                    g.tensor_tensor(vms[0:S], vo[0:S, PT, :].unsqueeze(1).to_broadcast([S, SB, P]),
                                    cmask_s[:, :].unsqueeze(2).to_broadcast([S, SB, P]), ALU.mult).then_inc(vm_ok, 1)
                    if h < HH:
                        gather(4)
                    pool.wait_ge(st_ok, 5 * h)
                    pool.dma_start(hgo_p[0, 0, o, :, :], st[:, NCH, :]).then_inc(hgo_out, 16)
                    pool.dma_start(hgo_s[0, :, o, :, :].rearrange("b k v -> k b v"), s1s).then_inc(hgo_out, 16)
                if h < HH:
                    gather(8 - 4 * (h > 0))
            for b in range(SB):
                pool.dma_start(win_s[0, b, 0:WIN - ST].rearrange("w h g d -> w (h g d)"),
                               win_kv[0, b, ST:WIN].rearrange("w h g d -> w (h g d)")).then_inc(win_out, 16)
            for n, (i, h, br) in enumerate(UNITS):
                pool.wait_ge(cf_ok, n + 1)
                v = pr[n % 4][:, 0:(i + 1) * P]
                g.tensor_scalar(v, v, cfa[:, n % 4:n % 4 + 1], None, ALU.mult).then_inc(pn_ok, 1)
            for b in range(SB):
                pool.wait_ge(ecf_ok, b + 1)
                for k, piece in enumerate(PIECES):
                    for q, (a, n) in enumerate(piece):
                        v = sc[b % 2][:, a:a + n]
                        ins = g.tensor_scalar(v, v, est[:, b % 2, 20 + (q > 0):21 + (q > 0)], None, ALU.mult)
                    ins.then_inc(epn_ok, 1)
            for j in range(NF):
                pool.wait_ge(ext_ok, j + 1)
                wait(pool, cot_ok, j - 1)
                for a in range(2):
                    e, o = ext[j % 2][a], cog[j % 2][:, a * NCO:(a + 1) * NCO]
                    g.tensor_copy(o[:, 0:2], e[:, T:T + 2])
                    ins = g.tensor_copy(o[:, 2:NCO].rearrange("p (b w) -> p b w", w=2),
                                        e[:, EXS:EXT].rearrange("p (b t) -> p b t", t=ST + 2)[:, :, ST:ST + 2])
                ins.then_inc(cog_ok, 1)

        @block.scalar
        def _(act):
            a = nc.scalar
            n_a = [0]

            def link(ins):
                ins.then_inc(a_dn, 1)
                n_a[0] += 1
                act.wait_ge(a_dn, n_a[0])

            a.preload_act_table_set("natural_log_exp_and_others")
            for q in range(4):
                act.dma_start(pti[q:P:4, :], ptab.rearrange("b j -> j b"), allow_slow_non_contiguous=True).then_inc(pt_in, 16)
            act.wait_ge(dconst, 1)
            a.activation(lbt[:, 1:3, :], lbt[:, 1:3, :], ACT.Exp).then_inc(actc, 1)

            def factor(rows, ss, rs):
                link(a.activation(rs, ss, ACT.Ln, scale=1.0 / D, bias=epsc[0:rows]))
                a.activation(rs, rs, ACT.Exp, scale=-0.5).then_inc(rs_ok, 1)

            act.wait_ge(const, NCST + 2)
            for i in range(TT):
                n = TR[i]
                act.wait_ge(x_in[i % 2], 16 * (i // 2 + 1))
                link(a.activation(junk[0:n, :], xt[i % 2][0:n, :], ACT.Square, accum_out=st_ss[0:n, 0, i:i + 1]))
                factor(n, st_ss[0:n, 0, i:i + 1], st_rs[0:n, 0, i:i + 1])

            def unit(u):
                act.wait_ge(proj, u + 1)

            def h_ef(h):
                u = 4 * h
                unit(u)
                wait(act, ohg_ok, h - 1)
                a.activation(halves(eb[h % 2]), pu(u), ACT.Exp, scale=-1.0).then_inc(ef_ok, 1)

            def h_lf(h):
                act.wait_ge(rr_ok, h + 1)
                a.activation(fb[h % 2], rb[h % 2], ACT.Ln, scale=oml[:, h:h + 1], bias=lb[:, h:h + 1]).then_inc(lf_ok, 1)

            def h_eq(h, k, buf):
                u = 4 * h + k
                unit(u)
                a.activation(halves(buf[h % 2]), pu(u), ACT.Exp, scale=-1.0).then_inc(eq_ok, 1)

            def h_v(h):
                u = 4 * h + 2
                unit(u)
                b0 = 2 * (u % 2)
                a.activation(vt[h % 2][:, 0:PT, :], ps[:, b0, :].rearrange("p (i c) -> p i c", c=P), ACT.Copy)
                a.activation(vt[h % 2][0:S, PT, :], ps[0:S, b0 + 1, 0:P], ACT.Copy).then_inc(vt_ok, 1)

            def h_exps(h):
                act.wait_ge(d_ok, h + 1)
                x, f, r = xb[h % 2], fb[h % 2], rb[h % 2]
                link(a.activation(x, f, ACT.Exp))
                a.activation(f, f, ACT.Exp, scale=-1.0)
                a.activation(r, r, ACT.Exp).then_inc(ex_ok, 1)

            def h_ktok(h):
                act.wait_ge(ktr_ok, h + 1)
                a.activation(ktok, ps[:, 4, :].rearrange("p (i t) -> p i t", t=P), ACT.Copy)
                act.wait_ge(at_ok, h + 1)
                a.activation(ktok_s[0:S, :], ps[0:S, 6, 0:P], ACT.Copy).then_inc(ktok_ok, 1)

            def h_osq(h):
                act.wait_ge(o_ok, h + 1)
                a.activation(fb[h % 2][:, 0:T], ps[:, 7, :], ACT.Square)
                a.activation(fb[h % 2][:, T:N], ps[:, 6, 192:192 + S], ACT.Square).then_inc(osq_ok, 1)

            def h_rs(h):
                act.wait_ge(oss_ok, h + 1)
                act.wait_ge(kq_ok, h + 1)
                q = qb[h % 2]
                link(a.activation(halves(q), ps[:, 4:6, 0:NHF], ACT.Ln, scale=1.0 / P, bias=epsc[:, :]))
                a.activation(q, q, ACT.Exp, scale=-0.5).then_inc(ors_ok, 1)

            def kv_rows(u):
                b, k = divmod(u - U_KV, 3)
                unit(u)
                c0 = b * KV
                if k < 2:
                    ins = a.activation(kvt[:, 2 * k:2 * k + 2, c0:c0 + KV], ps[:, 2 * (u % 2):2 * (u % 2) + 2, 0:KV], ACT.Copy)
                else:
                    ins = a.activation(kvt[0:S, PT, c0:c0 + KV], ps[0:S, 2 * (u % 2), 0:KV], ACT.Copy)
                ins.then_inc(kv_ok, 1)

            for h in range(HH + 1):
                new, old = h < HH, h > 0
                if new:
                    h_ef(h)
                else:
                    act.wait_ge(cg_used, SB * 8)
                    kv_rows(U_KV)
                if old:
                    h_ktok(h - 1)
                if new:
                    h_eq(h, 1, qb)
                    h_lf(h)
                else:
                    kv_rows(U_KV + 1)
                if new:
                    h_v(h)
                else:
                    kv_rows(U_KV + 2)
                if old:
                    h_osq(h - 1)
                if new:
                    h_exps(h)
                    h_eq(h, 3, gb)
                else:
                    kv_rows(U_KV + 3)
                if old:
                    h_rs(h - 1)
            for u in range(U_KV + 4, U_KT):
                kv_rows(u)
            act.wait_ge(kv_ok, U_KT - U_KV)
            for k, (op, os) in enumerate(((cmp_p, cmp_s), (sel_p, sel_s), (win_p, None))):
                c0 = 2 * KV * k
                act.dma_start(op[0, 0].rearrange("(i p) h g d -> p i (h g d)", p=P), kvt[:, 0:PT, c0:c0 + 2 * KV]).then_inc(kvo_out, 16)
                if os is not None:
                    act.dma_start(os[0].rearrange("b t h g d -> (b t) (h g d)"), kvt[0:S, PT, c0:c0 + 2 * KV]).then_inc(kvo_out, 16)
            for b in range(SB):
                act.dma_start(win_s[0, b, WIN - ST:WIN].rearrange("w h g d -> w (h g d)"),
                              kvt[b * ST:(b + 1) * ST, PT, C_KW:C_KW + 2 * KV]).then_inc(kvo_out, 16)
            act.wait_ge(ohg_ok, HH)
            act.wait_ge(hgo_out, 32 * HH)
            for u in range(U_KT, U_CM):
                br, gp = divmod(u - U_KT, 2)
                unit(u)
                a.activation(kT[:, br, gp, 0:T], ps[:, 2 * (u % 2), :], ACT.Copy)
                a.activation(kT[:, br, gp, T:N], ps[:, 2 * (u % 2) + 1, 0:S], ACT.Copy).then_inc(kT_ok, 1)
            for u in range(U_NQ, U_NG):
                unit(u)
                a.activation(halves(nqT[:, u - U_NQ, :]), pu(u), ACT.Copy, scale=SCALE).then_inc(nq_ok, 1)
            unit(U_NG)
            for i in range(TT):
                ins = a.activation(gate[0:TR[i], i, :], ps[0:TR[i], 2 * (U_NG % 2), i * NH * BR:(i + 1) * NH * BR], ACT.Exp, scale=-1.0)
            ins.then_inc(ge_ok, 1)

            def c_exp(i):
                act.wait_ge(cms_ok, i + 1)
                a.activation(pcw, pcw, ACT.Exp).then_inc(cex_ok, 1)

            def c_evac(i):
                act.wait_ge(cpt_ok, i + 1)
                if i >= 2:
                    act.wait_ge(pv_ok, (i - 1) * NU // PT)
                a.activation(pcT[i % 2], ps[:, 7, :].rearrange("p (g t) -> p g t", t=P), ACT.Copy).then_inc(cpT_ok, 1)

            c_exp(0)
            for n in range(NU + TLAG):
                if n < NU:
                    i, h, br = UNITS[n]
                    w = (i + 1) * P
                    act.wait_ge(nm_ok, n + 1)
                    wait(act, t_ok, n - 3)
                    a.activation(pr[n % 4][:, 0:w], ps[:, n % 3, 0:w], ACT.Exp, bias=nmx[:, n % 4:n % 4 + 1],
                                 accum_out=ssm[:, n % 4:n % 4 + 1]).then_inc(p_ok, 1)
                m = n - TLAG
                if m >= 0:
                    i, h, br = UNITS[m]
                    if m % (NU // PT) == 0:
                        c_evac(i)
                    act.wait_ge(t_ok, m + 1)
                    wait(act, pv_ok, m - 3)
                    a.activation(pT[m % 4][:, 0:i + 1, :], ps[:, 3 + m % 2, 0:(i + 1) * P].rearrange("p (j t) -> p j t", t=P),
                                 ACT.Copy).then_inc(pT_ok, 1)
                if n % (NU // PT) == NU // PT - 4 and n < NU - 4:
                    c_exp(n // (NU // PT) + 1)

            def e_c2(b):
                act.wait_ge(c1_ok, b + 1)
                a.activation(kcs, cbank(b)[:, 0:2 * P].rearrange("p (g n) -> p g n", g=2), ACT.Copy, scale=1.0 / CB).then_inc(c2_ok, 1)

            def e_c5(b):
                act.wait_ge(c4_ok, b + 1)
                a.activation(psm, cbank(b)[:, 256:384], ACT.Exp, bias=cst2[:, 0:1], accum_out=cst2[:, 1:2]).then_inc(c5_ok, 1)

            def e_c7(b):
                act.wait_ge(c7_ok, b + 1)
                if b >= 2:
                    act.wait_ge(epv_ok, NC * (b - 2) + 1)
                a.activation(pscT[b % 2], cbank(b)[:, 384:512], ACT.Copy).then_inc(c10_ok, 1)

            def e_exp(b, ks):
                for k in ks:
                    if k == 0:
                        act.wait_ge(enm_ok, b + 1)
                    for q, (o, n) in enumerate(PIECES[k]):
                        v = sc[b % 2][:, o:o + n]
                        ins = a.activation(v, v, ACT.Exp, bias=est[:, b % 2, 12 + (q > 0):13 + (q > 0)],
                                           accum_out=est[:, b % 2, 14 + k + (q > 0):15 + k + (q > 0)])
                if 4 in ks:
                    ins.then_inc(eex_ok, 1)

            act.wait_ge(pv_ok, NU)
            act.wait_ge(kvo_out, 16 * (5 + SB))
            act.wait_ge(qbd_ok, 1)
            e_c2(0)
            e_c5(0)
            e_c7(0)
            for s in range(NC * SB + LAG):
                b, c = divmod(s, NC)
                if b < SB and c <= NPC:
                    kq = b * (NPC + 1) + c
                    act.wait_ge(ek_ok, kq + 1)
                    if kq >= 2:
                        bb, cc = divmod(kq - 2, NPC + 1)
                        act.wait_ge(es_ok, NC * bb + cc + 1)
                    a.activation(kTs[kq % 2], ps[:, 0:2, :], ACT.Copy).then_inc(ekT_ok, 1)
                m = s - LAG
                if m >= 0:
                    bb, cc = divmod(m, NC)
                    act.wait_ge(et_ok, m + 1)
                    wait(act, epv_ok, m - 1)
                    src = ps[:, 4 + m % 2, :].rearrange("p (j q) -> p j q", q=P)
                    if cc < NC - 1:
                        ins = a.activation(pTs[m % 2], src, ACT.Copy)
                    else:
                        ins = a.activation(pTs[m % 2][0:S, 0:2, :], src[0:S, 0:2, :], ACT.Copy)
                    ins.then_inc(epT_ok, 1)
                if b + 1 < SB:
                    if c == 3:
                        e_c2(b + 1)
                    if c == 5:
                        e_c5(b + 1)
                    if c == 7:
                        e_c7(b + 1)
                if c == NC - 1 and b < SB:
                    e_exp(b, [0, 1])
                if c == 0 and 0 < b <= SB:
                    e_exp(b - 1, [2, 3, 4])

            for u in range(U_MG, U_UP):
                unit(u)
                wait(act, u_hT, u - U_MG - 1)
                a.activation(halves(mgb[u % 2]), pu(u), ACT.Exp, scale=-1.0)\
                    .then_inc(mge_ok, 1)

            for i in range(TT):
                n = TR[i]
                w = WSEQ.index(("wo", i)) % 4
                act.wait_ge(wo_ok, i + 1)
                link(a.activation(junk2[0:n].rearrange("p (a c) -> p a c", a=2), ps[0:n, 2 * w:2 * w + 2, :], ACT.Square,
                                  accum_out=st_ss[0:n, 1, i:i + 1]))
                factor(n, st_ss[0:n, 1, i:i + 1], st_rs[0:n, 1, i:i + 1])
                act.wait_ge(x1_ok, i + 1)
                link(a.activation(junk2[0:n], x1[0:n, i, :], ACT.Square, accum_out=st_ss[0:n, 2, i:i + 1]))
                factor(n, st_ss[0:n, 2, i:i + 1], st_rs[0:n, 2, i:i + 1])

            act.wait_ge(hT_ok, 2 * TT)
            for x in range(2):
                for y in range(2):
                    a.activation(ext[x][y][:, 0:2], ones[:, 0:2], ACT.Copy, scale=0.0)

            def f_out(j):
                act.wait_ge(cot_ok, j + 1)
                a.activation(cvo.rearrange("p (a c) -> p a c", a=2)[:, :, j * P:(j + 1) * P],
                             ps[0:NCO, 6 + j % 2, 0:2 * P].rearrange("p (a c) -> p a c", a=2), ACT.Copy).then_inc(cvo_ok, 1)

            for j in range(NF):
                act.wait_ge(cin_ok, j + 1)
                wait(act, g_ok, j - 1)
                wait(act, cog_ok, j - 1)
                for x in range(2):
                    u = U_UP + 2 * j + x
                    unit(u)
                    e = ext[j % 2][x]
                    es = e[:, EXS:EXT].rearrange("p (b t) -> p b t", t=ST + 2)
                    a.activation(e[:, 2:2 + T], ps[:, 2 * (u % 2), :], ACT.Copy)
                    a.activation(es[:, :, 2:2 + ST], ps[:, 2 * (u % 2) + 1, 0:S].rearrange("p (b t) -> p b t", t=ST), ACT.Copy)\
                        .then_inc(up_ok, 1)
                    ins = a.activation(es[:, :, 0:2], ps[:, 4 + j % 2, x * 16:(x + 1) * 16].rearrange("p (b w) -> p b w", w=2), ACT.Copy)
                ins.then_inc(ext_ok, 1)
                if j >= 1:
                    f_out(j - 1)
                act.wait_ge(cnv_ok, j + 1)
                a.activation(sge[j % 2][:, 0:CVW], cva[j % 2][0][:, 0:CVW], ACT.Exp, scale=-1.0).then_inc(sg_ok, 1)
            f_out(NF - 1)
            for h in range(2):
                for i in range(TT):
                    n = TR[i]
                    bank = (TT * h + i) % 8
                    act.wait_ge(dn_ok, TT * h + i + 1)
                    wait(act, fo_ok, TT * h + i)
                    if h == 0:
                        a.activation(junk3[0:n, 0:512], ps[0:n, bank, :], ACT.Square, accum_out=st_ss[0:n, 0, i:i + 1])
                        a.activation(fo[0:n, i, :], ps[0:n, bank, :], ACT.Copy).then_inc(fo_ok, 1)
                    else:
                        a.activation(junk3[0:n, 0:512], ps[0:n, bank, :], ACT.Square, accum_out=st_ss[0:n, 3, i:i + 1]).then_inc(fo_ok, 1)
                        act.wait_ge(ssum_ok, i + 1)
                        factor(n, st_ss[0:n, 3, i:i + 1], st_rs[0:n, 3, i:i + 1])

        @block.vector
        def _(dve):
            v = nc.vector
            n_v = [0]

            def mark(ins):
                ins.then_inc(v_dn, 1)
                n_v[0] += 1

            def link(ins):
                mark(ins)
                dve.wait_ge(v_dn, n_v[0])

            dve.wait_ge(econst, 1)
            v.tensor_copy(par[:, :], ps[:, 4, 0:33])
            link(v.tensor_copy(cpar[:, :, :], ps[:, 5, 0:8 * NF].rearrange("p (a c) -> p a c", a=4)))
            l0, l1 = par[:, 16:24], par[:, 24:32]
            link(v.tensor_tensor(lbt[:, 0, :], l0, l1, ALU.max))
            v.tensor_tensor(lbt[:, 1, :], l0, lbt[:, 0, :], ALU.subtract)
            v.tensor_tensor(lbt[:, 2, :], l1, lbt[:, 0, :], ALU.subtract).then_inc(dconst, 1)
            v.tensor_copy(identb[:, :], ident[:, :])
            v.tensor_copy(penb[:, :], penf[:, :])
            v.tensor_copy(swap[:, 0:HD], ident[:, HD:P])
            v.tensor_copy(swap[:, HD:P], ident[:, 0:HD])
            v.memset(avm[:], 0.0)
            link(v.tensor_scalar(amean[:, :], cmask[:, :], 1.0 / CB, None, ALU.mult))
            for i in range(PT):
                v.tensor_copy(avm[:, i, :, i * CPT:(i + 1) * CPT], amean[:, :].unsqueeze(1).to_broadcast([P, R, CPT]))
            v.tensor_scalar(cpen[:, :, :], cm01[:, :, :], -NEG, NEG, ALU.mult, ALU.add)
            v.tensor_reduce(rmat[:, :], ident[:, :].rearrange("p (g r t) -> p g t r", g=G, r=R), AX.X, ALU.add)
            iv = ident[0:G * ST, 0:G * ST].rearrange("p (g t) -> p g t", g=G)
            for r in range(R):
                v.tensor_copy(rmatT[:, :].rearrange("p (g r t) -> p g r t", g=G, r=R)[:, :, r, :], iv)
            link(v.tensor_copy(rep8[:, :].rearrange("p (h t) -> p h t", t=ST), ident[0:ST, 0:ST].unsqueeze(1).to_broadcast([ST, NH, ST])))
            dve.wait_ge(pt_in, 80)
            v.tensor_scalar(q8i[:, :], q8i[:, :], 24, None, ALU.bitwise_and)
            link(v.tensor_copy(ptf[:, :], pti[:, :]))
            link(v.tensor_copy(q8f[:, :], q8i[:, :]))
            link(v.tensor_scalar(ptf[:, :], ptf[:, :], 32.0, q8f[:, 0:1], ALU.mult, ALU.add))
            for q in range(8):
                ins = v.tensor_scalar(pidx[:, :, q], ptf[:, :], float(q), None, ALU.add)
            ins.then_inc(idx_ok, 1)
            dve.wait_ge(actc, 1)
            link(v.tensor_tensor(lbt[:, 0, :], lbt[:, 1, :], lbt[:, 2, :], ALU.add))
            link(v.reciprocal(lbt[:, 0, :], lbt[:, 0, :]))
            link(v.tensor_tensor(lb[:, :], lbt[:, 1, :], lbt[:, 0, :], ALU.mult))
            link(v.tensor_scalar(oml[:, :], lb[:, :], -1.0, 1.0, ALU.mult, ALU.add))
            dve.wait_ge(econst, 2)
            link(v.tensor_copy(pen8[:, :, :], ps[:, 6, 0:2 * ST].rearrange("p (a t) -> p a t", a=2)))
            for b in range(SB):
                ins = v.tensor_copy(pnew[:, b, b * ST:(b + 1) * ST], pen8[:, 0, :])
            mark(ins)

            def norm_tile(i):
                n = TR[i]
                dve.wait_ge(rs_ok, i + 1)
                wait(dve, xtr_ok, i - 1)
                v.tensor_scalar(xn[i % 2][0:n, :], xt[i % 2][0:n, :], st_rs[0:n, 0, i:i + 1], None, ALU.mult).then_inc(xn_ok, 1)

            def tile_out(i, pairn, gcol, count):
                n = TR[i]
                dve.wait_ge(xtr_ok, count)
                src = ps[:, 2 * pairn:2 * pairn + 2, :].rearrange("p a (k n) -> p (a k) n", n=P)[:, :, 0:n]
                v.tensor_tensor(hT[:, :, i * P:i * P + n], src, par[:, gcol:gcol + 8].unsqueeze(2).to_broadcast([P, KD, n]),
                                ALU.mult).then_inc(hT_ok, 1)

            norm_tile(0)
            for i in range(TT):
                if i + 1 < TT:
                    norm_tile(i + 1)
                tile_out(i, i % 2, 0, i + 1)
            mark(v.memset(att, 0.0))
            mark(v.memset(att_s, 0.0))

            sums = [0]

            def rowsum(n):
                for _ in range(n):
                    k = sums[0]
                    if k == SB * 8:
                        return
                    b, q = divmod(k, 8)
                    dve.wait_ge(cg_in[k % 3], 16 * (k // 3 + 1))
                    out = cmt[:, b, :] if q == 0 else cpart
                    ins = v.tensor_reduce(out, cring[k % 3].rearrange("p (r c) -> p c r", r=4), AX.X, ALU.add)
                    ins.then_inc(cg_used, 1)
                    dve.wait_ge(cg_used, k + 1)
                    if q:
                        link(v.tensor_tensor(cmt[:, b, :], cmt[:, b, :], cpart, ALU.add))
                    sums[0] += 1

            def prep1(h):
                e, r = eb[h % 2], rb[h % 2]
                dve.wait_ge(ef_ok, h + 1)
                link(v.tensor_scalar(e, e, 1e30, None, ALU.min))
                link(v.tensor_scalar(r, e, 1.0, None, ALU.add))
                v.reciprocal(r, r).then_inc(rr_ok, 1)
                dve.wait_ge(rr_ok, h + 1)
                mark(v.scalar_tensor_tensor(e, e, oml[:, h:h + 1], r, ALU.mult, ALU.mult))

            def prep2(h):
                r, f = rb[h % 2], fb[h % 2]
                dve.wait_ge(lf_ok, h + 1)
                dve.wait_ge(v_dn, n_v[0])
                link(v.tensor_tensor_scan(r, scanm[:, :], f, 0.0, ALU.mult, ALU.add))
                for (o, m, c, t) in ((0, T, NCH, CH), (T, S, SB, ST)):
                    rv = r[:, o:o + m].rearrange("p (c t) -> p c t", t=t)
                    ins = v.tensor_tensor(f[:, o:o + m].rearrange("p (c t) -> p c t", t=t), rv,
                                          rv[:, :, t - 1:t].to_broadcast([P, c, t]), ALU.subtract)
                ins.then_inc(d_ok, 1)

            def silu(h, k, buf, count):
                u = 4 * h + k
                b = buf[h % 2]
                dve.wait_ge(eq_ok, count)
                link(v.tensor_scalar(b, b, 1.0, None, ALU.add))
                link(v.reciprocal(b, b))
                v.tensor_tensor(halves(b), pu(u), halves(b), ALU.mult).then_inc(qg_ok, 1)

            def kq(h):
                q, e, r, f, x = qb[h % 2], eb[h % 2], rb[h % 2], fb[h % 2], xb[h % 2]
                dve.wait_ge(ex_ok, h + 1)
                dve.wait_ge(qg_ok, 2 * h + 1)
                for (o, m, t, k, n) in ((0, T, CH, 0, NCH), (T, S, ST, NCH, SB)):
                    mark(v.tensor_copy(dec[h % 2][:, k:k + n], r[:, o:o + m].rearrange("p (c t) -> p c t", t=t)[:, :, t - 1]))
                dve.wait_ge(v_dn, n_v[0])
                v.tensor_tensor(e, e, f, ALU.mult)
                v.tensor_tensor(x, x, q, ALU.mult)
                v.tensor_tensor(r, r, q, ALU.mult).then_inc(kq_ok, 1)

            def masked(h):
                dve.wait_ge(at_ok, h + 1)
                v.copy_predicated(att, hmask[:, :].bitcast(U32).unsqueeze(1).to_broadcast([P, PT, P]),
                                  ps[:, 5, :].rearrange("p (i t) -> p i t", t=P))
                dve.wait_ge(ktok_ok, h + 1)
                v.copy_predicated(att_s[0:S, :], hmask_s[:, :].bitcast(U32), ps[0:S, 6, 128:128 + S]).then_inc(att_ok, 1)

            def states(h):
                d = dec[h % 2]
                wait(dve, hgo_out, 32 * h)
                for i in range(PT):
                    dve.wait_ge(u_ok, 6 * h + i + 1)
                    for c in range(CPT):
                        k = i * CPT + c
                        up = ps[:, 4 + i % 2, c * P:(c + 1) * P]
                        if k == 0:
                            ins = v.tensor_copy(st[:, 1, :], up)
                        else:
                            ins = v.scalar_tensor_tensor(st[:, k + 1, :], st[:, k, :], d[:, k:k + 1], up, ALU.mult, ALU.add)
                        if c < CPT - 1:
                            link(ins)
                    ins.then_inc(st_ok, 1)
                    dve.wait_ge(st_ok, 5 * h + i + 1)
                dve.wait_ge(s0_in[h % 2], 16 * (h // 2 + 1))
                for b in range(SB):
                    if b % 4 == 0:
                        dve.wait_ge(u_ok, 6 * h + 5 + b // 4)
                    ins = v.scalar_tensor_tensor(s1s[:, b, :], s0s[h % 2][:, b, :], d[:, NCH + b:NCH + b + 1],
                                                 ps[:, 4 + b // 4, (b % 4) * P:(b % 4 + 1) * P], ALU.mult, ALU.add)
                ins.then_inc(st_ok, 1)

            def head_out(h):
                q = qb[h % 2]
                dve.wait_ge(ors_ok, h + 1)
                dve.wait_ge(qg_ok, 2 * h + 2)
                v.scalar_tensor_tensor(q[:, 0:T], ps[:, 7, :], par[:, 32:33], q[:, 0:T], ALU.mult, ALU.mult)
                link(v.scalar_tensor_tensor(q[:, T:N], ps[:, 6, 192:192 + S], par[:, 32:33], q[:, T:N], ALU.mult, ALU.mult))
                v.tensor_tensor(ohg[:, h, :], q, gb[h % 2], ALU.mult).then_inc(ohg_ok, 1)

            for h in range(HH + 1):
                new, old = h < HH, h > 0
                if old:
                    masked(h - 1)
                if new:
                    prep1(h)
                    rowsum(2)
                if old:
                    states(h - 1)
                if new:
                    silu(h, 1, qb, 2 * h + 1)
                    prep2(h)
                    rowsum(3)
                    kq(h)
                    silu(h, 3, gb, 2 * h + 2)
                    rowsum(3)
                if old:
                    head_out(h - 1)

            dve.wait_ge(ohg_ok, HH)
            dve.wait_ge(hgo_out, 32 * HH)
            mark(v.memset(kcz, 0.0))
            link(v.memset(vcz, 0.0))
            dve.wait_ge(proj, U_CM + 1)
            b0 = 2 * (U_CM % 2)
            for e in range(2):
                v.tensor_copy(kcz[64 * e:64 * e + 64, :, e, :], ps[64 * e:64 * e + 64, b0, 0:2 * PB].rearrange("p (g c) -> p g c", g=2))
            for r in range(R):
                ins = v.tensor_copy(vcz[CB * r:CB * r + CB, :, r, :], ps[CB * r:CB * r + CB, b0 + 1, 0:KV].rearrange("p (g d) -> p g d", g=G))
            ins.then_inc(cm_ok, 1)
            link(v.memset(qbd, 0.0))
            dve.wait_ge(nq_ok, 8)
            for gp in range(2):
                for e in range(2):
                    for r in range(R):
                        src = nqT[64 * e:64 * e + 64, 4 * gp + r, T:N].rearrange("p (b t) -> p b t", t=ST)
                        o = e * R * ST + r * ST
                        ins = v.tensor_copy(qbd[64 * e:64 * e + 64, :, gp, o:o + ST], src)
            ins.then_inc(qbd_ok, 1)
            dve.wait_ge(ge_ok, 1)
            for a, b, n in ((0, PT, P), (PT, TT, S)):
                mark(v.tensor_scalar(gate[0:n, a:b, :], gate[0:n, a:b, :], 1.0, None, ALU.add))
            dve.wait_ge(v_dn, n_v[0])
            v.reciprocal(gate[:, 0:PT, :], gate[:, 0:PT, :])
            v.reciprocal(gate[0:S, PT:TT, :], gate[0:S, PT:TT, :]).then_inc(gate_ok, 1)
            mark(v.memset(pcm, 0.0))

            gv = gate[:, :, :].rearrange("p i (h r) -> p i h r", r=BR)

            def c_scores(i):
                wait(dve, cpr_ok, i)
                dve.wait_ge(csc_ok, i + 1)
                for gp in range(2):
                    mark(v.tensor_tensor(pcw[:, 8 * gp:8 * gp + 8, :].rearrange("p (e r) c -> p e r c", e=2),
                                         ps[:, 7, gp * P:(gp + 1) * P].rearrange("p (r e c) -> p e r c", r=R, e=2),
                                         cpen[:, i:i + 1, :].unsqueeze(1).to_broadcast([P, 2, R, PB]), ALU.add))
                dve.wait_ge(v_dn, n_v[0])
                link(v.tensor_reduce(cst1[:, 0, :], pcw, AX.X, ALU.max))
                v.tensor_tensor(pcw, pcw, cst1[:, 0, :].unsqueeze(2).to_broadcast([P, NH, PB]), ALU.subtract).then_inc(cms_ok, 1)

            def c_probs(i):
                dve.wait_ge(cex_ok, i + 1)
                link(v.tensor_tensor(pcw, pcw, cm01[:, i:i + 1, :].to_broadcast([P, NH, PB]), ALU.mult))
                link(v.tensor_reduce(cst1[:, 1, :], pcw, AX.X, ALU.add))
                link(v.tensor_scalar(cst1[:, 1, :], cst1[:, 1, :], 1e-30, None, ALU.max))
                link(v.reciprocal(cst1[:, 1, :], cst1[:, 1, :]))
                link(v.tensor_tensor(cst1[:, 2, :], cst1[:, 1, :], gv[:, i, :, 0], ALU.mult))
                wait(dve, cpt_ok, i)
                v.tensor_tensor(pcm[:, :, 0:PB], pcw, cst1[:, 2, :].unsqueeze(2).to_broadcast([P, NH, PB]), ALU.mult).then_inc(cpr_ok, 1)

            def pair_out(k):
                i, hp = divmod(k, NH // 2)
                dve.wait_ge(pv_ok, 4 * (k + 1))
                v.tensor_copy(onsa[:, hp, i * P:(i + 1) * P], ps[:, 5 + k % 2, 0:P]).then_inc(on_ok, 1)

            dve.wait_ge(gate_ok, 1)
            c_scores(0)
            c_probs(0)
            for n in range(NU + VLAG + 1):
                if n < NU:
                    i, h, br = UNITS[n]
                    dve.wait_ge(sc_ok, n + 1)
                    wait(dve, p_ok, n - 3)
                    v.tensor_reduce(nmx[:, n % 4:n % 4 + 1], ps[:, n % 3, 0:(i + 1) * P], AX.X, ALU.max, negate=True).then_inc(nm_ok, 1)
                m = n - 1
                if 0 <= m < NU:
                    i, h, br = UNITS[m]
                    dve.wait_ge(p_ok, m + 1)
                    link(v.reciprocal(ssm[:, m % 4:m % 4 + 1], ssm[:, m % 4:m % 4 + 1]))
                    wait(dve, pn_ok, m - 3)
                    v.tensor_tensor(cfa[:, m % 4:m % 4 + 1], ssm[:, m % 4:m % 4 + 1], gv[:, i, h, 1 + br:2 + br], ALU.mult).then_inc(cf_ok, 1)
                m = n - VLAG - 1
                if m >= 0 and m % 4 == 3:
                    pair_out(m // 4)
                q = NU // PT
                if n % q == q - 6 and n < NU - 6:
                    c_scores(n // q + 1)
                if n % q == q - 3 and n < NU - 3:
                    c_probs(n // q + 1)

            def e_c4(b):
                dve.wait_ge(c3_ok, b + 1)
                v.tensor_reduce(cst2[:, 0:1], cbank(b)[:, 256:384], AX.X, ALU.max, negate=True).then_inc(c4_ok, 1)

            def e_c6(b):
                dve.wait_ge(c5_ok, b + 1)
                link(v.reciprocal(cst2[:, 2:3], cst2[:, 1:2]))
                link(v.tensor_scalar(psm, psm, cst2[:, 2:3], None, ALU.mult))
                wait(dve, c7_ok, b)
                v.tensor_scalar(psg, psm, gateq[:, b, 0:1], 1.0 / CB, ALU.mult, ALU.mult)
                pv2 = psm.rearrange("p (s c) -> p s c", c=2)
                v.tensor_tensor(pair, pv2[:, :, 0], pv2[:, :, 1], ALU.add).then_inc(c6_ok, 1)

            def e_c8(b):
                q = G * ST
                dve.wait_ge(c7_ok, b + 1)
                dve.wait_ge(c10_ok, b + 1)
                wait(dve, c9_ok, b)
                v.memset(imp[0:q, NSB:NSB + 1], BONUS)
                v.tensor_copy(imp[0:q, 1:NSB], cbank(b)[0:q, 1:NSB])
                link(v.tensor_scalar(imp[0:q, 0:1], cbank(b)[0:q, 0:1], BONUS, None, ALU.add))
                link(v.max(out=est[0:q, 0, 24:32], in_=imp[0:q, :]))
                link(v.match_replace(out=imr[0:q, :], in_to_replace=est[0:q, 0, 24:32], in_values=imp[0:q, :], imm_value=-1.0))
                link(v.tensor_tensor(pen32[0:q, :], imr[0:q, :], imp[0:q, :], ALU.is_equal))
                v.tensor_scalar(pen32[0:q, :], pen32[0:q, :], NEG, None, ALU.mult).then_inc(c8_ok, 1)

            def e_c10(b):
                dve.wait_ge(c9_ok, b + 1)
                v.tensor_copy(penq[b % 2], cbank(b)[:, 64:64 + NSB + 1]).then_inc(pq_ok, 1)
                dve.wait_ge(pq_ok, b + 1)

            def e_out(b):
                dve.wait_ge(epv_ok, NC * (b + 1))
                for e in range(2):
                    src = ps[64 * e:64 * e + 64, 6 + b % 2, 0:P].rearrange("p (g q) -> p g q", g=2)
                    ins = v.tensor_copy(osb[64 * e:64 * e + 64, b, :, :], src[:, :, e * R * ST:(e + 1) * R * ST])
                ins.then_inc(eo_ok, 1)

            dve.wait_ge(pv_ok, NU)
            dve.wait_ge(kvo_out, 16 * (5 + SB))
            dve.wait_ge(gq_in, 16 * NH)
            e_c4(0)
            e_c6(0)
            e_c8(0)
            e_c10(0)
            for s in range(NC * SB + LAG + 1):
                b, c = divmod(s, NC)
                w = sc[b % 2]
                if b < SB:
                    x = est[:, b % 2, :]
                    dve.wait_ge(es_ok, s + 1)
                    if c == 0 and b >= 2:
                        dve.wait_ge(et_ok, NC * (b - 1))
                    dve.wait_ge(v_dn, n_v[0])
                    bank = ps[:, 2 + s % 2, :]
                    if c < NPC:
                        link(v.tensor_tensor(w[:, c * 512:(c + 1) * 512].rearrange("p (s k) -> p s k", k=SELB),
                                             bank.rearrange("p (s k) -> p s k", k=SELB),
                                             penq[b % 2][:, 8 * c:8 * c + 8].unsqueeze(2).to_broadcast([P, 8, SELB]), ALU.add))
                        v.tensor_reduce(x[:, c:c + 1], w[:, c * 512:(c + 1) * 512], AX.X, ALU.max).then_inc(esc_ok, 1)
                    elif c == NPC:
                        v.tensor_tensor(w[:, SELW:SELW + ST], bank[:, 0:ST], pen8[:, 1, :], ALU.add)
                        link(v.tensor_copy(w[:, SELW + ST:SELW + WIN], bank[:, ST:WIN]))
                        v.tensor_reduce(x[:, 10:11], w[:, SELW:SELW + WIN], AX.X, ALU.max).then_inc(esc_ok, 1)
                    else:
                        mark(v.tensor_tensor(w[:, NPG * P:SELW], bank[:, 0:S], pnew[:, b, :], ALU.add))
                        link(v.tensor_tensor(w[:, SELW + WIN:SCW], bank[:, S:2 * S], pnew[:, b, :], ALU.add))
                        mark(v.tensor_reduce(x[:, 8:9], w[:, NPG * P:SELW], AX.X, ALU.max))
                        v.tensor_reduce(x[:, 11:12], w[:, SELW + WIN:SCW], AX.X, ALU.max).then_inc(esc_ok, 1)
                        dve.wait_ge(esc_ok, s + 1)
                        v.tensor_reduce(x[:, 12:13], x[:, 0:9], AX.X, ALU.max, negate=True)
                        v.tensor_reduce(x[:, 13:14], x[:, 10:12], AX.X, ALU.max, negate=True).then_inc(enm_ok, 1)
                if c == 1 and 0 < b <= SB:
                    y = est[:, (b - 1) % 2, :]
                    dve.wait_ge(eex_ok, b)
                    link(v.tensor_reduce(y[:, 20:21], y[:, 14:19], AX.X, ALU.add))
                    link(v.reciprocal(y[:, 20:21], y[:, 20:21]))
                    link(v.reciprocal(y[:, 21:22], y[:, 19:20]))
                    v.tensor_tensor(y[:, 20:22], y[:, 20:22], gateq[:, b - 1, 1:3], ALU.mult).then_inc(ecf_ok, 1)
                if b + 1 < SB:
                    if c == 4:
                        e_c4(b + 1)
                    if c == 5:
                        e_c6(b + 1)
                    if c == 7:
                        e_c8(b + 1)
                    if c == 9:
                        e_c10(b + 1)
                m = s - LAG - 1
                if m >= 0 and m % NC == NC - 1:
                    e_out(m // NC)
            dve.wait_ge(sw_ok, 1)
            for e in range(2):
                for gp in range(2):
                    for r in range(R):
                        h = 4 * (2 * gp + e) + r
                        d = 64 * (h % 2)
                        src = osb if h % 2 == e else ps[:, 0, :].rearrange("p (b g q) -> p b g q", b=SB, g=2)
                        ins = v.tensor_copy(onsa[d:d + 64, h // 2, T:N].rearrange("p (b t) -> p b t", t=ST),
                                            src[d:d + 64, :, gp, r * ST:(r + 1) * ST])
            ins.then_inc(ons_ok, 1)

            for u in range(U_MG, U_UP):
                k = u - U_MG
                j = k % KD
                m = mgb[u % 2]
                dve.wait_ge(mge_ok, k + 1)
                link(v.tensor_scalar(m, m, 1.0, None, ALU.add))
                link(v.reciprocal(m, m))
                if k < KD:
                    v.tensor_tensor(ohg[:, j, :], ohg[:, j, :], m, ALU.mult).then_inc(u_hT, 1)
                else:
                    if k == KD:
                        dve.wait_ge(ons_ok, 1)
                        dve.wait_ge(u_hT, KD)
                    link(v.tensor_tensor(m, onsa[:, j, :], m, ALU.mult))
                    v.tensor_tensor(ohg[:, j, :], ohg[:, j, :], m, ALU.add).then_inc(u_hT, 1)

            dve.wait_ge(par_in, 16 * 8)
            for i in range(TT + 1):
                if i < TT:
                    n = TR[i]
                    w = WSEQ.index(("wo", i)) % 4
                    dve.wait_ge(rs_ok, TT + 2 * i + 1)
                    dve.wait_ge(xr_in[i % 2], 16 * (i // 2 + 1))
                    wait(dve, xtr_ok, TT + i - 1)
                    hv = hn[i % 2][0:n]
                    link(v.scalar_tensor_tensor(hv.rearrange("p (a c) -> p a c", a=2), ps[0:n, 2 * w:2 * w + 2, :],
                                                st_rs[0:n, 1, i:i + 1], gqm[0:n].rearrange("p (a c) -> p a c", a=2), ALU.mult, ALU.mult))
                    v.tensor_tensor(x1[0:n, i, :], hv, xr[i % 2][0:n], ALU.add).then_inc(x1_ok, 1)
                if i >= 1:
                    tile_out(i - 1, WSEQ.index(("tr", i - 1)) % 4, 8, TT + i)
                if i < TT:
                    dve.wait_ge(rs_ok, TT + 2 * i + 2)
                    v.tensor_scalar(hv, x1[0:n, i, :], st_rs[0:n, 2, i:i + 1], None, ALU.mult).then_inc(xn_ok, 1)

            for j in range(NF):
                dve.wait_ge(ext_ok, j + 1)
                wait(dve, g_ok, j - 1)
                for tap in range(3):
                    for x in range(2):
                        e, o = ext[j % 2][x][:, tap:tap + CVW], cva[j % 2][x][:, 0:CVW]
                        k = x * NF + j
                        if tap == 0:
                            ins = v.tensor_scalar(o, e, cpar[:, 0, k:k + 1], cpar[:, 3, k:k + 1], ALU.mult, ALU.add)
                        else:
                            ins = v.scalar_tensor_tensor(o, e, cpar[:, tap, k:k + 1], o, ALU.mult, ALU.add)
                        if tap < 2:
                            mark(ins)
                    if tap < 2:
                        dve.wait_ge(v_dn, n_v[0])
                ins.then_inc(cnv_ok, 1)
                s = sge[j % 2][:, 0:EXT]
                dve.wait_ge(sg_ok, j + 1)
                sw = s[:, 0:CVW]
                link(v.tensor_scalar(sw, sw, 1.0, None, ALU.add))
                link(v.reciprocal(sw, sw))
                link(v.tensor_tensor(sw, sw, cva[j % 2][0][:, 0:CVW], ALU.mult))
                v.tensor_tensor(gT[:, j, 0:T], s[:, 0:T], cva[j % 2][1][:, 0:T], ALU.mult)
                s3, b3 = [y[:, EXS:EXT].rearrange("p (b t) -> p b t", t=ST + 2)[:, :, 0:ST] for y in (s, cva[j % 2][1])]
                v.tensor_tensor(gT[:, j, T:N].rearrange("p (b t) -> p b t", t=ST), s3, b3, ALU.mult).then_inc(g_ok, 1)

            for i in range(TT):
                n = TR[i]
                dve.wait_ge(fo_ok, TT + i + 1)
                v.tensor_tensor(st_ss[0:n, 3, i:i + 1], st_ss[0:n, 3, i:i + 1], st_ss[0:n, 0, i:i + 1], ALU.add).then_inc(ssum_ok, 1)
                dve.wait_ge(rs_ok, 3 * TT + i + 1)
                for h in range(2):
                    src = fo[0:n, i, :] if h == 0 else ps[0:n, (TT + i) % 8, :]
                    link(v.scalar_tensor_tensor(ftmp[0:n, :], src, st_rs[0:n, 3, i:i + 1], gqf[0:n, h * 512:(h + 1) * 512], ALU.mult, ALU.mult))
                    ins = v.tensor_tensor(x1[0:n, i, h * 512:(h + 1) * 512], x1[0:n, i, h * 512:(h + 1) * 512], ftmp[0:n, :], ALU.add)
                    if h == 0:
                        link(ins)
                    else:
                        ins.then_inc(y_ok, 1)
                dve.wait_ge(y_ok, i + 1)

        @block.tensor
        def _(pe):
            t = nc.tensor

            def weights(b):
                pe.wait_ge(w_in_s[b % NSLOT], landed[b])

            def banks_free(u):
                o = u - 2
                if o < 0:
                    return
                if o < U_KV:
                    h, k = divmod(o, 4)
                    if k == 0:
                        pe.wait_ge(ef_ok, h + 1)
                    elif k == 2:
                        pe.wait_ge(vt_ok, h + 1)
                    else:
                        pe.wait_ge(qg_ok, 2 * h + 1 + k // 2)
                elif o < U_KT:
                    pe.wait_ge(kv_ok, o - U_KV + 1)
                elif o < U_CM:
                    pe.wait_ge(kT_ok, o - U_KT + 1)
                elif o < U_NQ:
                    pe.wait_ge(cm_ok, 1)
                elif o < U_NG:
                    pe.wait_ge(nq_ok, o - U_NQ + 1)
                elif o < U_MG:
                    pe.wait_ge(ge_ok, 1)
                elif o < U_UP:
                    pe.wait_ge(mge_ok, o - U_MG + 1)
                else:
                    pe.wait_ge(up_ok, o - U_UP + 1)

            def feature(u, lhs, last_of=False):
                banks_free(u)
                for a in range(2):
                    for k in range(KD):
                        mm = t.matmul(ps[:, 2 * (u % 2) + a, 0:NHF], lhs(k), hT[:, k, a * NHF:(a + 1) * NHF],
                                      start=(k == 0), stop=(k == KD - 1))
                mm.then_inc(proj, 1)

            def rows(u, k3, b):
                banks_free(u)
                w = wslot[b % NSLOT].rearrange("p (k c) -> p k c", c=WB)
                for a, i in enumerate(range(2 * k3, min(2 * k3 + 2, TT))):
                    n = TR[i]
                    for k in range(KD):
                        mm = t.matmul(ps[0:n, 2 * (u % 2) + a, 0:WB], hT[:, k, i * P:i * P + n], w[:, k, :],
                                      start=(k == 0), stop=(k == KD - 1))
                mm.then_inc(proj, 1)

            def wcol(b, m):
                w = wslot[b % NSLOT].rearrange("p (k c) -> p k c", c=WB)
                return lambda k: w[:, k, m * P:(m + 1) * P]

            def head_unit(h, k):
                u = b = 4 * h + k
                weights(b)
                if k != 2:
                    feature(u, wcol(b, 0))
                    return
                banks_free(u)
                for i in range(TT):
                    n = TR[i]
                    for j in range(KD):
                        mm = t.matmul(ps[0:n, 2 * (u % 2) + i // PT, (i % PT) * P:(i % PT + 1) * P], hT[:, j, i * P:i * P + n],
                                      wcol(b, 0)(j), start=(j == 0), stop=(j == KD - 1))
                mm.then_inc(proj, 1)

            pe.wait_ge(par_in, 96)
            pe.wait_ge(const, NCST + 2)
            t.transpose(ps[:, 4, 0:33], prow[:, :], ident[0:33, 0:33])
            for k in range(4):
                mm = t.transpose(ps[:, 5, 2 * NF * k:2 * NF * (k + 1)], crow[0:2 * NF, k, :], ident[0:2 * NF, 0:2 * NF])
            mm.then_inc(econst, 1)
            pe.wait_ge(idx_ok, 1)
            t.matmul(ps[:, 6, 0:2 * ST], rep8[:, :], c16[:, :, :], start=True, stop=True).then_inc(econst, 1)

            def transposes(i, pairn, src):
                n = TR[i]
                for k in range(KD):
                    mm = t.transpose(ps[:, 2 * pairn + k // 4, (k % 4) * P:(k % 4) * P + n], src[0:n, k * P:(k + 1) * P],
                                     ident[0:n, 0:n])
                mm.then_inc(xtr_ok, 1)

            for i in range(TT):
                pe.wait_ge(xn_ok, i + 1)
                wait(pe, hT_ok, i - 1)
                transposes(i, i % 2, xn[i % 2])

            def h_keys(h):
                e, x = eb[h % 2], xb[h % 2]
                pe.wait_ge(kq_ok, h + 1)
                wait(pe, ohg_ok, h)
                if h == 0:
                    pe.wait_ge(econst, 2)
                    pe.wait_ge(dconst, 1)
                for i in range(PT):
                    t.transpose(ps[:, 4, i * P:(i + 1) * P], e[:, i * P:(i + 1) * P], ident[:, :])
                t.transpose(ps[0:S, 6, 0:P], e[:, T:N], ident[:, :]).then_inc(ktr_ok, 1)
                for i in range(PT):
                    t.matmul(ps[:, 5, i * P:(i + 1) * P], e[:, i * P:(i + 1) * P], x[:, i * P:(i + 1) * P], start=True, stop=True)
                t.matmul(ps[0:S, 6, 128:128 + S], e[:, T:N], x[:, T:N], start=True, stop=True).then_inc(at_ok, 1)

            def h_updates(h):
                pe.wait_ge(ktok_ok, h + 1)
                pe.wait_ge(att_ok, h + 1)
                for i in range(PT):
                    pe.wait_ge(vm_ok, 5 * h + i + 1)
                    if i >= 2:
                        pe.wait_ge(st_ok, 5 * h + i - 1)
                    t.matmul(ps[:, 4 + i % 2, :], ktok[:, i, :], vm[i % 2].rearrange("p c v -> p (c v)"), start=True, stop=True)\
                        .then_inc(u_ok, 1)
                pe.wait_ge(vm_ok, 5 * h + 5)
                for a in range(2):
                    pe.wait_ge(st_ok, 5 * h + 3 + a)
                    t.matmul(ps[:, 4 + a, :], ktok_s[0:S, :], vms[0:S, 4 * a:4 * a + 4, :].rearrange("p b v -> p (b v)"),
                             start=True, stop=True).then_inc(u_ok, 1)

            def h_out(h):
                r = rb[h % 2]
                vv = vt[h % 2]
                pe.wait_ge(vt_ok, h + 1)
                for i in range(PT):
                    pe.wait_ge(st_ok, 5 * h + i + 1)
                    t.matmul(ps[:, 7, i * P:(i + 1) * P], vv[:, i, :], att[:, i, :], start=True, stop=False,
                             skip_group_check=True)
                    for c in range(CPT):
                        k = i * CPT + c
                        if k:
                            t.matmul(ps[:, 7, k * CH:(k + 1) * CH], st[:, k, :], r[:, k * CH:(k + 1) * CH], start=False,
                                     stop=(c == CPT - 1), skip_group_check=True)
                t.matmul(ps[:, 6, 192:192 + S], vv[0:S, PT, :], att_s[0:S, :], start=True, stop=False, skip_group_check=True)
                pe.wait_ge(s0_in[h % 2], 16 * (h // 2 + 1))
                for b in range(SB):
                    mm = t.matmul(ps[:, 6, 192 + b * ST:192 + (b + 1) * ST], s0s[h % 2][:, b, :], r[:, T + b * ST:T + (b + 1) * ST],
                                  start=False, stop=(b == SB - 1), skip_group_check=True)
                mm.then_inc(o_ok, 1)

            def h_sums(h):
                pe.wait_ge(osq_ok, h + 1)
                pe.wait_ge(st_ok, 5 * h + 5)
                for a in range(2):
                    mm = t.matmul(ps[:, 4 + a, 0:NHF], ones[:, :], fb[h % 2][:, a * NHF:(a + 1) * NHF], start=True, stop=True)
                mm.then_inc(oss_ok, 1)

            def kv_unit(u):
                b, k = divmod(u - U_KV, 3)
                if k == 0:
                    weights(B_KV + b)
                rows(u, k, B_KV + b)

            pe.wait_ge(hT_ok, TT)
            STAGES = (h_keys, h_updates, h_out, h_sums)
            for h in range(HH + 1):
                for k in range(4):
                    if h < HH:
                        head_unit(h, k)
                    else:
                        kv_unit(U_KV + k)
                    if h > 0:
                        STAGES[k](h - 1)
            for u in range(U_KV + 4, U_KT):
                kv_unit(u)

            pe.wait_ge(kv_ok, U_KT - U_KV)
            for u in range(U_KT, U_CM):
                br, gp = divmod(u - U_KT, 2)
                c0 = (C_KS, C_KW)[br] + gp * P
                banks_free(u)
                for i in range(TT):
                    n = TR[i]
                    mm = t.transpose(ps[:, 2 * (u % 2) + i // PT, (i % PT) * P:(i % PT) * P + n], kvt[0:n, i, c0:c0 + P], ident[0:n, 0:n])
                mm.then_inc(proj, 1)
            banks_free(U_CM)
            b0 = 2 * (U_CM % 2)
            for gp in range(2):
                for i in range(PT):
                    t.matmul(ps[:, b0, gp * PB + i * CPT:gp * PB + (i + 1) * CPT], kvt[:, i, gp * P:(gp + 1) * P], amean[:, :],
                             start=True, stop=True)
            for i in range(PT):
                mm = t.matmul(ps[:, b0 + 1, 0:KV], avm[:, i, :, :].rearrange("p r c -> p (r c)"), kvt[:, i, KV:2 * KV],
                              start=(i == 0), stop=(i == PT - 1))
            mm.then_inc(proj, 1)
            for u in range(U_NQ, U_NG):
                j = u - U_NQ
                b = B_NQ + j // 2
                if j % 2 == 0:
                    weights(b)
                feature(u, wcol(b, j % 2))
            banks_free(U_NG)
            weights(B_NG)
            w = wslot[B_NG % NSLOT][:, 0:KD * NH * BR].rearrange("p (k c) -> p k c", c=NH * BR)
            for i in range(TT):
                n = TR[i]
                for k in range(KD):
                    mm = t.matmul(ps[0:n, 2 * (U_NG % 2), i * NH * BR:(i + 1) * NH * BR], hT[:, k, i * P:i * P + n], w[:, k, :],
                                  start=(k == 0), stop=(k == KD - 1))
            mm.then_inc(proj, 1)

            def c_scores(i):
                if i:
                    pe.wait_ge(cpT_ok, i)
                for j in range(8):
                    gp = j // R
                    mm = t.matmul(ps[:, 7, j * 2 * PB:(j + 1) * 2 * PB], nqT[:, j, i * P:(i + 1) * P],
                                  kcz[:, gp, :, :].rearrange("p e c -> p (e c)"), start=True, stop=True)
                mm.then_inc(csc_ok, 1)

            def c_transposes(i):
                pe.wait_ge(cpr_ok, i + 1)
                for g in range(G):
                    mm = t.transpose(ps[:, 7, g * P:(g + 1) * P], pcm[:, g * R:(g + 1) * R, :].rearrange("p r c -> p (r c)"), ident[:, :])
                mm.then_inc(cpt_ok, 1)

            def values(m):
                i, h, br = UNITS[m]
                gp, e, tile = head(h)
                g = h // R
                k = i * (NH // 2) + h // 2
                out = ps[64 * (h % 2):64 * (h % 2) + 64, 5 + k % 2, 0:P]
                if br == 0:
                    if h == 0:
                        pe.wait_ge(cpT_ok, i + 1)
                    if h % 2 == 0:
                        wait(pe, on_ok, k - 1)
                    t.matmul(out, vcz[:, g, h % R, :], pcT[i % 2][:, g, :], start=True, stop=False, skip_group_check=True)
                pe.wait_ge(pT_ok, m + 1)
                c0 = (C_VS, C_VW)[br] + g * HD
                for j in range(i + 1):
                    mm = t.matmul(out, kvt[:, j, c0:c0 + HD], pT[m % 4][:, j, :], start=False, stop=(br == 1 and j == i),
                                  skip_group_check=True)
                mm.then_inc(pv_ok, 1)

            pe.wait_ge(nq_ok, 8)
            pe.wait_ge(cm_ok, 1)
            pe.wait_ge(kT_ok, 4)
            pe.wait_ge(ge_ok, 1)
            c_scores(0)
            q = NU // PT
            for n in range(NU + VLAG):
                if n < NU:
                    i, h, br = UNITS[n]
                    gp, e, tile = head(h)
                    w = (i + 1) * P
                    wait(pe, p_ok, n - 2)
                    wait(pe, nm_ok, n - 2)
                    t.matmul(ps[:, n % 3, 0:w], nqT[64 * e:64 * e + 64, tile, i * P:w], kT[64 * e:64 * e + 64, br, gp, 0:w],
                             start=True, stop=False, skip_group_check=True)
                    t.matmul(ps[:, n % 3, i * P:w], identb[:, :], penb[:, :], start=False, stop=True, skip_group_check=True)\
                        .then_inc(sc_ok, 1)
                m = n - TLAG
                if 0 <= m < NU:
                    i, h, br = UNITS[m]
                    if m % q == 0:
                        c_transposes(i)
                    pe.wait_ge(pn_ok, m + 1)
                    wait(pe, pT_ok, m - 1)
                    for j in range(i + 1):
                        mm = t.transpose(ps[:, 3 + m % 2, j * P:(j + 1) * P], pr[m % 4][:, j * P:(j + 1) * P], ident[:, :])
                    mm.then_inc(t_ok, 1)
                m = n - VLAG
                if m >= 0:
                    values(m)
                if n % q == q - 6 and n < NU - 6:
                    c_scores(n // q + 1)

            def e_c1(b):
                wait(pe, eo_ok, b - 2)
                for gp in range(2):
                    mm = t.transpose(cbank(b)[:, gp * P:(gp + 1) * P], cmt[:, b, gp * P:(gp + 1) * P], ident[:, :])
                mm.then_inc(c1_ok, 1)

            def e_c3(b):
                pe.wait_ge(c2_ok, b + 1)
                for gp in range(2):
                    mm = t.matmul(cbank(b)[64 * gp:64 * gp + 64, 256:384], qbd[:, b, gp, :], kcs[:, gp, :], start=True, stop=True)
                mm.then_inc(c3_ok, 1)

            def e_c7(b):
                pe.wait_ge(c6_ok, b + 1)
                t.transpose(cbank(b)[:, 384:512], psg, ident[:, :])
                t.matmul(cbank(b)[0:G * ST, 0:NSB], rmat[:, :], pair, start=True, stop=True).then_inc(c7_ok, 1)

            def e_c9(b):
                pe.wait_ge(c8_ok, b + 1)
                t.matmul(cbank(b)[:, 64:64 + NSB + 1], rmatT[:, :], pen32[0:G * ST, :], start=True, stop=True).then_inc(c9_ok, 1)

            pe.wait_ge(on_ok, PT * NH // 2)
            pe.wait_ge(qbd_ok, 1)
            e_c1(0)
            e_c3(0)
            e_c7(0)
            e_c9(0)
            pe.wait_ge(p_ok, NU)
            for s in range(NC * SB + LAG):
                b, c = divmod(s, NC)
                m = s - LAG
                bb, cc = divmod(m, NC)
                keys = b < SB and c <= NPC
                kq = b * (NPC + 1) + c
                if keys:
                    pe.wait_ge(pg_k[kq % NKR], kland[kq])
                    wait(pe, ekT_ok, kq)
                    for gp in range(2):
                        for j in range(PGC):
                            mm = t.transpose(ps[:, gp, j * P:(j + 1) * P], kring[kq % NKR][:, j, gp * P:(gp + 1) * P], ident[:, :])
                    mm.then_inc(ek_ok, 1)
                if m >= 0:
                    pe.wait_ge(epn_ok, NP * bb + min(cc // 2, NP - 1) + 1)
                    wait(pe, epT_ok, m - 1)
                    if cc < NC - 1:
                        o = cc * 512 if cc < NPC else SELW
                        for j in range(PGC):
                            mm = t.transpose(ps[:, 4 + m % 2, j * P:(j + 1) * P], sc[bb % 2][:, o + j * P:o + (j + 1) * P], ident[:, :])
                    else:
                        for j, o in enumerate((NPG * P, SELW + WIN)):
                            mm = t.transpose(ps[0:S, 4 + m % 2, j * P:(j + 1) * P], sc[bb % 2][:, o:o + S], ident[:, :])
                    mm.then_inc(et_ok, 1)
                if b < SB:
                    wait(pe, esc_ok, s - 1)
                    for gp in range(2):
                        out = ps[64 * gp:64 * gp + 64, 2 + s % 2, :]
                        if keys:
                            if gp == 0:
                                pe.wait_ge(ekT_ok, kq + 1)
                            mm = t.matmul(out, qbd[:, b, gp, :], kTs[kq % 2][:, gp, :], start=True, stop=True)
                        else:
                            for br in range(2):
                                mm = t.matmul(out[:, br * S:(br + 1) * S], qbd[:, b, gp, :], kT[:, br, gp, T:N], start=True, stop=True)
                    mm.then_inc(es_ok, 1)
                if m >= 0:
                    ob = 6 + bb % 2
                    if cc == 0:
                        wait(pe, eo_ok, bb - 1)
                        pe.wait_ge(c10_ok, bb + 1)
                        pe.wait_ge(pq_ok, min(bb + 2, SB))
                        t.matmul(ps[:, ob, 0:P], identb[:, :], zerob[:, :], start=True, stop=False, skip_group_check=True)
                        for gp in range(2):
                            t.matmul(ps[:, ob, gp * S:(gp + 1) * S], cmt[:, bb, KV + gp * P:KV + (gp + 1) * P],
                                     pscT[bb % 2][:, gp * S:(gp + 1) * S], start=False, stop=False, skip_group_check=True)
                    pe.wait_ge(epT_ok, m + 1)
                    if cc <= NPC:
                        vq = bb * (NPC + 1) + cc
                        pe.wait_ge(pg_v[vq % NVR], vland[vq])
                    for gp in range(2):
                        out = ps[:, ob, gp * S:(gp + 1) * S]
                        if cc <= NPC:
                            for j in range(PGC):
                                mm = t.matmul(out, vring[vq % NVR][:, j, gp * P:(gp + 1) * P], pTs[m % 2][:, j, gp * S:(gp + 1) * S],
                                              start=False, stop=False, skip_group_check=True)
                        else:
                            for br in range(2):
                                c0 = (C_VS, C_VW)[br] + gp * P
                                mm = t.matmul(out, kvt[0:S, PT, c0:c0 + P], pTs[m % 2][0:S, br, gp * S:(gp + 1) * S],
                                              start=False, stop=(br == 1), skip_group_check=True)
                    mm.then_inc(epv_ok, 1)
                if b + 1 < SB:
                    if c == 3:
                        e_c1(b + 1)
                    if c == 4:
                        e_c3(b + 1)
                    if c == 6:
                        e_c7(b + 1)
                    if c == 8:
                        e_c9(b + 1)
            pe.wait_ge(eo_ok, SB)
            t.matmul(ps[:, 0, :], swap[:, :], osb.rearrange("p b g q -> p (b g q)"), start=True, stop=True).then_inc(sw_ok, 1)
            pe.wait_ge(ons_ok, 1)

            for u in range(U_MG, U_UP):
                b = B_MG + (u - U_MG) // 2
                if (u - U_MG) % 2 == 0:
                    weights(b)
                feature(u, wcol(b, (u - U_MG) % 2))

            pe.wait_ge(u_hT, 2 * KD)
            for idx, (what, i) in enumerate(WSEQ):
                w = idx % 4
                if idx >= 4:
                    ww, j = WSEQ[idx - 4]
                    pe.wait_ge(x1_ok if ww == "wo" else hT_ok, j + 1 if ww == "wo" else TT + j + 1)
                n = TR[i]
                if what == "tr":
                    pe.wait_ge(xn_ok, TT + i + 1)
                    transposes(i, w, hn[i % 2])
                    continue
                for b in range(B_WO, B_UP):
                    if i == 0:
                        weights(b)
                for a in range(2):
                    for k in range(KD):
                        ws = wslot[(B_WO + k // 2) % NSLOT].rearrange("p (k c) -> p k c", c=D)
                        mm = t.matmul(ps[0:n, 2 * w + a, :], ohg[:, k, i * P:i * P + n], ws[:, k % 2, a * 512:(a + 1) * 512],
                                      start=(k == 0), stop=(k == KD - 1))
                mm.then_inc(wo_ok, 1)

            def cin(j):
                wait(pe, ext_ok, j - 1)
                for x in range(2):
                    mm = t.transpose(ps[:, 4 + j % 2, x * 2 * SB:(x + 1) * 2 * SB], cvi[:, x * FF + j * P:x * FF + (j + 1) * P],
                                     ident[0:2 * SB, 0:2 * SB])
                mm.then_inc(cin_ok, 1)

            def cot(j):
                pe.wait_ge(cog_ok, j + 1)
                wait(pe, cvo_ok, j - 1)
                for x in range(2):
                    mm = t.transpose(ps[0:NCO, 6 + j % 2, x * P:(x + 1) * P], cog[j % 2][:, x * NCO:(x + 1) * NCO], ident[:, :])
                mm.then_inc(cot_ok, 1)

            pe.wait_ge(hT_ok, 2 * TT)
            pe.wait_ge(cvi_in, 16)
            for j in range(NF):
                cin(j)
                weights(B_UP + j)
                for x in range(2):
                    u = U_UP + 2 * j + x
                    banks_free(u)
                    lhs = wcol(B_UP + j, x)
                    for a, (o, n) in enumerate(((0, T), (T, S))):
                        for k in range(KD):
                            mm = t.matmul(ps[:, 2 * (u % 2) + a, 0:n], lhs(k), hT[:, k, o:o + n], start=(k == 0), stop=(k == KD - 1))
                    mm.then_inc(proj, 1)
                if j >= 1:
                    cot(j - 1)
            cot(NF - 1)
            pe.wait_ge(up_ok, 2 * NF)
            pe.wait_ge(ext_ok, NF)
            for h in range(2):
                if h == 1:
                    pe.wait_ge(cvo_ok, NF)
                for q, (k0, nk) in enumerate(DN_T):
                    b = B_DN + h * len(DN_T) + q
                    weights(b)
                    ws = wslot[b % NSLOT].rearrange("p (k c) -> p k c", c=512)
                    for k in range(k0, k0 + nk):
                        if h == 0:
                            pe.wait_ge(g_ok, k + 1)
                        for i in range(TT):
                            n = TR[i]
                            bank = (TT * h + i) % 8
                            if k == 0 and TT * h + i >= 8:
                                pe.wait_ge(fo_ok, TT * h + i - 8 + 1)
                            mm = t.matmul(ps[0:n, bank, :], gT[:, k, i * P:i * P + n], ws[:, k - k0, :], start=(k == 0), stop=(k == NF - 1))
                            if k == NF - 1:
                                mm.then_inc(dn_ok, 1)
                    if q < len(DN_T) - 1:
                        mm.then_inc(dnb_ok, 1)


_INS = ['x_prompt', 'x_sample', 'cache_cmp_kv', 'cache_sel_kv', 'page_table', 'state_win_kv', 'state_hgrn', 'state_conv',
        'w_in', 'hg_lb_logits', 'hg_norm_g', 'w_out', 'w_up', 'conv_w', 'conv_b', 'w_down',
        'g_pre_mix', 'g_post_mix', 'g_pre_ffn', 'g_post_ffn']
_OUTS = [(1, T, D), (SB, ST, D), (1, 1, T, 2, G, HD), (1, SB, ST, 2, G, HD), (1, 1, T, 2, G, HD), (1, SB, ST, 2, G, HD),
         (1, 1, WIN, 2, G, HD), (1, SB, WIN, 2, G, HD), (1, 1, HH, P, P), (1, SB, HH, P, P), (1, 1, 2, 2 * FF), (1, SB, 2, 2 * FF)]


def kernel(**inputs):
    import concourse.bacc as bacc
    from concourse.bass_utils import run_bass_kernel_spmd

    nc = bacc.Bacc("TRN2", target_bir_lowering=False, num_devices=1)
    arrays, args = {}, []
    for name in _INS:
        a = np.ascontiguousarray(inputs[name])
        arrays[f"in_{name}"] = a
        args.append(nc.dram_tensor(f"in_{name}", a.shape, mybir.dt.from_np(a.dtype), kind="ExternalInput").ap())
    for i, shape in enumerate(_OUTS):
        args.append(nc.dram_tensor(f"out_{i}", shape, F32, kind="ExternalOutput").ap())
    build(nc, *args)
    r = run_bass_kernel_spmd(nc, [arrays], core_ids=[0])
    return tuple(r.results[0][f"out_{i}"] for i in range(len(_OUTS)))
```

```python
import numpy as np
import concourse.bass as bass
from concourse import mybir
from contextlib import ExitStack

F32 = mybir.dt.float32
BF16 = mybir.dt.bfloat16
U32 = mybir.dt.uint32
I32 = mybir.dt.int32
ALU = mybir.AluOpType
ACT = mybir.ActivationFunctionType
AX = mybir.AxisListType

P = 128
D = 1024
T = 512
SB = 8
ST = 8
S = SB * ST
N = T + S
NHF = N // 2
KD = D // P
PT = T // P
TT = PT + 1
TR = [P] * PT + [S]
HH = 8
CH = 32
NCH = T // CH
CPT = P // CH
NH, G, R, HD = 16, 4, 4, 64
KV = G * HD
BR = 3
CB = 32
PB = T // CB
NPG = 32
SELB = 64
NSB = NPG * P // SELB
WIN = 512
FF = 2816
NF = FF // P
EPS = 1e-6
NEG = -1.0e30
BONUS = 1.0e4
SCALE = HD ** -0.5
WB = 256
O_HQ, O_HF, O_HI, O_HG, O_NQ, O_KV = 0, D, 2 * D, 3 * D, 4 * D, 5 * D
O_NG = O_KV + 6 * KV
O_MG = O_NG + NH * BR
C_KS, C_VS, C_KW, C_VW = 2 * KV, 3 * KV, 4 * KV, 5 * KV
NSLOT = 4
U_KV = 4 * HH
U_KT = U_KV + 18
U_CM = U_KT + 4
U_NQ = U_CM + 1
U_NG = U_NQ + 8
U_MG = U_NG + 1
U_UP = U_MG + 16
B_KV = 4 * HH
B_NQ = B_KV + 6
B_NG = B_NQ + 4
B_MG = B_NG + 1
B_WO = B_MG + 8
B_UP = B_WO + 4
B_DN = B_UP + NF
DN_T = [(0, 4), (4, 4), (8, 4), (12, 4), (16, 4), (20, 2)]
PGC = 4
NPC = NPG // PGC
NC = NPC + 2
LAG = NC + 6
K_POOL = (0, 1, 2)
KAHEAD, VAHEAD = 4, 3
NKR, NVR = 6, 5


def wait(eng, semaphore, value):
    if value > 0:
        eng.wait_ge(semaphore, value)


def build(nc, x_p, x_s, cache_c, cache_s, ptab, win_kv, st_hg, st_cv, w_in, lb_lg, hg_g, w_out, w_up,
          conv_w, conv_b, w_down, g_pm, g_qm, g_pf, g_qf,
          y_p, y_s, cmp_p, cmp_s, sel_p, sel_s, win_p, win_s, hgo_p, hgo_s, cv_p, cv_s):
    ctx = ExitStack()
    with ctx:
        def sb(name, shape, dt=F32):
            return ctx.enter_context(nc.sbuf_tensor(name, shape, dt))

        def sem(name):
            return ctx.enter_context(nc.semaphore(name))

        ident = sb("ident", [P, P])
        identb = sb("identb", [P, P], BF16)
        ones = sb("ones", [P, P])
        zerob = sb("zerob", [P, P], BF16)
        penf = sb("penf", [P, P])
        penb = sb("penb", [P, P], BF16)
        hmask = sb("hmask", [P, P])
        hmask_s = sb("hmask_s", [S, S])
        scanm = sb("scanm", [P, N])
        cmask = sb("cmask", [P, CPT])
        cmask_s = sb("cmask_s", [S, SB])
        amean = sb("amean", [P, CPT])
        avm = sb("avm", [P, PT, R, CB])
        cm01 = sb("cm01", [P, PT, PB])
        cpen = sb("cpen", [P, PT, PB])
        rmat = sb("rmat", [P, G * ST])
        rmatT = sb("rmatT", [G * ST, P])
        rep8 = sb("rep8", [ST, P])
        c16 = sb("c16", [ST, 2, ST])
        pen8 = sb("pen8", [P, 2, ST])
        pnew = sb("pnew", [P, SB, S])
        epsc = sb("epsc", [P, 1])
        prow = sb("prow", [33, P])
        par = sb("par", [P, 33])
        cpar = sb("cpar", [P, 4, 2 * NF])
        lbt = sb("lbt", [P, 4, HH])
        lb = sb("lb", [P, HH])
        oml = sb("oml", [P, HH])
        q4i = sb("q4i", [P, 1], I32)
        q4f = sb("q4f", [P, 1])
        sidx = sb("sidx", [P, SB * NPG], U32)
        pti = sb("pti", [P, SB], I32)
        ptf = sb("ptf", [P, SB])
        q8i = sb("q8i", [P, 1], I32)
        q8f = sb("q8f", [P, 1])
        pidx = sb("pidx", [P, SB, 8], U32)
        gate = sb("gate", [P, TT, NH * BR])
        gateq = sb("gateq", [P, SB, BR])
        st_ss = sb("st_ss", [P, 4, TT])
        st_rs = sb("st_rs", [P, 4, TT])
        nmx = sb("nmx", [P, 4])
        ssm = sb("ssm", [P, 4])
        cst1 = sb("cst1", [P, 3, NH])
        est = sb("est", [P, 2, 32])
        cst2 = sb("cst2", [P, 4])

        M = 48892
        mem = sb("mem", [P, M])
        at = [0]

        def view(n, start=None):
            a = at[0] if start is None else start
            at[0] = a + n
            assert at[0] <= M, (at[0], M)
            return mem[:, a:a + n]

        hT = view(KD * N).rearrange("p (k n) -> p k n", n=N)
        a_ohg = at[0]
        ohg = view(KD * N).rearrange("p (k n) -> p k n", n=N)
        wring = view(NSLOT * KD * WB)
        wslot = [wring[:, s * KD * WB:(s + 1) * KD * WB] for s in range(NSLOT)]
        cmt = view(SB * 2 * KV).rearrange("p (b c) -> p b c", c=2 * KV)
        a_kvt = at[0]
        kvt = view(TT * 6 * KV).rearrange("p (i c) -> p i c", c=6 * KV)
        a_r = at[0]
        CROW = 4 * 2 * KV
        cring = [view(CROW, a_kvt + i * CROW) for i in range(3)]
        cpart = view(2 * KV)
        at[0] = a_r
        qb, gb, eb, rb, fb, xb = [[view(N) for _ in range(2)] for _ in range(6)]
        vt = [view(TT * P).rearrange("p (i c) -> p i c", c=P) for _ in range(2)]
        vm = [view(CPT * P).rearrange("p (c v) -> p c v", v=P) for _ in range(PT)]
        vms = view(SB * P).rearrange("p (b v) -> p b v", v=P)
        att = view(T).rearrange("p (i t) -> p i t", t=P)
        att_s = view(S)
        ktok = view(T).rearrange("p (i t) -> p i t", t=P)
        ktok_s = view(P)
        dec = [view(NCH + SB) for _ in range(2)]
        st = view((NCH + 1) * P).rearrange("p (c v) -> p c v", v=P)
        s0s = [view(SB * P).rearrange("p (b v) -> p b v", v=P) for _ in range(2)]
        s1s = view(SB * P).rearrange("p (b v) -> p b v", v=P)
        at[0] = a_r
        xt = [view(D) for _ in range(2)]
        xn = [view(D) for _ in range(2)]
        junk = view(D)
        crow = view(4 * P).rearrange("p (a c) -> p a c", c=P)
        ptb, ptc = view(SB * NPG).bitcast(I32), view(SB * NPG)
        at[0] = a_r
        onsa = view(KD * N).rearrange("p (k n) -> p k n", n=N)
        kT = view(4 * N).rearrange("p (b g n) -> p b g n", b=2, g=2)
        kcz = view(4 * PB).rearrange("p (g e c) -> p g e c", g=2, e=2)
        qbd = view(SB * 2 * S).rearrange("p (b g q) -> p b g q", b=SB, g=2)
        a_vcz = at[0]
        vcz = view(G * R * HD).rearrange("p (g r d) -> p g r d", g=G, r=R)
        a_d = at[0]
        nqT = view(KD * N).rearrange("p (k n) -> p k n", n=N)
        pr = [view(T) for _ in range(4)]
        pT = [view(T).rearrange("p (j t) -> p j t", t=P) for _ in range(4)]
        pcw = view(NH * PB).rearrange("p (h c) -> p h c", c=PB)
        pcm = view(NH * CB).rearrange("p (h c) -> p h c", c=CB)
        pcT = [view(T).rearrange("p (g t) -> p g t", t=P) for _ in range(2)]
        at[0] = a_d
        SELW = NPG * P + S
        SCW = SELW + WIN + S
        sc = [view(SCW), None]
        nr = NSLOT * KD * WB // (PGC * KV)
        ering = [wring[:, s * PGC * KV:(s + 1) * PGC * KV].rearrange("p (g c) -> p g c", c=KV)
                 for s in [(B_MG % NSLOT * (nr // NSLOT) + i) % nr for i in range(nr)]]
        ering += [view(PGC * KV).rearrange("p (g c) -> p g c", c=KV) for _ in range(NKR + NVR - len(ering))]
        kTs = [view(2 * PGC * P).rearrange("p (g n) -> p g n", g=2) for _ in range(2)]
        pTs = [view(PGC * P).rearrange("p (j q) -> p j q", q=P)]
        kring, vring = ering[0:NKR], ering[NKR:]
        sc[1] = view(SCW, a_kvt)
        osb = view(SB * HD).rearrange("p (b d) -> p b d", b=SB)
        kcs = view(2 * P).rearrange("p (g n) -> p g n", g=2)
        pTs.append(view(PGC * P).rearrange("p (j q) -> p j q", q=P))
        assert at[0] <= a_kvt + PT * 6 * KV
        at[0] = a_vcz
        psm, psg, pscT = view(P), view(P), [view(P) for _ in range(2)]
        pair, imp, imr, pen32 = view(NSB), view(NSB + 1), view(NSB + 1), view(NSB + 1)
        penq = [view(NSB + 1) for _ in range(2)]
        assert at[0] <= a_d
        a_x1 = a_kvt - SB * 2 * KV
        at[0] = a_x1
        x1 = view(TT * D).rearrange("p (i c) -> p i c", c=D)
        gqm, gqf = view(D), view(D)
        a_f = at[0]
        xr = [view(D) for _ in range(2)]
        hn = [view(D) for _ in range(2)]
        assert at[0] <= a_r
        at[0] = a_r + KD * N
        mgb = [view(N) for _ in range(2)]
        junk2 = view(D)
        at[0] = a_f
        gT = view(NF * N).rearrange("p (j n) -> p j n", n=N)
        EXS = 2 + T
        EXT = EXS + SB * (ST + 2)
        ext = [[view(EXT) for _ in range(2)] for _ in range(2)]
        CVW = EXT - 2
        cva = [[view(EXT) for _ in range(2)] for _ in range(2)]
        sge = [view(EXT) for _ in range(2)]
        cog = [view(2 * (2 + 2 * SB)) for _ in range(2)]
        NCO = 2 + 2 * SB
        cvx = view(2 * FF)
        cvi, cvo = cvx[0:2 * SB, :], cvx[32:32 + NCO, :]
        fo = view(TT * 512, a_ohg).rearrange("p (i c) -> p i c", c=512)
        junk3 = view(D)
        ftmp = view(512)
        ps = ctx.enter_context(nc.psum_tensor("ps", [P, 8, 512], F32))

        par_in = sem("par_in")
        pt_in = sem("pt_in")
        const = sem("const")
        dconst = sem("dconst")
        econst = sem("econst")
        actc = sem("actc")
        x_in = [sem("x_in0"), sem("x_in1")]
        rs_ok = sem("rs_ok")
        xn_ok = sem("xn_ok")
        xtr_ok = sem("xtr_ok")
        hT_ok = sem("hT_ok")
        w_in_s = [sem(f"w_in{i}") for i in range(NSLOT)]
        dnb_ok = sem("dnb_ok")
        proj = sem("proj")
        qg_ok = sem("qg_ok")
        cm_ok = sem("cm_ok")
        up_ok = sem("up_ok")
        ssum_ok = sem("ssum_ok")
        a_dn = sem("a_dn")
        v_dn = sem("v_dn")
        idx_ok = sem("idx_ok")
        cg_in = [sem(f"cg_in{i}") for i in range(3)]
        cg_used = sem("cg_used")
        ef_ok = sem("ef_ok")
        lf_ok = sem("lf_ok")
        d_ok = sem("d_ok")
        ex_ok = sem("ex_ok")
        eq_ok = sem("eq_ok")
        kq_ok = sem("kq_ok")
        vt_ok = sem("vt_ok")
        s0_in = [sem("s0_in0"), sem("s0_in1")]
        ktr_ok = sem("ktr_ok")
        ktok_ok = sem("ktok_ok")
        at_ok = sem("at_ok")
        att_ok = sem("att_ok")
        vm_ok = sem("vm_ok")
        u_ok = sem("u_ok")
        st_ok = sem("st_ok")
        o_ok = sem("o_ok")
        osq_ok = sem("osq_ok")
        oss_ok = sem("oss_ok")
        ors_ok = sem("ors_ok")
        ohg_ok = sem("ohg_ok")
        hgo_out = sem("hgo_out")
        kv_ok = sem("kv_ok")
        kvo_out = sem("kvo_out")
        kT_ok = sem("kT_ok")
        nq_ok = sem("nq_ok")
        qbd_ok = sem("qbd_ok")
        ge_ok = sem("ge_ok")
        gate_out = sem("gate_out")
        gq_in = sem("gq_in")
        csc_ok = sem("csc_ok")
        cms_ok = sem("cms_ok")
        cex_ok = sem("cex_ok")
        cpr_ok = sem("cpr_ok")
        cpt_ok = sem("cpt_ok")
        cpT_ok = sem("cpT_ok")
        sc_ok = sem("sc_ok")
        nm_ok = sem("nm_ok")
        p_ok = sem("p_ok")
        cf_ok = sem("cf_ok")
        pn_ok = [sem("pn_ok0"), sem("pn_ok1")]
        t_ok = sem("t_ok")
        pT_ok = sem("pT_ok")
        pv_ok = sem("pv_ok")
        on_ok = sem("on_ok")
        pg_k = [sem(f"pg_k{i}") for i in range(NKR)]
        pg_g = [sem(f"pg_g{i}") for i in range(NKR)]
        pg_v = [sem(f"pg_v{i}") for i in range(NVR)]
        ek_ok = sem("ek_ok")
        ekT_ok = sem("ekT_ok")
        es_ok = sem("es_ok")
        esc_ok = sem("esc_ok")
        enm_ok = sem("enm_ok")
        eex_ok = sem("eex_ok")
        ecf_ok = sem("ecf_ok")
        epn_ok = sem("epn_ok")
        et_ok = sem("et_ok")
        epT_ok = sem("epT_ok")
        epv_ok = sem("epv_ok")
        eo_ok = sem("eo_ok")
        c1_ok = sem("c1_ok")
        c2_ok = sem("c2_ok")
        c3_ok = sem("c3_ok")
        c4_ok = sem("c4_ok")
        c5_ok = sem("c5_ok")
        c6_ok = sem("c6_ok")
        c7_ok = sem("c7_ok")
        c8_ok = sem("c8_ok")
        c9_ok = sem("c9_ok")
        c10_ok = sem("c10_ok")
        pq_ok = sem("pq_ok")
        sw_ok = sem("sw_ok")
        ons_ok = sem("ons_ok")
        mge_ok = sem("mge_ok")
        u_hT = sem("u_hT")
        wo_ok = sem("wo_ok")
        x1_ok = sem("x1_ok")
        xr_in = [sem("xr_in0"), sem("xr_in1")]
        cvi_in = sem("cvi_in")
        cin_ok = sem("cin_ok")
        ext_ok = sem("ext_ok")
        cnv_ok = sem("cnv_ok")
        sg_ok = sem("sg_ok")
        g_ok = sem("g_ok")
        cog_ok = sem("cog_ok")
        cot_ok = sem("cot_ok")
        cvo_ok = sem("cvo_ok")
        dn_ok = sem("dn_ok")
        fo_ok = sem("fo_ok")
        y_ok = sem("y_ok")
        y_out = sem("y_out")
        win_out = sem("win_out")

        gate_d = nc.dram_tensor("gate_scratch", (S, NH * BR), F32, kind="Internal").ap()

        cache_rows = cache_c.rearrange("l n (q r) h g d -> (l n q) (r h g d)", r=4)
        pool_rows = cache_s.rearrange("l n r h g d -> (l n r h) (g d)")
        winr = win_kv.rearrange("l b w h g d -> (l b) w h (g d)")
        w_in3 = w_in.rearrange("l (k p) c -> p (l k) c", p=P)
        w_out3 = w_out.rearrange("l (k p) c -> p (l k) c", p=P)
        w_up3 = w_up.rearrange("l (k p) c -> p (l k) c", p=P)
        w_dn3 = w_down.rearrange("l (k p) c -> p (l k) c", p=P)
        xp2 = x_p.rearrange("b t c -> (b t) c")
        xs2 = x_s.rearrange("b t c -> (b t) c")

        def xrows(i):
            return xp2[i * P:(i + 1) * P, :] if i < PT else xs2

        def wcols(b):
            s = wslot[b % NSLOT]
            v = s.rearrange("p (k c) -> p k c", c=WB)
            if b < B_KV:
                o = [O_HQ, O_HF, O_HI, O_HG][b % 4] + P * (b // 4)
                return [(v[:, :, 0:P], w_in3[:, :, o:o + P])]
            if b < B_NQ:
                o = O_KV + WB * (b - B_KV)
                return [(v, w_in3[:, :, o:o + WB])]
            if b < B_NG:
                gp, rp = divmod(b - B_NQ, 2)
                o = O_NQ + 512 * gp + P * rp
                v4 = s.rearrange("p (k r e d) -> p k r e d", r=2, e=2, d=HD)
                return [(v4[:, :, r, e, :], w_in3[:, :, o + R * HD * e + r * HD:o + R * HD * e + (r + 1) * HD])
                        for r in range(2) for e in range(2)]
            if b < B_MG:
                return [(s[:, 0:KD * NH * BR].rearrange("p (k c) -> p k c", c=NH * BR),
                         w_in3[:, :, O_NG:O_NG + NH * BR])]
            if b < B_WO:
                o = O_MG + WB * (b - B_MG)
                return [(v, w_in3[:, :, o:o + WB])]
            if b < B_UP:
                k = 2 * (b - B_WO)
                return [(s.rearrange("p (k c) -> p k c", c=D), w_out3[:, k:k + 2, :])]
            if b < B_DN:
                j = b - B_UP
                return [(v[:, :, 0:P], w_up3[:, :, j * P:(j + 1) * P]),
                        (v[:, :, P:2 * P], w_up3[:, :, FF + j * P:FF + (j + 1) * P])]
            h, q = divmod(b - B_DN, len(DN_T))
            k, n = DN_T[q]
            return [(s[:, 0:n * 512].rearrange("p (k c) -> p k c", c=512),
                     w_dn3[:, k:k + n, h * 512:(h + 1) * 512])]

        B_ALL = B_DN + 2 * len(DN_T)
        landed, n_in = [], [0] * NSLOT
        for b in range(B_ALL):
            n_in[b % NSLOT] += 16 * len(wcols(b))
            landed.append(n_in[b % NSLOT])

        def pu(u):
            return ps[:, 2 * (u % 2):2 * (u % 2) + 2, 0:NHF]

        def halves(v):
            return v.rearrange("p (a n) -> p a n", a=2)

        def block_used(b):
            if b < B_KV:
                return proj, b + 1
            if b < B_NQ:
                return proj, U_KV + 3 * (b - B_KV) + 3
            if b < B_NG:
                return proj, U_NQ + 2 * (b - B_NQ) + 2
            if b < B_MG:
                return proj, U_NG + 1
            if b < B_WO:
                return proj, U_MG + 2 * (b - B_MG) + 2
            if b < B_UP:
                return wo_ok, TT
            if b < B_DN:
                return proj, U_UP + 2 * (b - B_UP) + 2
            h, q = divmod(b - B_DN, len(DN_T))
            return (dn_ok, TT * (h + 1)) if q == len(DN_T) - 1 else (dnb_ok, (len(DN_T) - 1) * h + q + 1)

        cbank = ps[:, 7, :]
        obank = ps[:, 6, :]

        block = ctx.enter_context(nc.Block())

        UNITS = [(i, h + e, br) for i in range(PT) for h in range(0, NH, 2) for br in range(2) for e in range(2)]
        NU = len(UNITS)
        TLAG, VLAG = 4, 7
        NP = 5
        PIECES = [[(2 * 512 * k, 1024)] for k in range(4)] + [[(NPG * P, S), (SELW, WIN + S)]]
        def lands(ring, pages, window):
            n = []
            for kq in range(SB * (NPC + 1)):
                n.append((n[kq - ring] if kq >= ring else 0) + 16 * (pages if kq % (NPC + 1) < NPC else window))
            return n

        kland, gland = lands(NKR, PGC - len(K_POOL), 1), lands(NKR, len(K_POOL), 0)
        vland = lands(NVR, PGC, 1)

        def v_used(kq):
            bb, cc = divmod(kq - NVR, NPC + 1)
            return NC * bb + cc + 1
        NCST = 30
        WSEQ = [("wo", 0)] + [x for i in range(1, TT) for x in (("wo", i), ("tr", i - 1))] + [("tr", TT - 1)]

        def head(h):
            gp, e, r = h // 8, (h // 4) % 2, h % 4
            return gp, e, gp * 4 + r

        @block.sync
        def _(sp):
            for k, a in enumerate((g_pm, g_pf)):
                sp.dma_start(prow[8 * k:8 * k + 8, :], a.rearrange("l (k p) -> (l k) p", p=P)).then_inc(par_in, 16)
            sp.dma_start(prow[16:32, :], lb_lg.rearrange("l (k p) -> (l k) p", p=P)).then_inc(par_in, 16)
            sp.dma_start(prow[32:33, :], hg_g).then_inc(par_in, 16)
            sp.dma_start(crow[0:2 * NF, 0:3, :], conv_w.rearrange("l w (c p) -> (l c) w p", p=P)).then_inc(par_in, 16)
            sp.dma_start(crow[0:2 * NF, 3, :], conv_b.rearrange("l (c p) -> (l c) p", p=P)).then_inc(par_in, 16)
            sp.dma_start(ptb[:, :], ptab.rearrange("(o b) j -> o (b j)", o=1).to_broadcast([P, SB * NPG])).then_inc(pt_in, 16)
            for i in range(TT):
                wait(sp, xn_ok, i - 1)
                sp.dma_start(xt[i % 2][0:TR[i], :], xrows(i)).then_inc(x_in[i % 2], 16)

            def weights(b):
                if b >= NSLOT:
                    sp.wait_ge(*block_used(b - NSLOT))
                for dst, src in wcols(b):
                    sp.dma_start(dst, src).then_inc(w_in_s[b % NSLOT], 16)

            for b in range(B_MG):
                weights(b)
            sp.wait_ge(ge_ok, 1)
            sp.dma_start(gate_d, gate[0:S, PT, :]).then_inc(gate_out, 16)
            sp.wait_ge(gate_out, 16)
            for h in range(NH):
                sp.dma_start(gateq[h * ST:(h + 1) * ST, :, :],
                             gate_d.rearrange("(b t) c -> t b c", t=ST)[:, :, h * BR:(h + 1) * BR]).then_inc(gq_in, 16)
            def e_load(kq, what, pages):
                b, c = divmod(kq, NPC + 1)
                ring, sems = ((kring, pg_k), (vring, pg_v))[what]
                slot, signal = ring[kq % len(ring)], sems[kq % len(ring)]
                if c == NPC:
                    sp.dma_start(slot, winr[b].rearrange("(j p) h c -> p j h c", p=P)[:, :, what, :]).then_inc(signal, 16)
                    return
                i = b * NPG + c * PGC + pages[0]
                regs = nc.values_load_multi_w_load_instructions(
                    sidx[0:1, i:i + len(pages)], engines=[sp.engine], min_val=0, max_val=2 * P * (cache_s.shape[1] - 1),
                    skip_runtime_bounds_check_because="page indices")[1]
                for j, v in zip(pages, regs):
                    sp.dma_start(slot[:, j, :], pool_rows[bass.ds(v, 2 * P), :].rearrange("(r h) c -> r h c", h=2)[:, what, :])\
                      .then_inc(signal, 16)

            K_SP = [j for j in range(PGC) if j not in K_POOL]
            sp.wait_ge(idx_ok, 1)
            sp.wait_ge(proj, U_NG + 1)
            for kq in range(KAHEAD):
                e_load(kq, 0, K_SP)
            sp.wait_ge(pv_ok, NU)
            sp.wait_ge(qbd_ok, 1)
            for s in range(NC * SB + LAG):
                b, c = divmod(s + KAHEAD, NC)
                if b < SB and c <= NPC:
                    kq = b * (NPC + 1) + c
                    if kq >= KAHEAD:
                        wait(sp, ek_ok, kq - NKR + 1)
                        e_load(kq, 0, K_SP)
                b, c = divmod(s + VAHEAD - LAG, NC)
                if 0 <= b < SB and c <= NPC:
                    kq = b * (NPC + 1) + c
                    if kq >= NVR:
                        sp.wait_ge(epv_ok, v_used(kq))
                    e_load(kq, 1, list(range(PGC)))
            sp.wait_ge(ek_ok, SB * (NPC + 1))
            for b in range(B_MG, B_MG + NKR // 2):
                weights(b)
            sp.wait_ge(epv_ok, NC * SB)
            sp.wait_ge(eo_ok, SB)
            sp.wait_ge(ons_ok, 1)
            sp.dma_start(gqm, g_qm.to_broadcast([P, D])).then_inc(par_in, 16)
            sp.dma_start(gqf, g_qf.to_broadcast([P, D])).then_inc(par_in, 16)
            sp.dma_start(cvi, st_cv.rearrange("l b w c -> (l b w) c")).then_inc(cvi_in, 16)
            for b in range(B_MG + NKR // 2, B_UP):
                weights(b)
            for i in range(TT):
                wait(sp, x1_ok, i - 1)
                sp.dma_start(xr[i % 2][0:TR[i], :], xrows(i)).then_inc(xr_in[i % 2], 16)
            for b in range(B_UP, B_ALL):
                weights(b)
            sp.wait_ge(cvo_ok, NF)
            sp.dma_start(cv_p.rearrange("l b w c -> (l b w) c"), cvo[0:2, :]).then_inc(y_out, 16)
            sp.dma_start(cv_s.rearrange("l b w c -> (l b w) c"), cvo[2:NCO, :]).then_inc(y_out, 16)
            for i in range(TT):
                sp.wait_ge(y_ok, i + 1)
                dst = y_p.rearrange("b t c -> (b t) c")[i * P:(i + 1) * P, :] if i < PT else y_s.rearrange("b t c -> (b t) c")
                sp.dma_start(dst, x1[0:TR[i], i, :]).then_inc(y_out, 16)
            sp.wait_ge(y_out, 16 * (TT + 2))
            sp.wait_ge(kvo_out, 16 * (5 + SB))
            sp.wait_ge(hgo_out, 32 * HH)
            sp.wait_ge(win_out, 16 * SB)

        @block.gpsimd
        def _(pool):
            g = nc.gpsimd
            done = [0]

            def c(ins):
                ins.then_inc(const, 1)
                done[0] += 1

            for v, x in ((ident, 0.0), (ones, 1.0), (penf, 0.0), (hmask, 1.0), (hmask_s, 1.0), (scanm, 1.0),
                         (cmask, 1.0), (cmask_s, 1.0), (cm01, 1.0), (c16, 0.0), (epsc, EPS), (pnew, NEG), (zerob, 0.0)):
                c(g.memset(v[:], x))
            c(g.iota(q8i[:, :], [[0, 1]], base=0, channel_multiplier=8))
            c(g.iota(q4i[:, :], [[0, 1]], base=0, channel_multiplier=2))
            pool.wait_ge(const, done[0])

            def sel(v, pattern, base, mult, fill, op=ALU.is_ge):
                c(g.affine_select(out=v, in_=v, pattern=pattern, compare_op=op, fill=fill, base=base,
                                  channel_multiplier=mult))

            sel(ident[:, :], [[-1, P]], 0, 1, 1.0, ALU.not_equal)
            sel(penf[:, :], [[-1, P]], 0, 1, NEG)
            sel(hmask[:, :], [[1, P]], 0, -1, 0.0)
            sel(hmask_s[:, :], [[1, S]], 0, -1, 0.0)
            c(g.memset(scanm[:, 0:T].rearrange("p (c t) -> p c t", t=CH)[:, :, 0:1], 0.0))
            c(g.memset(scanm[:, T:N].rearrange("p (c t) -> p c t", t=ST)[:, :, 0:1], 0.0))
            sel(cmask[:, :], [[-CH, CPT]], 0, 1, 0.0)
            sel(cmask_s[:, :], [[-ST, SB]], 0, 1, 0.0)
            sel(cm01[:, :, :], [[P, PT], [-CB, PB]], 1 - CB, 1, 0.0)
            sel(c16[:, 0, :], [[-1, ST]], 0, 1, NEG)
            sel(c16[:, 1, :], [[1, ST]], -1, -1, NEG)
            pool.wait_ge(const, done[0])
            sel(hmask[:, :].rearrange("p (c t) -> p c t", t=CH), [[-CH, CPT], [0, CH]], 0, 1, 0.0)
            sel(hmask_s[:, :].rearrange("p (c t) -> p c t", t=ST), [[-ST, SB], [0, ST]], 0, 1, 0.0)
            sel(cmask[:, :], [[CH, CPT]], CH - 1, -1, 0.0)
            sel(cmask_s[:, :], [[ST, SB]], ST - 1, -1, 0.0)
            assert done[0] == NCST, done[0]

            pool.wait_ge(idx_ok, 1)
            gathers = [0]

            def gather(n):
                for _ in range(n):
                    k = gathers[0]
                    if k == SB * 8:
                        return
                    wait(pool, cg_used, k - 2)
                    b, q = divmod(k, 8)
                    pool.indirect_dma_start(cring[k % 3], None, cache_rows,
                                            bass.IndirectOffsetOnAxis(pidx[:, b, q:q + 1], 0)).then_inc(cg_in[k % 3], 16)
                    gathers[0] += 1

            gather(3)
            for h in range(HH + 1):
                if h < HH:
                    wait(pool, ohg_ok, h - 1)
                    pool.dma_start(s0s[h % 2], st_hg[0, :, h, :, :].rearrange("b k v -> k b v")).then_inc(s0_in[h % 2], 16)
                if h > 0:
                    o = h - 1
                    vo = vt[o % 2]
                    pool.wait_ge(vt_ok, o + 1)
                    for i in range(PT):
                        if o:
                            pool.wait_ge(u_ok, 6 * (o - 1) + i + 1)
                        g.tensor_tensor(vm[i], vo[:, i, :].unsqueeze(1).to_broadcast([P, CPT, P]),
                                        cmask[:, :].unsqueeze(2).to_broadcast([P, CPT, P]), ALU.mult).then_inc(vm_ok, 1)
                    wait(pool, u_ok, 6 * o)
                    g.tensor_tensor(vms[0:S], vo[0:S, PT, :].unsqueeze(1).to_broadcast([S, SB, P]),
                                    cmask_s[:, :].unsqueeze(2).to_broadcast([S, SB, P]), ALU.mult).then_inc(vm_ok, 1)
                    if h < HH:
                        gather(4)
                    pool.wait_ge(st_ok, 5 * h)
                    pool.dma_start(hgo_p[0, 0, o, :, :], st[:, NCH, :]).then_inc(hgo_out, 16)
                    pool.dma_start(hgo_s[0, :, o, :, :].rearrange("b k v -> k b v"), s1s).then_inc(hgo_out, 16)
                if h < HH:
                    gather(8 - 4 * (h > 0))
            for b in range(SB):
                pool.dma_start(win_s[0, b, 0:WIN - ST].rearrange("w h g d -> w (h g d)"),
                               win_kv[0, b, ST:WIN].rearrange("w h g d -> w (h g d)")).then_inc(win_out, 16)
            def e_gather(kq):
                b, c = divmod(kq, NPC + 1)
                for j in K_POOL:
                    i = b * NPG + c * PGC + j
                    pool.indirect_dma_start(kring[kq % NKR][:, j, :], None, pool_rows,
                                            bass.IndirectOffsetOnAxis(sidx[:, i:i + 1], 0)).then_inc(pg_g[kq % NKR], 16)

            pool.wait_ge(proj, U_NG + 1)
            for kq in range(KAHEAD):
                e_gather(kq)
            for n, (i, h, br) in enumerate(UNITS):
                if n % 2:
                    continue
                pool.wait_ge(cf_ok, n + 1)
                v = pr[n % 4][:, 0:(i + 1) * P]
                g.tensor_scalar(v, v, ssm[:, n % 4:n % 4 + 1], gate[:, i, BR * h + 1 + br:BR * h + 2 + br], ALU.mult, ALU.mult)\
                    .then_inc(pn_ok[0], 1)
            pool.wait_ge(pv_ok, NU)
            pool.wait_ge(qbd_ok, 1)
            for s in range(NC * SB + LAG):
                b, c = divmod(s + KAHEAD, NC)
                if b < SB and c < NPC:
                    kq = b * (NPC + 1) + c
                    if kq >= KAHEAD:
                        wait(pool, ek_ok, kq - NKR + 1)
                        e_gather(kq)
            for j in range(NF):
                pool.wait_ge(ext_ok, j + 1)
                wait(pool, cot_ok, j - 1)
                for a in range(2):
                    e, o = ext[j % 2][a], cog[j % 2][:, a * NCO:(a + 1) * NCO]
                    g.tensor_copy(o[:, 0:2], e[:, T:T + 2])
                    ins = g.tensor_copy(o[:, 2:NCO].rearrange("p (b w) -> p b w", w=2),
                                        e[:, EXS:EXT].rearrange("p (b t) -> p b t", t=ST + 2)[:, :, ST:ST + 2])
                ins.then_inc(cog_ok, 1)

        @block.scalar
        def _(act):
            a = nc.scalar
            n_a = [0]

            def link(ins):
                ins.then_inc(a_dn, 1)
                n_a[0] += 1
                act.wait_ge(a_dn, n_a[0])

            a.preload_act_table_set("natural_log_exp_and_others")
            for q in range(4):
                act.dma_start(pti[q:P:4, :], ptab.rearrange("b j -> j b"), allow_slow_non_contiguous=True).then_inc(pt_in, 16)
            act.wait_ge(dconst, 1)
            a.activation(lbt[:, 1:3, :], lbt[:, 1:3, :], ACT.Exp).then_inc(actc, 1)

            def factor(rows, ss, rs):
                link(a.activation(rs, ss, ACT.Ln, scale=1.0 / D, bias=epsc[0:rows]))
                a.activation(rs, rs, ACT.Exp, scale=-0.5).then_inc(rs_ok, 1)

            act.wait_ge(const, NCST)
            for i in range(TT):
                n = TR[i]
                act.wait_ge(x_in[i % 2], 16 * (i // 2 + 1))
                link(a.activation(junk[0:n, :], xt[i % 2][0:n, :], ACT.Square, accum_out=st_ss[0:n, 0, i:i + 1]))
                factor(n, st_ss[0:n, 0, i:i + 1], st_rs[0:n, 0, i:i + 1])

            def unit(u):
                act.wait_ge(proj, u + 1)

            def h_sig(h, k, buf):
                u = 4 * h + k
                unit(u)
                if k == 0:
                    wait(act, ohg_ok, h - 1)
                a.activation(halves(buf[h % 2]), pu(u), ACT.Sigmoid).then_inc(eq_ok, 1)

            def h_ef(h):
                u = 4 * h + 1
                unit(u)
                a.activation(halves(rb[h % 2]), pu(u), ACT.Sigmoid)
                a.activation(halves(eb[h % 2]), pu(u), ACT.Sigmoid, scale=-1.0).then_inc(ef_ok, 1)

            def h_lf(h):
                act.wait_ge(ef_ok, h + 1)
                a.activation(fb[h % 2], rb[h % 2], ACT.Ln, scale=oml[:, h:h + 1], bias=lb[:, h:h + 1]).then_inc(lf_ok, 1)

            def h_v(h):
                u = 4 * h + 2
                unit(u)
                b0 = 2 * (u % 2)
                a.activation(vt[h % 2][:, 0:PT, :], ps[:, b0, :].rearrange("p (i c) -> p i c", c=P), ACT.Copy)
                a.activation(vt[h % 2][0:S, PT, :], ps[0:S, b0 + 1, 0:P], ACT.Copy).then_inc(vt_ok, 1)

            def h_exps(h):
                act.wait_ge(d_ok, h + 1)
                x, f, r = xb[h % 2], fb[h % 2], rb[h % 2]
                link(a.activation(x, f, ACT.Exp))
                a.activation(f, f, ACT.Exp, scale=-1.0)
                a.activation(r, r, ACT.Exp).then_inc(ex_ok, 1)

            def h_ktok(h):
                act.wait_ge(ktr_ok, h + 1)
                a.activation(ktok, ps[:, 4, :].rearrange("p (i t) -> p i t", t=P), ACT.Copy)
                act.wait_ge(at_ok, h + 1)
                a.activation(ktok_s[0:S, :], ps[0:S, 6, 0:P], ACT.Copy).then_inc(ktok_ok, 1)

            def h_osq(h):
                act.wait_ge(o_ok, h + 1)
                a.activation(fb[h % 2][:, 0:T], ps[:, 7, :], ACT.Square)
                a.activation(fb[h % 2][:, T:N], ps[:, 6, 192:192 + S], ACT.Square).then_inc(osq_ok, 1)

            def h_rs(h):
                act.wait_ge(oss_ok, h + 1)
                act.wait_ge(kq_ok, h + 1)
                q = qb[h % 2]
                link(a.activation(halves(q), ps[:, 4:6, 0:NHF], ACT.Ln, scale=1.0 / P, bias=epsc[:, :]))
                a.activation(q, q, ACT.Exp, scale=-0.5).then_inc(ors_ok, 1)

            def kv_rows(u):
                b, k = divmod(u - U_KV, 3)
                unit(u)
                c0 = b * KV
                if k < 2:
                    ins = a.activation(kvt[:, 2 * k:2 * k + 2, c0:c0 + KV], ps[:, 2 * (u % 2):2 * (u % 2) + 2, 0:KV], ACT.Copy)
                else:
                    ins = a.activation(kvt[0:S, PT, c0:c0 + KV], ps[0:S, 2 * (u % 2), 0:KV], ACT.Copy)
                ins.then_inc(kv_ok, 1)

            for h in range(HH + 1):
                new, old = h < HH, h > 0
                if old:
                    h_sig(h - 1, 3, gb)
                if new:
                    h_sig(h, 0, qb)
                else:
                    act.wait_ge(cg_used, SB * 8)
                    kv_rows(U_KV)
                if old:
                    h_ktok(h - 1)
                if new:
                    h_ef(h)
                    h_lf(h)
                    h_v(h)
                    h_exps(h)
                else:
                    kv_rows(U_KV + 1)
                    kv_rows(U_KV + 2)
                if old:
                    h_osq(h - 1)
                if not new:
                    kv_rows(U_KV + 3)
                if old:
                    h_rs(h - 1)
            for u in range(U_KV + 4, U_KT):
                kv_rows(u)
            act.wait_ge(kv_ok, U_KT - U_KV)
            for k, (op, os) in enumerate(((cmp_p, cmp_s), (sel_p, sel_s), (win_p, None))):
                c0 = 2 * KV * k
                act.dma_start(op[0, 0].rearrange("(i p) h g d -> p i (h g d)", p=P), kvt[:, 0:PT, c0:c0 + 2 * KV]).then_inc(kvo_out, 16)
                if os is not None:
                    act.dma_start(os[0].rearrange("b t h g d -> (b t) (h g d)"), kvt[0:S, PT, c0:c0 + 2 * KV]).then_inc(kvo_out, 16)
            for b in range(SB):
                act.dma_start(win_s[0, b, WIN - ST:WIN].rearrange("w h g d -> w (h g d)"),
                              kvt[b * ST:(b + 1) * ST, PT, C_KW:C_KW + 2 * KV]).then_inc(kvo_out, 16)
            act.wait_ge(ohg_ok, HH)
            act.wait_ge(hgo_out, 32 * HH)
            for u in range(U_KT, U_CM):
                br, gp = divmod(u - U_KT, 2)
                unit(u)
                a.activation(kT[:, br, gp, 0:T], ps[:, 2 * (u % 2), :], ACT.Copy)
                a.activation(kT[:, br, gp, T:N], ps[:, 2 * (u % 2) + 1, 0:S], ACT.Copy).then_inc(kT_ok, 1)
            for u in range(U_NQ, U_NG):
                unit(u)
                a.activation(halves(nqT[:, u - U_NQ, :]), pu(u), ACT.Copy, scale=SCALE).then_inc(nq_ok, 1)
            unit(U_NG)
            for i in range(TT):
                ins = a.activation(gate[0:TR[i], i, :], ps[0:TR[i], 2 * (U_NG % 2), i * NH * BR:(i + 1) * NH * BR], ACT.Sigmoid)
            ins.then_inc(ge_ok, 1)

            def c_exp(i):
                act.wait_ge(cms_ok, i + 1)
                a.activation(pcw, pcw, ACT.Exp).then_inc(cex_ok, 1)

            def c_evac(i):
                act.wait_ge(cpt_ok, i + 1)
                if i >= 2:
                    act.wait_ge(pv_ok, (i - 1) * NU // PT)
                a.activation(pcT[i % 2], ps[:, 7, :].rearrange("p (g t) -> p g t", t=P), ACT.Copy).then_inc(cpT_ok, 1)

            c_exp(0)
            for n in range(NU + TLAG):
                if n < NU:
                    i, h, br = UNITS[n]
                    w = (i + 1) * P
                    act.wait_ge(nm_ok, n + 1)
                    wait(act, t_ok, n - 3)
                    a.activation(pr[n % 4][:, 0:w], ps[:, n % 3, 0:w], ACT.Exp, bias=nmx[:, n % 4:n % 4 + 1],
                                 accum_out=ssm[:, n % 4:n % 4 + 1]).then_inc(p_ok, 1)
                m = n - TLAG
                if m >= 0:
                    i, h, br = UNITS[m]
                    if m % (NU // PT) == 0:
                        c_evac(i)
                    act.wait_ge(t_ok, m + 1)
                    wait(act, pv_ok, m - 3)
                    a.activation(pT[m % 4][:, 0:i + 1, :], ps[:, 3 + m % 2, 0:(i + 1) * P].rearrange("p (j t) -> p j t", t=P),
                                 ACT.Copy).then_inc(pT_ok, 1)
                if n % (NU // PT) == NU // PT - 4 and n < NU - 4:
                    c_exp(n // (NU // PT) + 1)

            def e_c2(b):
                act.wait_ge(c1_ok, b + 1)
                a.activation(kcs, cbank[:, 0:2 * P].rearrange("p (g n) -> p g n", g=2), ACT.Copy, scale=1.0 / CB).then_inc(c2_ok, 1)

            def e_c5(b):
                act.wait_ge(c4_ok, b + 1)
                a.activation(psm, cbank[:, 256:384], ACT.Exp, bias=cst2[:, 0:1], accum_out=cst2[:, 1:2]).then_inc(c5_ok, 1)

            def e_c7(b):
                act.wait_ge(c7_ok, b + 1)
                if b >= 2:
                    act.wait_ge(epv_ok, NC * (b - 2) + 1)
                a.activation(pscT[b % 2], cbank[:, 384:512], ACT.Copy).then_inc(c10_ok, 1)

            def e_exp(b, ks):
                for k in ks:
                    if k == 0:
                        act.wait_ge(enm_ok, b + 1)
                    for q, (o, n) in enumerate(PIECES[k]):
                        v = sc[b % 2][:, o:o + n]
                        ins = a.activation(v, v, ACT.Exp, bias=est[:, b % 2, 12 + (q > 0):13 + (q > 0)],
                                           accum_out=est[:, b % 2, 14 + k + (q > 0):15 + k + (q > 0)])
                if 4 in ks:
                    ins.then_inc(eex_ok, 1)

            act.wait_ge(pv_ok, NU)
            act.wait_ge(kvo_out, 16 * (5 + SB))
            act.wait_ge(qbd_ok, 1)
            e_c2(0)
            e_c5(0)
            e_c7(0)
            for s in range(NC * SB + LAG):
                b, c = divmod(s, NC)
                if b < SB and c <= NPC:
                    kq = b * (NPC + 1) + c
                    act.wait_ge(ek_ok, kq + 1)
                    if kq >= 2:
                        bb, cc = divmod(kq - 2, NPC + 1)
                        act.wait_ge(es_ok, NC * bb + cc + 1)
                    a.activation(kTs[kq % 2], ps[:, 0:2, :], ACT.Copy).then_inc(ekT_ok, 1)
                m = s - LAG
                if m >= 0:
                    bb, cc = divmod(m, NC)
                    act.wait_ge(et_ok, m + 1)
                    wait(act, epv_ok, m - 1)
                    src = ps[:, 4 + m % 2, :].rearrange("p (j q) -> p j q", q=P)
                    if cc < NC - 1:
                        ins = a.activation(pTs[m % 2], src, ACT.Copy)
                    else:
                        ins = a.activation(pTs[m % 2][0:S, 0:2, :], src[0:S, 0:2, :], ACT.Copy)
                    ins.then_inc(epT_ok, 1)
                if b + 1 < SB:
                    if c == 3:
                        e_c2(b + 1)
                    if c == 5:
                        e_c5(b + 1)
                    if c == 7:
                        e_c7(b + 1)
                if c < 4 and 0 < b <= SB:
                    e_exp(b - 1, [c] if c < 3 else [3, 4])

            for u in range(U_MG, U_UP):
                unit(u)
                wait(act, u_hT, u - U_MG - 1)
                a.activation(halves(mgb[u % 2]), pu(u), ACT.Sigmoid).then_inc(mge_ok, 1)

            for i in range(TT):
                n = TR[i]
                w = WSEQ.index(("wo", i)) % 4
                act.wait_ge(wo_ok, i + 1)
                link(a.activation(junk2[0:n].rearrange("p (a c) -> p a c", a=2), ps[0:n, 2 * w:2 * w + 2, :], ACT.Square,
                                  accum_out=st_ss[0:n, 1, i:i + 1]))
                factor(n, st_ss[0:n, 1, i:i + 1], st_rs[0:n, 1, i:i + 1])
                act.wait_ge(x1_ok, i + 1)
                link(a.activation(junk2[0:n], x1[0:n, i, :], ACT.Square, accum_out=st_ss[0:n, 2, i:i + 1]))
                factor(n, st_ss[0:n, 2, i:i + 1], st_rs[0:n, 2, i:i + 1])

            act.wait_ge(hT_ok, 2 * TT)
            for x in range(2):
                for y in range(2):
                    a.activation(ext[x][y][:, 0:2], ones[:, 0:2], ACT.Copy, scale=0.0)

            def f_out(j):
                act.wait_ge(cot_ok, j + 1)
                a.activation(cvo.rearrange("p (a c) -> p a c", a=2)[:, :, j * P:(j + 1) * P],
                             ps[0:NCO, 6 + j % 2, 0:2 * P].rearrange("p (a c) -> p a c", a=2), ACT.Copy).then_inc(cvo_ok, 1)

            for j in range(NF):
                act.wait_ge(cin_ok, j + 1)
                wait(act, g_ok, j - 1)
                wait(act, cog_ok, j - 1)
                for x in range(2):
                    u = U_UP + 2 * j + x
                    unit(u)
                    e = ext[j % 2][x]
                    es = e[:, EXS:EXT].rearrange("p (b t) -> p b t", t=ST + 2)
                    a.activation(e[:, 2:2 + NHF], ps[:, 2 * (u % 2), 0:NHF], ACT.Copy)
                    a.activation(e[:, 2 + NHF:2 + T], ps[:, 2 * (u % 2) + 1, 0:T - NHF], ACT.Copy)
                    a.activation(es[:, :, 2:2 + ST], ps[:, 2 * (u % 2) + 1, T - NHF:NHF].rearrange("p (b t) -> p b t", t=ST), ACT.Copy)\
                        .then_inc(up_ok, 1)
                    ins = a.activation(es[:, :, 0:2], ps[:, 4 + j % 2, x * 16:(x + 1) * 16].rearrange("p (b w) -> p b w", w=2), ACT.Copy)
                ins.then_inc(ext_ok, 1)
                if j >= 1:
                    f_out(j - 1)
                act.wait_ge(cnv_ok, j + 1)
                a.activation(sge[j % 2][:, 0:CVW], cva[j % 2][0][:, 0:CVW], ACT.Sigmoid).then_inc(sg_ok, 1)
            f_out(NF - 1)
            for h in range(2):
                for i in range(TT):
                    n = TR[i]
                    bank = (TT * h + i) % 8
                    act.wait_ge(dn_ok, TT * h + i + 1)
                    wait(act, fo_ok, TT * h + i)
                    if h == 0:
                        a.activation(junk3[0:n, 0:512], ps[0:n, bank, :], ACT.Square, accum_out=st_ss[0:n, 0, i:i + 1])
                        a.activation(fo[0:n, i, :], ps[0:n, bank, :], ACT.Copy).then_inc(fo_ok, 1)
                    else:
                        a.activation(junk3[0:n, 0:512], ps[0:n, bank, :], ACT.Square, accum_out=st_ss[0:n, 3, i:i + 1]).then_inc(fo_ok, 1)
                        act.wait_ge(ssum_ok, i + 1)
                        factor(n, st_ss[0:n, 3, i:i + 1], st_rs[0:n, 3, i:i + 1])

        @block.vector
        def _(dve):
            v = nc.vector
            n_v = [0]

            def mark(ins):
                ins.then_inc(v_dn, 1)
                n_v[0] += 1

            def link(ins):
                mark(ins)
                dve.wait_ge(v_dn, n_v[0])

            dve.wait_ge(econst, 1)
            v.tensor_copy(par[:, :], ps[:, 4, 0:33])
            link(v.tensor_copy(cpar[:, :, :], ps[:, 5, 0:8 * NF].rearrange("p (a c) -> p a c", a=4)))
            l0, l1 = par[:, 16:24], par[:, 24:32]
            link(v.tensor_tensor(lbt[:, 0, :], l0, l1, ALU.max))
            v.tensor_tensor(lbt[:, 1, :], l0, lbt[:, 0, :], ALU.subtract)
            v.tensor_tensor(lbt[:, 2, :], l1, lbt[:, 0, :], ALU.subtract).then_inc(dconst, 1)
            v.tensor_copy(identb[:, :], ident[:, :])
            v.tensor_copy(penb[:, :], penf[:, :])
            v.memset(avm[:], 0.0)
            link(v.tensor_scalar(amean[:, :], cmask[:, :], 1.0 / CB, None, ALU.mult))
            for i in range(PT):
                v.tensor_copy(avm[:, i, :, i * CPT:(i + 1) * CPT], amean[:, :].unsqueeze(1).to_broadcast([P, R, CPT]))
            v.tensor_scalar(cpen[:, :, :], cm01[:, :, :], -NEG, NEG, ALU.mult, ALU.add)
            v.tensor_reduce(rmat[:, :], ident[:, :].rearrange("p (g r t) -> p g t r", g=G, r=R), AX.X, ALU.add)
            iv = ident[0:G * ST, 0:G * ST].rearrange("p (g t) -> p g t", g=G)
            for r in range(R):
                v.tensor_copy(rmatT[:, :].rearrange("p (g r t) -> p g r t", g=G, r=R)[:, :, r, :], iv)
            link(v.tensor_copy(rep8[:, :].rearrange("p (h t) -> p h t", t=ST), ident[0:ST, 0:ST].unsqueeze(1).to_broadcast([ST, NH, ST])))
            dve.wait_ge(pt_in, 80)
            v.tensor_scalar(q8i[:, :], q8i[:, :], 24, None, ALU.bitwise_and)
            link(v.tensor_copy(ptf[:, :], pti[:, :]))
            link(v.tensor_copy(q8f[:, :], q8i[:, :]))
            link(v.tensor_scalar(ptf[:, :], ptf[:, :], 32.0, q8f[:, 0:1], ALU.mult, ALU.add))
            link(v.tensor_copy(q4f[:, :], q4i[:, :]))
            link(v.tensor_copy(ptc, ptb))
            v.tensor_scalar(sidx[:, :], ptc, 2.0 * P, q4f[:, 0:1], ALU.mult, ALU.add)
            for q in range(8):
                ins = v.tensor_scalar(pidx[:, :, q], ptf[:, :], float(q), None, ALU.add)
            ins.then_inc(idx_ok, 1)
            dve.wait_ge(actc, 1)
            link(v.tensor_tensor(lbt[:, 0, :], lbt[:, 1, :], lbt[:, 2, :], ALU.add))
            link(v.reciprocal(lbt[:, 0, :], lbt[:, 0, :]))
            link(v.tensor_tensor(lb[:, :], lbt[:, 1, :], lbt[:, 0, :], ALU.mult))
            link(v.tensor_scalar(oml[:, :], lb[:, :], -1.0, 1.0, ALU.mult, ALU.add))
            dve.wait_ge(econst, 2)
            link(v.tensor_copy(pen8[:, :, :], ps[:, 6, 0:2 * ST].rearrange("p (a t) -> p a t", a=2)))
            for b in range(SB):
                ins = v.tensor_copy(pnew[:, b, b * ST:(b + 1) * ST], pen8[:, 0, :])
            mark(ins)

            def norm_tile(i):
                n = TR[i]
                dve.wait_ge(rs_ok, i + 1)
                wait(dve, xtr_ok, i - 1)
                v.tensor_scalar(xn[i % 2][0:n, :], xt[i % 2][0:n, :], st_rs[0:n, 0, i:i + 1], None, ALU.mult).then_inc(xn_ok, 1)

            def tile_out(i, pairn, gcol, count):
                n = TR[i]
                dve.wait_ge(xtr_ok, count)
                src = ps[:, 2 * pairn:2 * pairn + 2, :].rearrange("p a (k n) -> p (a k) n", n=P)[:, :, 0:n]
                v.tensor_tensor(hT[:, :, i * P:i * P + n], src, par[:, gcol:gcol + 8].unsqueeze(2).to_broadcast([P, KD, n]),
                                ALU.mult).then_inc(hT_ok, 1)

            norm_tile(0)
            for i in range(TT):
                if i + 1 < TT:
                    norm_tile(i + 1)
                tile_out(i, i % 2, 0, i + 1)
            mark(v.memset(att, 0.0))
            mark(v.memset(att_s, 0.0))

            sums = [0]

            def rowsum(n):
                for _ in range(n):
                    k = sums[0]
                    if k == SB * 8:
                        return
                    b, q = divmod(k, 8)
                    dve.wait_ge(cg_in[k % 3], 16 * (k // 3 + 1))
                    out = cmt[:, b, :] if q == 0 else cpart
                    ins = v.tensor_reduce(out, cring[k % 3].rearrange("p (r c) -> p c r", r=4), AX.X, ALU.add)
                    ins.then_inc(cg_used, 1)
                    dve.wait_ge(cg_used, k + 1)
                    if q:
                        link(v.tensor_tensor(cmt[:, b, :], cmt[:, b, :], cpart, ALU.add))
                    sums[0] += 1

            def prep2(h):
                r, f = rb[h % 2], fb[h % 2]
                dve.wait_ge(lf_ok, h + 1)
                link(v.tensor_tensor_scan(r, scanm[:, :], f, 0.0, ALU.mult, ALU.add))
                for (o, m, c, t) in ((0, T, NCH, CH), (T, S, SB, ST)):
                    rv = r[:, o:o + m].rearrange("p (c t) -> p c t", t=t)
                    ins = v.tensor_tensor(f[:, o:o + m].rearrange("p (c t) -> p c t", t=t), rv,
                                          rv[:, :, t - 1:t].to_broadcast([P, c, t]), ALU.subtract)
                ins.then_inc(d_ok, 1)

            def silu(h, k, buf, count):
                u = 4 * h + k
                b = buf[h % 2]
                dve.wait_ge(eq_ok, count)
                v.tensor_tensor(halves(b), pu(u), halves(b), ALU.mult).then_inc(qg_ok, 1)

            def kq(h):
                q, e, r, f, x = qb[h % 2], eb[h % 2], rb[h % 2], fb[h % 2], xb[h % 2]
                dve.wait_ge(ex_ok, h + 1)
                dve.wait_ge(qg_ok, 2 * h + 1)
                for (o, m, t, k, n) in ((0, T, CH, 0, NCH), (T, S, ST, NCH, SB)):
                    mark(v.tensor_copy(dec[h % 2][:, k:k + n], r[:, o:o + m].rearrange("p (c t) -> p c t", t=t)[:, :, t - 1]))
                dve.wait_ge(v_dn, n_v[0])
                v.scalar_tensor_tensor(e, e, oml[:, h:h + 1], f, ALU.mult, ALU.mult)
                v.tensor_tensor(x, x, q, ALU.mult)
                v.tensor_tensor(r, r, q, ALU.mult).then_inc(kq_ok, 1)

            def masked(h):
                dve.wait_ge(at_ok, h + 1)
                v.copy_predicated(att, hmask[:, :].bitcast(U32).unsqueeze(1).to_broadcast([P, PT, P]),
                                  ps[:, 5, :].rearrange("p (i t) -> p i t", t=P))
                dve.wait_ge(ktok_ok, h + 1)
                v.copy_predicated(att_s[0:S, :], hmask_s[:, :].bitcast(U32), ps[0:S, 6, 128:128 + S]).then_inc(att_ok, 1)

            def states(h):
                d = dec[h % 2]
                wait(dve, hgo_out, 32 * h)
                for i in range(PT):
                    dve.wait_ge(u_ok, 6 * h + i + 1)
                    for c in range(CPT):
                        k = i * CPT + c
                        up = ps[:, 4 + i % 2, c * P:(c + 1) * P]
                        if k == 0:
                            ins = v.tensor_copy(st[:, 1, :], up)
                        else:
                            ins = v.scalar_tensor_tensor(st[:, k + 1, :], st[:, k, :], d[:, k:k + 1], up, ALU.mult, ALU.add)
                        if c < CPT - 1:
                            link(ins)
                    ins.then_inc(st_ok, 1)
                    dve.wait_ge(st_ok, 5 * h + i + 1)
                dve.wait_ge(s0_in[h % 2], 16 * (h // 2 + 1))
                for b in range(SB):
                    if b % 4 == 0:
                        dve.wait_ge(u_ok, 6 * h + 5 + b // 4)
                    ins = v.scalar_tensor_tensor(s1s[:, b, :], s0s[h % 2][:, b, :], d[:, NCH + b:NCH + b + 1],
                                                 ps[:, 4 + b // 4, (b % 4) * P:(b % 4 + 1) * P], ALU.mult, ALU.add)
                ins.then_inc(st_ok, 1)

            def head_out(h):
                q = qb[h % 2]
                dve.wait_ge(ors_ok, h + 1)
                dve.wait_ge(qg_ok, 2 * h + 2)
                v.scalar_tensor_tensor(q[:, 0:T], ps[:, 7, :], par[:, 32:33], q[:, 0:T], ALU.mult, ALU.mult)
                link(v.scalar_tensor_tensor(q[:, T:N], ps[:, 6, 192:192 + S], par[:, 32:33], q[:, T:N], ALU.mult, ALU.mult))
                v.tensor_tensor(ohg[:, h, :], q, gb[h % 2], ALU.mult).then_inc(ohg_ok, 1)

            for h in range(HH + 1):
                new, old = h < HH, h > 0
                if old:
                    silu(h - 1, 3, gb, 2 * h)
                if new:
                    silu(h, 0, qb, 2 * h + 1)
                if old:
                    masked(h - 1)
                if new:
                    rowsum(2)
                if old:
                    states(h - 1)
                if new:
                    prep2(h)
                    rowsum(3)
                    kq(h)
                    rowsum(3)
                if old:
                    head_out(h - 1)

            dve.wait_ge(ohg_ok, HH)
            dve.wait_ge(hgo_out, 32 * HH)
            mark(v.memset(kcz, 0.0))
            link(v.memset(vcz, 0.0))
            dve.wait_ge(proj, U_CM + 1)
            b0 = 2 * (U_CM % 2)
            for e in range(2):
                v.tensor_copy(kcz[64 * e:64 * e + 64, :, e, :], ps[64 * e:64 * e + 64, b0, 0:2 * PB].rearrange("p (g c) -> p g c", g=2))
            for r in range(R):
                ins = v.tensor_copy(vcz[CB * r:CB * r + CB, :, r, :], ps[CB * r:CB * r + CB, b0 + 1, 0:KV].rearrange("p (g d) -> p g d", g=G))
            ins.then_inc(cm_ok, 1)
            link(v.memset(qbd, 0.0))
            dve.wait_ge(nq_ok, 8)
            for gp in range(2):
                for e in range(2):
                    for r in range(R):
                        src = nqT[64 * e:64 * e + 64, 4 * gp + r, T:N].rearrange("p (b t) -> p b t", t=ST)
                        o = e * R * ST + r * ST
                        ins = v.tensor_copy(qbd[64 * e:64 * e + 64, :, gp, o:o + ST], src)
            ins.then_inc(qbd_ok, 1)
            mark(v.memset(pcm, 0.0))

            gv = gate[:, :, :].rearrange("p i (h r) -> p i h r", r=BR)

            def c_scores(i):
                wait(dve, cpr_ok, i)
                dve.wait_ge(csc_ok, i + 1)
                for gp in range(2):
                    mark(v.tensor_tensor(pcw[:, 8 * gp:8 * gp + 8, :].rearrange("p (e r) c -> p e r c", e=2),
                                         ps[:, 7, gp * P:(gp + 1) * P].rearrange("p (r e c) -> p e r c", r=R, e=2),
                                         cpen[:, i:i + 1, :].unsqueeze(1).to_broadcast([P, 2, R, PB]), ALU.add))
                dve.wait_ge(v_dn, n_v[0])
                link(v.tensor_reduce(cst1[:, 0, :], pcw, AX.X, ALU.max))
                v.tensor_tensor(pcw, pcw, cst1[:, 0, :].unsqueeze(2).to_broadcast([P, NH, PB]), ALU.subtract).then_inc(cms_ok, 1)

            def c_probs(i):
                dve.wait_ge(cex_ok, i + 1)
                link(v.tensor_tensor(pcw, pcw, cm01[:, i:i + 1, :].to_broadcast([P, NH, PB]), ALU.mult))
                link(v.tensor_reduce(cst1[:, 1, :], pcw, AX.X, ALU.add))
                link(v.tensor_scalar(cst1[:, 1, :], cst1[:, 1, :], 1e-30, None, ALU.max))
                link(v.reciprocal(cst1[:, 1, :], cst1[:, 1, :]))
                link(v.tensor_tensor(cst1[:, 2, :], cst1[:, 1, :], gv[:, i, :, 0], ALU.mult))
                wait(dve, cpt_ok, i)
                v.tensor_tensor(pcm[:, :, 0:PB], pcw, cst1[:, 2, :].unsqueeze(2).to_broadcast([P, NH, PB]), ALU.mult).then_inc(cpr_ok, 1)

            def pair_out(k):
                i, hp = divmod(k, NH // 2)
                dve.wait_ge(pv_ok, 4 * (k + 1))
                v.tensor_copy(onsa[:, hp, i * P:(i + 1) * P], ps[:, 5 + k % 2, 0:P]).then_inc(on_ok, 1)

            dve.wait_ge(ge_ok, 1)
            c_scores(0)
            c_probs(0)
            for n in range(NU + VLAG + 1):
                if n < NU:
                    i, h, br = UNITS[n]
                    dve.wait_ge(sc_ok, n + 1)
                    wait(dve, p_ok, n - 3)
                    v.tensor_reduce(nmx[:, n % 4:n % 4 + 1], ps[:, n % 3, 0:(i + 1) * P], AX.X, ALU.max, negate=True).then_inc(nm_ok, 1)
                m = n - 2
                if 0 <= m < NU:
                    i, h, br = UNITS[m]
                    dve.wait_ge(p_ok, m + 1)
                    v.reciprocal(ssm[:, m % 4:m % 4 + 1], ssm[:, m % 4:m % 4 + 1]).then_inc(cf_ok, 1)
                    if m % 2:
                        dve.wait_ge(cf_ok, m + 1)
                        w = pr[m % 4][:, 0:(i + 1) * P]
                        v.tensor_scalar(w, w, ssm[:, m % 4:m % 4 + 1], gv[:, i, h, 1 + br:2 + br], ALU.mult, ALU.mult).then_inc(pn_ok[1], 1)
                m = n - VLAG - 1
                if m >= 0 and m % 4 == 3:
                    pair_out(m // 4)
                q = NU // PT
                if n % q == q - 6 and n < NU - 6:
                    c_scores(n // q + 1)
                if n % q == q - 3 and n < NU - 3:
                    c_probs(n // q + 1)

            def e_c4(b):
                dve.wait_ge(c3_ok, b + 1)
                v.tensor_reduce(cst2[:, 0:1], cbank[:, 256:384], AX.X, ALU.max, negate=True).then_inc(c4_ok, 1)

            def e_c6(b):
                dve.wait_ge(c5_ok, b + 1)
                link(v.reciprocal(cst2[:, 2:3], cst2[:, 1:2]))
                link(v.tensor_scalar(psm, psm, cst2[:, 2:3], None, ALU.mult))
                wait(dve, c7_ok, b)
                v.tensor_scalar(psg, psm, gateq[:, b, 0:1], 1.0 / CB, ALU.mult, ALU.mult)
                pv2 = psm.rearrange("p (s c) -> p s c", c=2)
                v.tensor_tensor(pair, pv2[:, :, 0], pv2[:, :, 1], ALU.add).then_inc(c6_ok, 1)

            def e_c8(b):
                q = G * ST
                dve.wait_ge(c7_ok, b + 1)
                dve.wait_ge(c10_ok, b + 1)
                wait(dve, c9_ok, b)
                v.memset(imp[0:q, NSB:NSB + 1], BONUS)
                v.tensor_copy(imp[0:q, 1:NSB], cbank[0:q, 1:NSB])
                link(v.tensor_scalar(imp[0:q, 0:1], cbank[0:q, 0:1], BONUS, None, ALU.add))
                link(v.max(out=est[0:q, 0, 24:32], in_=imp[0:q, :]))
                link(v.match_replace(out=imr[0:q, :], in_to_replace=est[0:q, 0, 24:32], in_values=imp[0:q, :], imm_value=-1.0))
                link(v.tensor_tensor(pen32[0:q, :], imr[0:q, :], imp[0:q, :], ALU.is_equal))
                v.tensor_scalar(pen32[0:q, :], pen32[0:q, :], NEG, None, ALU.mult).then_inc(c8_ok, 1)

            def e_c10(b):
                dve.wait_ge(c9_ok, b + 1)
                v.tensor_copy(penq[b % 2], cbank[:, 64:64 + NSB + 1]).then_inc(pq_ok, 1)
                dve.wait_ge(pq_ok, b + 1)

            def e_scale(b, pieces):
                for k in pieces:
                    for q, (a, n) in enumerate(PIECES[k]):
                        x = sc[b % 2][:, a:a + n]
                        ins = v.tensor_scalar(x, x, est[:, b % 2, 20 + (q > 0):21 + (q > 0)], None, ALU.mult)
                    ins.then_inc(epn_ok, 1)

            def e_out(b):
                dve.wait_ge(epv_ok, NC * (b + 1))
                for g in range(G):
                    q = R * ST
                    ins = v.tensor_copy(osb[q * g:q * g + q, b, :], obank[q * g:q * g + q, HD * (g % 2):HD * (g % 2) + HD])
                ins.then_inc(eo_ok, 1)

            dve.wait_ge(pv_ok, NU)
            dve.wait_ge(kvo_out, 16 * (5 + SB))
            dve.wait_ge(gq_in, 16 * NH)
            e_c4(0)
            e_c6(0)
            e_c8(0)
            e_c10(0)
            for s in range(NC * SB + LAG + 1):
                b, c = divmod(s, NC)
                w = sc[b % 2]
                m = s - LAG - 1
                if m >= 0 and m % NC == NC - 1:
                    e_out(m // NC)
                if b < SB:
                    x = est[:, b % 2, :]
                    dve.wait_ge(es_ok, s + 1)
                    if b >= 2:
                        dve.wait_ge(et_ok, s - 2 * NC + 1)
                    dve.wait_ge(v_dn, n_v[0])
                    bank = ps[:, 2 + s % 2, :]
                    if c < NPC:
                        link(v.tensor_tensor(w[:, c * 512:(c + 1) * 512].rearrange("p (s k) -> p s k", k=SELB),
                                             bank.rearrange("p (s k) -> p s k", k=SELB),
                                             penq[b % 2][:, 8 * c:8 * c + 8].unsqueeze(2).to_broadcast([P, 8, SELB]), ALU.add))
                        v.tensor_reduce(x[:, c:c + 1], w[:, c * 512:(c + 1) * 512], AX.X, ALU.max).then_inc(esc_ok, 1)
                    elif c == NPC:
                        v.tensor_tensor(w[:, SELW:SELW + ST], bank[:, 0:ST], pen8[:, 1, :], ALU.add)
                        link(v.tensor_copy(w[:, SELW + ST:SELW + WIN], bank[:, ST:WIN]))
                        v.tensor_reduce(x[:, 10:11], w[:, SELW:SELW + WIN], AX.X, ALU.max).then_inc(esc_ok, 1)
                    else:
                        mark(v.tensor_tensor(w[:, NPG * P:SELW], bank[:, 0:S], pnew[:, b, :], ALU.add))
                        link(v.tensor_tensor(w[:, SELW + WIN:SCW], bank[:, S:2 * S], pnew[:, b, :], ALU.add))
                        mark(v.tensor_reduce(x[:, 8:9], w[:, NPG * P:SELW], AX.X, ALU.max))
                        v.tensor_reduce(x[:, 11:12], w[:, SELW + WIN:SCW], AX.X, ALU.max).then_inc(esc_ok, 1)
                        dve.wait_ge(esc_ok, s + 1)
                        v.tensor_reduce(x[:, 12:13], x[:, 0:9], AX.X, ALU.max, negate=True)
                        v.tensor_reduce(x[:, 13:14], x[:, 10:12], AX.X, ALU.max, negate=True).then_inc(enm_ok, 1)
                if c == 4 and 0 < b <= SB:
                    y = est[:, (b - 1) % 2, :]
                    dve.wait_ge(eex_ok, b)
                    link(v.tensor_reduce(y[:, 20:21], y[:, 14:19], AX.X, ALU.add))
                    link(v.reciprocal(y[:, 20:21], y[:, 20:21]))
                    link(v.reciprocal(y[:, 21:22], y[:, 19:20]))
                    v.tensor_tensor(y[:, 20:22], y[:, 20:22], gateq[:, b - 1, 1:3], ALU.mult).then_inc(ecf_ok, 1)
                    dve.wait_ge(ecf_ok, b)
                if 4 <= c < 7 and 0 < b <= SB:
                    e_scale(b - 1, ([0, 1], [2, 3], [4])[c - 4])
                if b + 1 < SB:
                    if c == 4:
                        e_c4(b + 1)
                    if c == 5:
                        e_c6(b + 1)
                    if c == 7:
                        e_c8(b + 1)
                    if c == 9:
                        e_c10(b + 1)
            dve.wait_ge(sw_ok, 1)
            ins = v.tensor_copy(onsa[:, :, T:N].rearrange("p k (b t) -> p b k t", t=ST),
                                ps[:, 0, :].rearrange("p (b k t) -> p b k t", k=KD, t=ST))
            ins.then_inc(ons_ok, 1)

            for u in range(U_MG, U_UP):
                k = u - U_MG
                j = k % KD
                m = mgb[u % 2]
                dve.wait_ge(mge_ok, k + 1)
                if k < KD:
                    v.tensor_tensor(ohg[:, j, :], ohg[:, j, :], m, ALU.mult).then_inc(u_hT, 1)
                else:
                    if k == KD:
                        dve.wait_ge(ons_ok, 1)
                        dve.wait_ge(u_hT, KD)
                    link(v.tensor_tensor(m, onsa[:, j, :], m, ALU.mult))
                    v.tensor_tensor(ohg[:, j, :], ohg[:, j, :], m, ALU.add).then_inc(u_hT, 1)

            dve.wait_ge(par_in, 16 * 8)
            for i in range(TT + 1):
                if i < TT:
                    n = TR[i]
                    w = WSEQ.index(("wo", i)) % 4
                    dve.wait_ge(rs_ok, TT + 2 * i + 1)
                    dve.wait_ge(xr_in[i % 2], 16 * (i // 2 + 1))
                    wait(dve, xtr_ok, TT + i - 1)
                    hv = hn[i % 2][0:n]
                    link(v.scalar_tensor_tensor(hv.rearrange("p (a c) -> p a c", a=2), ps[0:n, 2 * w:2 * w + 2, :],
                                                st_rs[0:n, 1, i:i + 1], gqm[0:n].rearrange("p (a c) -> p a c", a=2), ALU.mult, ALU.mult))
                    v.tensor_tensor(x1[0:n, i, :], hv, xr[i % 2][0:n], ALU.add).then_inc(x1_ok, 1)
                if i >= 1:
                    tile_out(i - 1, WSEQ.index(("tr", i - 1)) % 4, 8, TT + i)
                if i < TT:
                    dve.wait_ge(rs_ok, TT + 2 * i + 2)
                    v.tensor_scalar(hv, x1[0:n, i, :], st_rs[0:n, 2, i:i + 1], None, ALU.mult).then_inc(xn_ok, 1)

            for j in range(NF):
                dve.wait_ge(ext_ok, j + 1)
                wait(dve, g_ok, j - 1)
                for tap in range(3):
                    for x in range(2):
                        e, o = ext[j % 2][x][:, tap:tap + CVW], cva[j % 2][x][:, 0:CVW]
                        k = x * NF + j
                        if tap == 0:
                            ins = v.tensor_scalar(o, e, cpar[:, 0, k:k + 1], cpar[:, 3, k:k + 1], ALU.mult, ALU.add)
                        else:
                            ins = v.scalar_tensor_tensor(o, e, cpar[:, tap, k:k + 1], o, ALU.mult, ALU.add)
                        if tap < 2:
                            mark(ins)
                    if tap < 2:
                        dve.wait_ge(v_dn, n_v[0])
                ins.then_inc(cnv_ok, 1)
                s = sge[j % 2][:, 0:EXT]
                dve.wait_ge(sg_ok, j + 1)
                sw = s[:, 0:CVW]
                link(v.tensor_tensor(sw, sw, cva[j % 2][0][:, 0:CVW], ALU.mult))
                v.tensor_tensor(gT[:, j, 0:T], s[:, 0:T], cva[j % 2][1][:, 0:T], ALU.mult)
                s3, b3 = [y[:, EXS:EXT].rearrange("p (b t) -> p b t", t=ST + 2)[:, :, 0:ST] for y in (s, cva[j % 2][1])]
                v.tensor_tensor(gT[:, j, T:N].rearrange("p (b t) -> p b t", t=ST), s3, b3, ALU.mult).then_inc(g_ok, 1)

            def half_sums(i):
                n = TR[i]
                dve.wait_ge(fo_ok, TT + i + 1)
                v.tensor_tensor(st_ss[0:n, 3, i:i + 1], st_ss[0:n, 3, i:i + 1], st_ss[0:n, 0, i:i + 1], ALU.add).then_inc(ssum_ok, 1)

            half_sums(0)
            for i in range(TT):
                n = TR[i]
                if i + 1 < TT:
                    half_sums(i + 1)
                dve.wait_ge(rs_ok, 3 * TT + i + 1)
                for h in range(2):
                    src = fo[0:n, i, :] if h == 0 else ps[0:n, (TT + i) % 8, :]
                    link(v.scalar_tensor_tensor(ftmp[0:n, :], src, st_rs[0:n, 3, i:i + 1], gqf[0:n, h * 512:(h + 1) * 512], ALU.mult, ALU.mult))
                    ins = v.tensor_tensor(x1[0:n, i, h * 512:(h + 1) * 512], x1[0:n, i, h * 512:(h + 1) * 512], ftmp[0:n, :], ALU.add)
                    if h == 0:
                        link(ins)
                    else:
                        ins.then_inc(y_ok, 1)
                dve.wait_ge(y_ok, i + 1)

        @block.tensor
        def _(pe):
            t = nc.tensor

            def weights(b):
                pe.wait_ge(w_in_s[b % NSLOT], landed[b])

            def banks_free(u):
                o = u - 2
                if o < 0:
                    return
                if o < U_KV:
                    h, k = divmod(o, 4)
                    if k == 1:
                        pe.wait_ge(ef_ok, h + 1)
                    elif k == 2:
                        pe.wait_ge(vt_ok, h + 1)
                    else:
                        pe.wait_ge(qg_ok, 2 * h + 1 + k // 3)
                elif o < U_KT:
                    pe.wait_ge(kv_ok, o - U_KV + 1)
                elif o < U_CM:
                    pe.wait_ge(kT_ok, o - U_KT + 1)
                elif o < U_NQ:
                    pe.wait_ge(cm_ok, 1)
                elif o < U_NG:
                    pe.wait_ge(nq_ok, o - U_NQ + 1)
                elif o < U_MG:
                    pe.wait_ge(ge_ok, 1)
                elif o < U_UP:
                    pe.wait_ge(mge_ok, o - U_MG + 1)
                else:
                    pe.wait_ge(up_ok, o - U_UP + 1)

            def feature(u, lhs):
                banks_free(u)
                for a in range(2):
                    for k in range(KD):
                        mm = t.matmul(ps[:, 2 * (u % 2) + a, 0:NHF], lhs(k), hT[:, k, a * NHF:(a + 1) * NHF],
                                      start=(k == 0), stop=(k == KD - 1))
                mm.then_inc(proj, 1)

            def rows(u, k3, b):
                banks_free(u)
                w = wslot[b % NSLOT].rearrange("p (k c) -> p k c", c=WB)
                for a, i in enumerate(range(2 * k3, min(2 * k3 + 2, TT))):
                    n = TR[i]
                    for k in range(KD):
                        mm = t.matmul(ps[0:n, 2 * (u % 2) + a, 0:WB], hT[:, k, i * P:i * P + n], w[:, k, :],
                                      start=(k == 0), stop=(k == KD - 1))
                mm.then_inc(proj, 1)

            def wcol(b, m):
                w = wslot[b % NSLOT].rearrange("p (k c) -> p k c", c=WB)
                return lambda k: w[:, k, m * P:(m + 1) * P]

            def head_unit(h, k):
                u = b = 4 * h + k
                weights(b)
                if k != 2:
                    feature(u, wcol(b, 0))
                    return
                banks_free(u)
                for i in range(TT):
                    n = TR[i]
                    if i == 2 and h > 0:
                        h_updates(h - 1, (2, 3))
                    for j in range(KD):
                        mm = t.matmul(ps[0:n, 2 * (u % 2) + i // PT, (i % PT) * P:(i % PT + 1) * P], hT[:, j, i * P:i * P + n],
                                      wcol(b, 0)(j), start=(j == 0), stop=(j == KD - 1))
                mm.then_inc(proj, 1)

            pe.wait_ge(par_in, 96)
            pe.wait_ge(const, NCST)
            t.transpose(ps[:, 4, 0:33], prow[:, :], ident[0:33, 0:33])
            for k in range(4):
                mm = t.transpose(ps[:, 5, 2 * NF * k:2 * NF * (k + 1)], crow[0:2 * NF, k, :], ident[0:2 * NF, 0:2 * NF])
            mm.then_inc(econst, 1)
            pe.wait_ge(idx_ok, 1)
            t.matmul(ps[:, 6, 0:2 * ST], rep8[:, :], c16[:, :, :], start=True, stop=True).then_inc(econst, 1)

            def transposes(i, pairn, src):
                n = TR[i]
                for k in range(KD):
                    mm = t.transpose(ps[:, 2 * pairn + k // 4, (k % 4) * P:(k % 4) * P + n], src[0:n, k * P:(k + 1) * P],
                                     ident[0:n, 0:n])
                mm.then_inc(xtr_ok, 1)

            for i in range(TT):
                pe.wait_ge(xn_ok, i + 1)
                wait(pe, hT_ok, i - 1)
                transposes(i, i % 2, xn[i % 2])

            def h_keys(h):
                e, x = eb[h % 2], xb[h % 2]
                pe.wait_ge(kq_ok, h + 1)
                wait(pe, ohg_ok, h)
                if h == 0:
                    pe.wait_ge(econst, 2)
                    pe.wait_ge(dconst, 1)
                for i in range(PT):
                    t.transpose(ps[:, 4, i * P:(i + 1) * P], e[:, i * P:(i + 1) * P], ident[:, :])
                t.transpose(ps[0:S, 6, 0:P], e[:, T:N], ident[:, :]).then_inc(ktr_ok, 1)
                for i in range(PT):
                    t.matmul(ps[:, 5, i * P:(i + 1) * P], e[:, i * P:(i + 1) * P], x[:, i * P:(i + 1) * P], start=True, stop=True)
                t.matmul(ps[0:S, 6, 128:128 + S], e[:, T:N], x[:, T:N], start=True, stop=True).then_inc(at_ok, 1)

            def h_updates(h, tiles):
                if tiles[0] == 0:
                    pe.wait_ge(ktok_ok, h + 1)
                    pe.wait_ge(att_ok, h + 1)
                for i in tiles:
                    pe.wait_ge(vm_ok, 5 * h + i + 1)
                    if i >= 2:
                        pe.wait_ge(st_ok, 5 * h + i - 1)
                    t.matmul(ps[:, 4 + i % 2, :], ktok[:, i, :], vm[i].rearrange("p c v -> p (c v)"), start=True, stop=True)\
                        .then_inc(u_ok, 1)

            def h_updates_s(h):
                pe.wait_ge(vm_ok, 5 * h + 5)
                for a in range(2):
                    pe.wait_ge(st_ok, 5 * h + 3 + a)
                    t.matmul(ps[:, 4 + a, :], ktok_s[0:S, :], vms[0:S, 4 * a:4 * a + 4, :].rearrange("p b v -> p (b v)"),
                             start=True, stop=True).then_inc(u_ok, 1)

            def h_out(h):
                r = rb[h % 2]
                vv = vt[h % 2]
                pe.wait_ge(vt_ok, h + 1)
                for i in range(PT):
                    pe.wait_ge(st_ok, 5 * h + i + 1)
                    t.matmul(ps[:, 7, i * P:(i + 1) * P], vv[:, i, :], att[:, i, :], start=True, stop=False,
                             skip_group_check=True)
                    for c in range(CPT):
                        k = i * CPT + c
                        if k:
                            t.matmul(ps[:, 7, k * CH:(k + 1) * CH], st[:, k, :], r[:, k * CH:(k + 1) * CH], start=False,
                                     stop=(c == CPT - 1), skip_group_check=True)
                t.matmul(ps[:, 6, 192:192 + S], vv[0:S, PT, :], att_s[0:S, :], start=True, stop=False, skip_group_check=True)
                pe.wait_ge(s0_in[h % 2], 16 * (h // 2 + 1))
                for b in range(SB):
                    mm = t.matmul(ps[:, 6, 192 + b * ST:192 + (b + 1) * ST], s0s[h % 2][:, b, :], r[:, T + b * ST:T + (b + 1) * ST],
                                  start=False, stop=(b == SB - 1), skip_group_check=True)
                mm.then_inc(o_ok, 1)

            def h_sums(h):
                pe.wait_ge(osq_ok, h + 1)
                pe.wait_ge(st_ok, 5 * h + 5)
                for a in range(2):
                    mm = t.matmul(ps[:, 4 + a, 0:NHF], ones[:, :], fb[h % 2][:, a * NHF:(a + 1) * NHF], start=True, stop=True)
                mm.then_inc(oss_ok, 1)

            def kv_unit(u):
                b, k = divmod(u - U_KV, 3)
                if k == 0:
                    weights(B_KV + b)
                rows(u, k, B_KV + b)

            pe.wait_ge(hT_ok, TT)
            def h_first(h):
                h_updates(h, (0, 1))

            def h_rest(h):
                if h == HH - 1:
                    h_updates(h, (2, 3))
                h_updates_s(h)
                h_out(h)

            STAGES = (h_keys, h_first, h_rest, h_sums)
            for h in range(HH + 1):
                for k in range(4):
                    if h < HH:
                        head_unit(h, k)
                    else:
                        kv_unit(U_KV + k)
                    if h > 0:
                        STAGES[k](h - 1)
            for u in range(U_KV + 4, U_KT):
                kv_unit(u)

            pe.wait_ge(kv_ok, U_KT - U_KV)
            for u in range(U_KT, U_CM):
                br, gp = divmod(u - U_KT, 2)
                c0 = (C_KS, C_KW)[br] + gp * P
                banks_free(u)
                for i in range(TT):
                    n = TR[i]
                    mm = t.transpose(ps[:, 2 * (u % 2) + i // PT, (i % PT) * P:(i % PT) * P + n], kvt[0:n, i, c0:c0 + P], ident[0:n, 0:n])
                mm.then_inc(proj, 1)
            banks_free(U_CM)
            b0 = 2 * (U_CM % 2)
            for gp in range(2):
                for i in range(PT):
                    t.matmul(ps[:, b0, gp * PB + i * CPT:gp * PB + (i + 1) * CPT], kvt[:, i, gp * P:(gp + 1) * P], amean[:, :],
                             start=True, stop=True)
            for i in range(PT):
                mm = t.matmul(ps[:, b0 + 1, 0:KV], avm[:, i, :, :].rearrange("p r c -> p (r c)"), kvt[:, i, KV:2 * KV],
                              start=(i == 0), stop=(i == PT - 1))
            mm.then_inc(proj, 1)
            for u in range(U_NQ, U_NG):
                j = u - U_NQ
                b = B_NQ + j // 2
                if j % 2 == 0:
                    weights(b)
                feature(u, wcol(b, j % 2))
            banks_free(U_NG)
            weights(B_NG)
            w = wslot[B_NG % NSLOT][:, 0:KD * NH * BR].rearrange("p (k c) -> p k c", c=NH * BR)
            for i in range(TT):
                n = TR[i]
                for k in range(KD):
                    mm = t.matmul(ps[0:n, 2 * (U_NG % 2), i * NH * BR:(i + 1) * NH * BR], hT[:, k, i * P:i * P + n], w[:, k, :],
                                  start=(k == 0), stop=(k == KD - 1))
            mm.then_inc(proj, 1)

            def c_scores(i):
                if i:
                    pe.wait_ge(cpT_ok, i)
                for j in range(8):
                    gp = j // R
                    mm = t.matmul(ps[:, 7, j * 2 * PB:(j + 1) * 2 * PB], nqT[:, j, i * P:(i + 1) * P],
                                  kcz[:, gp, :, :].rearrange("p e c -> p (e c)"), start=True, stop=True)
                mm.then_inc(csc_ok, 1)

            def c_transposes(i):
                pe.wait_ge(cpr_ok, i + 1)
                for g in range(G):
                    mm = t.transpose(ps[:, 7, g * P:(g + 1) * P], pcm[:, g * R:(g + 1) * R, :].rearrange("p r c -> p (r c)"), ident[:, :])
                mm.then_inc(cpt_ok, 1)

            def values(m):
                i, h1, br = UNITS[m]
                k = i * (NH // 2) + h1 // 2
                outs = [(n % 4, h, ps[64 * (h % 2):64 * (h % 2) + 64, 5 + k % 2, 0:P])
                        for n, h in ((m - 1, h1 - 1), (m, h1))]
                if br == 0:
                    pe.wait_ge(cpT_ok, i + 1)
                    wait(pe, on_ok, k - 1)
                    for _, h, out in outs:
                        t.matmul(out, vcz[:, h // R, h % R, :], pcT[i % 2][:, h // R, :], start=True, stop=False,
                                 skip_group_check=True)
                pe.wait_ge(pT_ok, m + 1)
                for j in range(i + 1):
                    for slot, h, out in outs:
                        c0 = (C_VS, C_VW)[br] + h // R * HD
                        mm = t.matmul(out, kvt[:, j, c0:c0 + HD], pT[slot][:, j, :], start=False,
                                      stop=(br == 1 and j == i), skip_group_check=True)
                mm.then_inc(pv_ok, 2)

            pe.wait_ge(nq_ok, 8)
            pe.wait_ge(cm_ok, 1)
            pe.wait_ge(kT_ok, 4)
            pe.wait_ge(ge_ok, 1)
            c_scores(0)
            q = NU // PT
            for n in range(NU + VLAG):
                if n < NU:
                    i, h, br = UNITS[n]
                    gp, e, tile = head(h)
                    w = (i + 1) * P
                    wait(pe, p_ok, n - 2)
                    wait(pe, nm_ok, n - 2)
                    t.matmul(ps[:, n % 3, 0:w], nqT[64 * e:64 * e + 64, tile, i * P:w], kT[64 * e:64 * e + 64, br, gp, 0:w],
                             start=True, stop=False, skip_group_check=True)
                    t.matmul(ps[:, n % 3, i * P:w], identb[:, :], penb[:, :], start=False, stop=True, skip_group_check=True)\
                        .then_inc(sc_ok, 1)
                m = n - TLAG
                if 0 <= m < NU:
                    i, h, br = UNITS[m]
                    if m % q == 0:
                        c_transposes(i)
                    pe.wait_ge(pn_ok[m % 2], m // 2 + 1)
                    wait(pe, pT_ok, m - 1)
                    for j in range(i + 1):
                        mm = t.transpose(ps[:, 3 + m % 2, j * P:(j + 1) * P], pr[m % 4][:, j * P:(j + 1) * P], ident[:, :])
                    mm.then_inc(t_ok, 1)
                m = n - VLAG
                if m >= 0 and m % 2:
                    values(m)
                if n % q == q - 6 and n < NU - 6:
                    c_scores(n // q + 1)

            def e_c1(b):
                wait(pe, pq_ok, b)
                for gp in range(2):
                    mm = t.transpose(cbank[:, gp * P:(gp + 1) * P], cmt[:, b, gp * P:(gp + 1) * P], ident[:, :])
                mm.then_inc(c1_ok, 1)

            def e_c3(b):
                pe.wait_ge(c2_ok, b + 1)
                for gp in range(2):
                    mm = t.matmul(cbank[64 * gp:64 * gp + 64, 256:384], qbd[:, b, gp, :], kcs[:, gp, :], start=True, stop=True)
                mm.then_inc(c3_ok, 1)

            def e_c7(b):
                pe.wait_ge(c6_ok, b + 1)
                t.transpose(cbank[:, 384:512], psg, ident[:, :])
                t.matmul(cbank[0:G * ST, 0:NSB], rmat[:, :], pair, start=True, stop=True).then_inc(c7_ok, 1)

            def e_c9(b):
                pe.wait_ge(c8_ok, b + 1)
                t.matmul(cbank[:, 64:64 + NSB + 1], rmatT[:, :], pen32[0:G * ST, :], start=True, stop=True).then_inc(c9_ok, 1)

            def e_values(m):
                bb, cc = divmod(m, NC)
                if cc == 0:
                    wait(pe, eo_ok, bb)
                    pe.wait_ge(c10_ok, bb + 1)
                    t.matmul(obank[:, 0:P], identb[:, :], zerob[:, :], start=True, stop=False, skip_group_check=True)
                    for gp in range(2):
                        t.matmul(obank[gp * S:(gp + 1) * S, 0:P], pscT[bb % 2][:, gp * S:(gp + 1) * S],
                                 cmt[:, bb, KV + gp * P:KV + (gp + 1) * P], start=False, stop=False, skip_group_check=True)
                pe.wait_ge(epT_ok, m + 1)
                if cc <= NPC:
                    vq = bb * (NPC + 1) + cc
                    pe.wait_ge(pg_v[vq % NVR], vland[vq])
                if cc <= NPC:
                    parts = [(j, gp, vring[vq % NVR][:, j, gp * P:(gp + 1) * P]) for j in range(PGC) for gp in range(2)]
                else:
                    parts = [(br, gp, kvt[0:S, PT, (C_VS, C_VW)[br] + gp * P:(C_VS, C_VW)[br] + (gp + 1) * P])
                             for br in range(2) for gp in range(2)]
                rows_in = P if cc <= NPC else S
                for j, gp, values in parts:
                    mm = t.matmul(obank[gp * S:(gp + 1) * S, 0:P], pTs[m % 2][0:rows_in, j, gp * S:(gp + 1) * S], values,
                                  start=False, stop=(cc == NC - 1 and j == 1), skip_group_check=True)
                mm.then_inc(epv_ok, 1)

            pe.wait_ge(on_ok, PT * NH // 2)
            pe.wait_ge(qbd_ok, 1)
            e_c1(0)
            e_c3(0)
            e_c7(0)
            e_c9(0)
            pe.wait_ge(p_ok, NU)
            for s in range(NC * SB + LAG):
                b, c = divmod(s, NC)
                m = s - LAG
                bb, cc = divmod(m, NC)
                keys = b < SB and c <= NPC
                kq = b * (NPC + 1) + c
                if keys:
                    pe.wait_ge(pg_k[kq % NKR], kland[kq])
                    pe.wait_ge(pg_g[kq % NKR], gland[kq])
                    wait(pe, ekT_ok, kq)
                    for gp in range(2):
                        for j in range(PGC):
                            mm = t.transpose(ps[:, gp, j * P:(j + 1) * P], kring[kq % NKR][:, j, gp * P:(gp + 1) * P], ident[:, :])
                    mm.then_inc(ek_ok, 1)
                if m >= 0:
                    pe.wait_ge(epn_ok, NP * bb + min(cc // 2, NP - 1) + 1)
                    wait(pe, epT_ok, m - 1)
                    if cc < NC - 1:
                        o = cc * 512 if cc < NPC else SELW
                        for j in range(PGC):
                            mm = t.transpose(ps[:, 4 + m % 2, j * P:(j + 1) * P], sc[bb % 2][:, o + j * P:o + (j + 1) * P], ident[:, :])
                    else:
                        for j, o in enumerate((NPG * P, SELW + WIN)):
                            mm = t.transpose(ps[0:S, 4 + m % 2, j * P:(j + 1) * P], sc[bb % 2][:, o:o + S], ident[:, :])
                    mm.then_inc(et_ok, 1)
                if m >= 1:
                    e_values(m - 1)
                if b < SB:
                    wait(pe, esc_ok, s - 1)
                    for gp in range(2):
                        out = ps[64 * gp:64 * gp + 64, 2 + s % 2, :]
                        if keys:
                            if gp == 0:
                                pe.wait_ge(ekT_ok, kq + 1)
                            mm = t.matmul(out, qbd[:, b, gp, :], kTs[kq % 2][:, gp, :], start=True, stop=True)
                        else:
                            for br in range(2):
                                mm = t.matmul(out[:, br * S:(br + 1) * S], qbd[:, b, gp, :], kT[:, br, gp, T:N], start=True, stop=True)
                    mm.then_inc(es_ok, 1)
                if b + 1 < SB:
                    if c == 3:
                        e_c1(b + 1)
                    if c == 4:
                        e_c3(b + 1)
                    if c == 6:
                        e_c7(b + 1)
                    if c == 8:
                        e_c9(b + 1)
            e_values(NC * SB - 1)
            pe.wait_ge(eo_ok, SB)
            heads = ident[:, :].rearrange("p (k e t) -> p k e t", e=2, t=ST)
            for b in range(SB):
                for e in range(2):
                    mm = t.matmul(ps[64 * e:64 * e + 64, 0, b * S:(b + 1) * S], osb[:, b, :], heads[:, :, e, :], start=True, stop=True)
            mm.then_inc(sw_ok, 1)
            pe.wait_ge(ons_ok, 1)

            for u in range(U_MG, U_UP):
                b = B_MG + (u - U_MG) // 2
                if (u - U_MG) % 2 == 0:
                    weights(b)
                feature(u, wcol(b, (u - U_MG) % 2))

            pe.wait_ge(u_hT, 2 * KD)
            for idx, (what, i) in enumerate(WSEQ):
                w = idx % 4
                if idx >= 4:
                    ww, j = WSEQ[idx - 4]
                    pe.wait_ge(x1_ok if ww == "wo" else hT_ok, j + 1 if ww == "wo" else TT + j + 1)
                n = TR[i]
                if what == "tr":
                    pe.wait_ge(xn_ok, TT + i + 1)
                    transposes(i, w, hn[i % 2])
                    continue
                for b in range(B_WO, B_UP):
                    if i == 0:
                        weights(b)
                for a in range(2):
                    for k in range(KD):
                        ws = wslot[(B_WO + k // 2) % NSLOT].rearrange("p (k c) -> p k c", c=D)
                        mm = t.matmul(ps[0:n, 2 * w + a, :], ohg[:, k, i * P:i * P + n], ws[:, k % 2, a * 512:(a + 1) * 512],
                                      start=(k == 0), stop=(k == KD - 1))
                mm.then_inc(wo_ok, 1)

            def cin(j):
                wait(pe, ext_ok, j - 1)
                for x in range(2):
                    mm = t.transpose(ps[:, 4 + j % 2, x * 2 * SB:(x + 1) * 2 * SB], cvi[:, x * FF + j * P:x * FF + (j + 1) * P],
                                     ident[0:2 * SB, 0:2 * SB])
                mm.then_inc(cin_ok, 1)

            def cot(j):
                pe.wait_ge(cog_ok, j + 1)
                wait(pe, cvo_ok, j - 1)
                for x in range(2):
                    mm = t.transpose(ps[0:NCO, 6 + j % 2, x * P:(x + 1) * P], cog[j % 2][:, x * NCO:(x + 1) * NCO], ident[:, :])
                mm.then_inc(cot_ok, 1)

            pe.wait_ge(hT_ok, 2 * TT)
            pe.wait_ge(cvi_in, 16)
            for j in range(NF):
                cin(j)
                weights(B_UP + j)
                for x in range(2):
                    u = U_UP + 2 * j + x
                    banks_free(u)
                    lhs = wcol(B_UP + j, x)
                    for a in range(2):
                        for k in range(KD):
                            mm = t.matmul(ps[:, 2 * (u % 2) + a, 0:NHF], lhs(k), hT[:, k, a * NHF:(a + 1) * NHF],
                                          start=(k == 0), stop=(k == KD - 1))
                    mm.then_inc(proj, 1)
                if j >= 1:
                    cot(j - 1)
            cot(NF - 1)
            pe.wait_ge(up_ok, 2 * NF)
            pe.wait_ge(ext_ok, NF)
            for h in range(2):
                if h == 1:
                    pe.wait_ge(cvo_ok, NF)
                for q, (k0, nk) in enumerate(DN_T):
                    b = B_DN + h * len(DN_T) + q
                    weights(b)
                    ws = wslot[b % NSLOT].rearrange("p (k c) -> p k c", c=512)
                    steps = [(k, i) for k in range(k0, k0 + nk) for i in range(TT)]
                    if h == 1 and q == len(DN_T) - 1:
                        steps.sort(key=lambda x: x[1])
                    for k, i in steps:
                        if h == 0 and i == 0:
                            pe.wait_ge(g_ok, k + 1)
                        n = TR[i]
                        bank = (TT * h + i) % 8
                        if k == 0 and TT * h + i >= 8:
                            pe.wait_ge(fo_ok, TT * h + i - 8 + 1)
                        mm = t.matmul(ps[0:n, bank, :], gT[:, k, i * P:i * P + n], ws[:, k - k0, :], start=(k == 0), stop=(k == NF - 1))
                        if k == NF - 1:
                            mm.then_inc(dn_ok, 1)
                    if q < len(DN_T) - 1:
                        mm.then_inc(dnb_ok, 1)


_INS = ['x_prompt', 'x_sample', 'cache_cmp_kv', 'cache_sel_kv', 'page_table', 'state_win_kv', 'state_hgrn', 'state_conv',
        'w_in', 'hg_lb_logits', 'hg_norm_g', 'w_out', 'w_up', 'conv_w', 'conv_b', 'w_down',
        'g_pre_mix', 'g_post_mix', 'g_pre_ffn', 'g_post_ffn']
_OUTS = [(1, T, D), (SB, ST, D), (1, 1, T, 2, G, HD), (1, SB, ST, 2, G, HD), (1, 1, T, 2, G, HD), (1, SB, ST, 2, G, HD),
         (1, 1, WIN, 2, G, HD), (1, SB, WIN, 2, G, HD), (1, 1, HH, P, P), (1, SB, HH, P, P), (1, 1, 2, 2 * FF), (1, SB, 2, 2 * FF)]


def kernel(**inputs):
    import concourse.bacc as bacc
    from concourse.bass_utils import run_bass_kernel_spmd

    nc = bacc.Bacc("TRN2", target_bir_lowering=False, num_devices=1)
    arrays, args = {}, []
    for name in _INS:
        a = np.ascontiguousarray(inputs[name])
        arrays[f"in_{name}"] = a
        args.append(nc.dram_tensor(f"in_{name}", a.shape, mybir.dt.from_np(a.dtype), kind="ExternalInput").ap())
    for i, shape in enumerate(_OUTS):
        args.append(nc.dram_tensor(f"out_{i}", shape, F32, kind="ExternalOutput").ap())
    build(nc, *args)
    r = run_bass_kernel_spmd(nc, [arrays], core_ids=[0])
    return tuple(r.results[0][f"out_{i}"] for i in range(len(_OUTS)))
```
